# Optimizing a Trainium2 kernel written in Bass

```python
import math
import jax, jax.numpy as jnp
from jax import lax
import numpy as np

'''One inference step of a hybrid streaming encoder trunk (YOCO-style dual path).

Layer pattern (DEPTH=2): layer 0 = Mamba-2 SSD mixer (mixer A), layer 1 = multi-head latent
attention (mixer B) that reads ONE shared compressed KV latent + decoupled rotary key computed
from the residual stream after the last A layer. Every layer is a macaron block:
  h += 1/2 * SwiGLU(RMSNorm(h)); h += Mixer(RMSNorm(h)); h += 1/2 * SwiGLU(RMSNorm(h));
  h += (p[i] @ W_ple) * sigmoid(RMSNorm(h) @ W_gate)      (per-layer input embedding)
Attention uses the block-causal chunk mask (CHUNK=64); the SSD scan is per-token causal.

Inputs:
  x_prompt (BATCH, SEQ, D_MODEL)            first SEQ frames of BATCH new streams (pos 0..SEQ-1)
  x_sample (DEC_BATCH, DEC_SEQ, D_MODEL)    next frames of running streams (pos PAST_LEN..)
  p_prompt (DEPTH, BATCH, SEQ, PLE_DIM), p_sample (DEPTH, DEC_BATCH, DEC_SEQ, PLE_DIM)
  state_conv (N_A, DEC_BATCH, CONV_W-1, CONV_DIM)                   last pre-conv x/B/C rows
  state_ssm  (N_A, DEC_BATCH, SSM_HEADS, SSM_HEAD_DIM, D_STATE)     SSD recurrent state
  cache_kv_latent (DEC_BATCH, PAST_LEN, KV_LORA)                    shared MLA latent rows
  cache_k_rope    (DEC_BATCH, PAST_LEN, QK_ROPE)                    shared rotary key rows
Returns the tuple
  (y_prompt (BATCH, SEQ, D_MODEL), y_sample (DEC_BATCH, DEC_SEQ, D_MODEL),
   conv_prompt (N_A, BATCH, CONV_W-1, CONV_DIM), ssm_prompt (N_A, BATCH, SSM_HEADS, SSM_HEAD_DIM, D_STATE),
   kv_latent_prompt (BATCH, SEQ, KV_LORA), k_rope_prompt (BATCH, SEQ, QK_ROPE),
   conv_sample (N_A, DEC_BATCH, CONV_W-1, CONV_DIM), ssm_sample (N_A, DEC_BATCH, SSM_HEADS, SSM_HEAD_DIM, D_STATE),
   kv_latent_sample (DEC_BATCH, DEC_SEQ, KV_LORA), k_rope_sample (DEC_BATCH, DEC_SEQ, QK_ROPE))
'''

D_MODEL = 1024
BATCH = 1
SEQ = 256
DEPTH = 2
DEC_BATCH = 8
DEC_SEQ = 16
PAST_LEN = 512

CHUNK = 64
N_A = max(1, DEPTH // 2)
N_B = DEPTH - N_A
EPS = 1e-6

D_FF = 2816
PLE_DIM = 256

SSM_EXPAND = 2
D_INNER = SSM_EXPAND * D_MODEL
SSM_HEAD_DIM = 64
SSM_HEADS = D_INNER // SSM_HEAD_DIM
SSM_GROUPS = 4
SSM_HPG = SSM_HEADS // SSM_GROUPS
D_STATE = 128
CONV_W = 4
GN = SSM_GROUPS * D_STATE
CONV_DIM = D_INNER + 2 * GN
IN_A = D_INNER + CONV_DIM + SSM_HEADS
SSD_CHUNK = CHUNK

MLA_HEADS = 16
Q_LORA = 512
KV_LORA = 256
QK_NOPE = 64
QK_ROPE = 32
V_HEAD = 64
ROPE_BASE = 10000.0
ATTN_SCALE = (QK_NOPE + QK_ROPE) ** -0.5
Q_BLOCK = 128

kernel_name = 'yoco_ssd_mla_macaron_stream_step'

def rmsnorm(x, g):
    xf = x.astype(jnp.float32)
    y = xf * lax.rsqrt(jnp.mean(xf * xf, axis=-1, keepdims=True) + EPS)
    return (y * g.astype(jnp.float32)).astype(x.dtype)

def swiglu(u, wg, wu, wd):
    return (jax.nn.silu(u @ wg) * (u @ wu)) @ wd

def rope(x, pos):
    half = QK_ROPE // 2
    inv = ROPE_BASE ** (-jnp.arange(half, dtype=jnp.float32) / half)
    ang = pos.astype(jnp.float32)[:, None] * inv[None, :]
    shape = (pos.shape[0],) + (1,) * (x.ndim - 3) + (half,)
    cos = jnp.cos(ang).reshape(shape)
    sin = jnp.sin(ang).reshape(shape)
    xf = x.astype(jnp.float32)
    x1, x2 = xf[..., :half], xf[..., half:]
    return jnp.concatenate([x1 * cos - x2 * sin, x1 * sin + x2 * cos], axis=-1).astype(x.dtype)

def causal_conv(u, buf, w, b):
    T = u.shape[1]
    up = jnp.concatenate([buf.astype(u.dtype), u], axis=1)
    y = b + sum(up[:, k:k + T] * w[k] for k in range(CONV_W))
    return y, up[:, -(CONV_W - 1):]

def ssd_scan(x, dt, A, Bm, Cm, s0):
    b, T = x.shape[0], x.shape[1]
    L = min(SSD_CHUNK, T)
    nc = T // L
    f32 = jnp.float32
    xdt = (x.astype(f32) * dt[..., None]).reshape(b, nc, L, SSM_GROUPS, SSM_HPG, SSM_HEAD_DIM)
    a = (dt * A).reshape(b, nc, L, SSM_GROUPS, SSM_HPG)
    Bc = Bm.astype(f32).reshape(b, nc, L, SSM_GROUPS, D_STATE)
    Cc = Cm.astype(f32).reshape(b, nc, L, SSM_GROUPS, D_STATE)
    causal = jnp.tril(jnp.ones((L, L), dtype=bool))

    def step(s, inp):
        xk, ak, bk, ck = inp
        acs = jnp.cumsum(ak, axis=1)
        at = jnp.moveaxis(acs, 1, -1)
        seg = jnp.exp(jnp.where(causal, at[..., :, None] - at[..., None, :], -jnp.inf))
        cb = jnp.einsum('blgn,bsgn->bgls', ck, bk)
        y_diag = jnp.einsum('bghls,bsghp->blghp', cb[:, :, None] * seg, xk)
        y_off = jnp.einsum('blgn,bghpn->blghp', ck, s) * jnp.exp(acs)[..., None]
        to_end = jnp.exp(acs[:, -1:] - acs)
        s_new = s * jnp.exp(acs[:, -1])[..., None, None] + jnp.einsum('blgn,blghp->bghpn', bk, xk * to_end[..., None])
        return s_new, y_diag + y_off

    sw = lambda t: jnp.swapaxes(t, 0, 1)
    s_init = s0.astype(f32).reshape(b, SSM_GROUPS, SSM_HPG, SSM_HEAD_DIM, D_STATE)
    s_fin, y = lax.scan(step, s_init, (sw(xdt), sw(a), sw(Bc), sw(Cc)))
    y = sw(y).reshape(b, T, SSM_HEADS, SSM_HEAD_DIM)
    return y, s_fin.reshape(b, SSM_HEADS, SSM_HEAD_DIM, D_STATE)

def mamba2_mixer(u, conv_buf, ssm_state, w_in, conv_w, conv_b, dt_bias, A_log, Dp, norm_g, w_out):
    b, T, _ = u.shape
    zxbcdt = u @ w_in
    z = zxbcdt[..., :D_INNER]
    xbc = zxbcdt[..., D_INNER:D_INNER + CONV_DIM]
    dt_raw = zxbcdt[..., D_INNER + CONV_DIM:]
    xbc, new_buf = causal_conv(xbc, conv_buf, conv_w, conv_b)
    xbc = jax.nn.silu(xbc)
    xs = xbc[..., :D_INNER].reshape(b, T, SSM_HEADS, SSM_HEAD_DIM)
    Bm = xbc[..., D_INNER:D_INNER + GN].reshape(b, T, SSM_GROUPS, D_STATE)
    Cm = xbc[..., D_INNER + GN:].reshape(b, T, SSM_GROUPS, D_STATE)
    dt = jax.nn.softplus(dt_raw.astype(jnp.float32) + dt_bias.astype(jnp.float32))
    A = -jnp.exp(A_log.astype(jnp.float32))
    y, s_new = ssd_scan(xs, dt, A, Bm, Cm, ssm_state)
    y = y + Dp.astype(jnp.float32)[:, None] * xs.astype(jnp.float32)
    y = y.reshape(b, T, D_INNER).astype(u.dtype)
    y = rmsnorm(y * jax.nn.silu(z), norm_g)
    return y @ w_out, new_buf, s_new

def mla_kv_side(h, pos, ln_kv, w_kv_a, kv_norm, kr_norm):
    kv = rmsnorm(h, ln_kv) @ w_kv_a
    c_kv = rmsnorm(kv[..., :KV_LORA], kv_norm)
    k_rope = rope(rmsnorm(kv[..., KV_LORA:], kr_norm), pos)
    return c_kv, k_rope

def mla_expand(c_kv, w_kv_b, k_norm):
    b, S, _ = c_kv.shape
    kvb = (c_kv @ w_kv_b).reshape(b, S, MLA_HEADS, QK_NOPE + V_HEAD)
    k_nope = rmsnorm(kvb[..., :QK_NOPE], k_norm)
    return k_nope, kvb[..., QK_NOPE:]

def mla_queries(u, pos, w_dq, q_norm, w_q_b, qn_nope, qn_rope):
    b, T, _ = u.shape
    cq = rmsnorm(u @ w_dq, q_norm)
    q = (cq @ w_q_b).reshape(b, T, MLA_HEADS, QK_NOPE + QK_ROPE)
    q_nope = rmsnorm(q[..., :QK_NOPE], qn_nope)
    q_rope = rope(rmsnorm(q[..., QK_NOPE:], qn_rope), pos)
    return q_nope, q_rope

def attend(q_nope, q_rope, k_nope, k_rope, v, q_pos, k_pos):
    s = (jnp.einsum('bqhd,bkhd->bhqk', q_nope, k_nope)
         + jnp.einsum('bqhr,bkr->bhqk', q_rope, k_rope)).astype(jnp.float32) * ATTN_SCALE
    mask = (k_pos // CHUNK)[None, :] <= (q_pos // CHUNK)[:, None]
    s = jnp.where(mask[None, None], s, -jnp.inf)
    p = jax.nn.softmax(s, axis=-1).astype(v.dtype)
    return jnp.einsum('bhqk,bkhd->bqhd', p, v)

def attend_blocked(q_nope, q_rope, k_nope, k_rope, v, pos):
    b, T = q_nope.shape[0], q_nope.shape[1]
    nb = T // Q_BLOCK
    qn = jnp.swapaxes(q_nope.reshape(b, nb, Q_BLOCK, MLA_HEADS, QK_NOPE), 0, 1)
    qr = jnp.swapaxes(q_rope.reshape(b, nb, Q_BLOCK, MLA_HEADS, QK_ROPE), 0, 1)
    qp = pos.reshape(nb, Q_BLOCK)
    out = lax.map(lambda a: attend(a[0], a[1], k_nope, k_rope, v, a[2], pos), (qn, qr, qp))
    return jnp.swapaxes(out, 0, 1).reshape(b, T, MLA_HEADS, V_HEAD)

def setup_inputs(seed: int = 0) -> dict:
    key = jax.random.key(seed)
    ks = iter(jax.random.split(key, 64))
    f32 = jnp.float32

    def nrm(shape, fan_in):
        return jax.random.normal(next(ks), shape, f32) * fan_in ** -0.5

    def gain(shape):
        return 1.0 + 0.05 * jax.random.normal(next(ks), shape, f32)

    x_prompt = jax.random.normal(next(ks), (BATCH, SEQ, D_MODEL), f32)
    x_sample = jax.random.normal(next(ks), (DEC_BATCH, DEC_SEQ, D_MODEL), f32)
    p_prompt = jax.random.normal(next(ks), (DEPTH, BATCH, SEQ, PLE_DIM), f32)
    p_sample = jax.random.normal(next(ks), (DEPTH, DEC_BATCH, DEC_SEQ, PLE_DIM), f32)
    state_conv = jax.random.normal(next(ks), (N_A, DEC_BATCH, CONV_W - 1, CONV_DIM), f32)
    state_ssm = 0.1 * jax.random.normal(next(ks), (N_A, DEC_BATCH, SSM_HEADS, SSM_HEAD_DIM, D_STATE), f32)
    cache_kv_latent = jax.random.normal(next(ks), (DEC_BATCH, PAST_LEN, KV_LORA), f32)
    cache_k_rope = jax.random.normal(next(ks), (DEC_BATCH, PAST_LEN, QK_ROPE), f32)

    ln_ffn1 = gain((DEPTH, D_MODEL))
    w1_gate = nrm((DEPTH, D_MODEL, D_FF), D_MODEL)
    w1_up = nrm((DEPTH, D_MODEL, D_FF), D_MODEL)
    w1_down = nrm((DEPTH, D_FF, D_MODEL), D_FF)
    ln_mix = gain((DEPTH, D_MODEL))
    ln_ffn2 = gain((DEPTH, D_MODEL))
    w2_gate = nrm((DEPTH, D_MODEL, D_FF), D_MODEL)
    w2_up = nrm((DEPTH, D_MODEL, D_FF), D_MODEL)
    w2_down = nrm((DEPTH, D_FF, D_MODEL), D_FF)
    ln_ple = gain((DEPTH, D_MODEL))
    w_ple_in = nrm((DEPTH, PLE_DIM, D_MODEL), PLE_DIM)
    w_ple_gate = nrm((DEPTH, D_MODEL, D_MODEL), D_MODEL)

    a_in_proj = nrm((N_A, D_MODEL, IN_A), D_MODEL)
    a_conv_w = nrm((N_A, CONV_W, CONV_DIM), CONV_W)
    a_conv_b = 0.01 * jax.random.normal(next(ks), (N_A, CONV_DIM), f32)
    dt0 = jnp.exp(jax.random.uniform(next(ks), (N_A, SSM_HEADS), f32, math.log(1e-3), math.log(1e-1)))
    a_dt_bias = dt0 + jnp.log(-jnp.expm1(-dt0))
    a_A_log = jnp.log(jax.random.uniform(next(ks), (N_A, SSM_HEADS), f32, 1.0, 16.0))
    a_D = 1.0 + 0.1 * jax.random.normal(next(ks), (N_A, SSM_HEADS), f32)
    a_norm = gain((N_A, D_INNER))
    a_out_proj = nrm((N_A, D_INNER, D_MODEL), D_INNER)

    ln_kv = gain((D_MODEL,))
    w_kv_a = nrm((D_MODEL, KV_LORA + QK_ROPE), D_MODEL)
    kv_norm = gain((KV_LORA,))
    kr_norm = gain((QK_ROPE,))
    w_kv_b = nrm((KV_LORA, MLA_HEADS * (QK_NOPE + V_HEAD)), KV_LORA)
    k_norm = gain((QK_NOPE,))

    b_w_dq = nrm((N_B, D_MODEL, Q_LORA), D_MODEL)
    b_q_norm = gain((N_B, Q_LORA))
    b_w_q_b = nrm((N_B, Q_LORA, MLA_HEADS * (QK_NOPE + QK_ROPE)), Q_LORA)
    b_qn_nope = gain((N_B, QK_NOPE))
    b_qn_rope = gain((N_B, QK_ROPE))
    b_w_o = nrm((N_B, MLA_HEADS * V_HEAD, D_MODEL), MLA_HEADS * V_HEAD)

    return {'x_prompt': x_prompt, 'x_sample': x_sample, 'p_prompt': p_prompt, 'p_sample': p_sample,
            'state_conv': state_conv, 'state_ssm': state_ssm,
            'cache_kv_latent': cache_kv_latent, 'cache_k_rope': cache_k_rope,
            'ln_ffn1': ln_ffn1, 'w1_gate': w1_gate, 'w1_up': w1_up, 'w1_down': w1_down,
            'ln_mix': ln_mix, 'ln_ffn2': ln_ffn2, 'w2_gate': w2_gate, 'w2_up': w2_up, 'w2_down': w2_down,
            'ln_ple': ln_ple, 'w_ple_in': w_ple_in, 'w_ple_gate': w_ple_gate,
            'a_in_proj': a_in_proj, 'a_conv_w': a_conv_w, 'a_conv_b': a_conv_b, 'a_dt_bias': a_dt_bias,
            'a_A_log': a_A_log, 'a_D': a_D, 'a_norm': a_norm, 'a_out_proj': a_out_proj,
            'ln_kv': ln_kv, 'w_kv_a': w_kv_a, 'kv_norm': kv_norm, 'kr_norm': kr_norm,
            'w_kv_b': w_kv_b, 'k_norm': k_norm,
            'b_w_dq': b_w_dq, 'b_q_norm': b_q_norm, 'b_w_q_b': b_w_q_b,
            'b_qn_nope': b_qn_nope, 'b_qn_rope': b_qn_rope, 'b_w_o': b_w_o}

def reference(x_prompt, x_sample, p_prompt, p_sample, state_conv, state_ssm, cache_kv_latent, cache_k_rope,
              ln_ffn1, w1_gate, w1_up, w1_down, ln_mix, ln_ffn2, w2_gate, w2_up, w2_down,
              ln_ple, w_ple_in, w_ple_gate,
              a_in_proj, a_conv_w, a_conv_b, a_dt_bias, a_A_log, a_D, a_norm, a_out_proj,
              ln_kv, w_kv_a, kv_norm, kr_norm, w_kv_b, k_norm,
              b_w_dq, b_q_norm, b_w_q_b, b_qn_nope, b_qn_rope, b_w_o):

    def run_group(x, p, pos, conv_in, ssm_in, past_ckv, past_kr):
        b, T = x.shape[0], x.shape[1]
        h = x
        convs, ssms = [], []
        ckv_new = kr_new = k_nope = v = k_rope_all = k_pos = None
        for i in range(DEPTH):
            h = h + 0.5 * swiglu(rmsnorm(h, ln_ffn1[i]), w1_gate[i], w1_up[i], w1_down[i])
            u = rmsnorm(h, ln_mix[i])
            if i < N_A:
                mix, cbuf, sst = mamba2_mixer(u, conv_in[i], ssm_in[i], a_in_proj[i], a_conv_w[i], a_conv_b[i],
                                              a_dt_bias[i], a_A_log[i], a_D[i], a_norm[i], a_out_proj[i])
                convs.append(cbuf)
                ssms.append(sst)
            else:
                j = i - N_A
                q_nope, q_rope = mla_queries(u, pos, b_w_dq[j], b_q_norm[j], b_w_q_b[j], b_qn_nope[j], b_qn_rope[j])
                if past_ckv is None:
                    o = attend_blocked(q_nope, q_rope, k_nope, k_rope_all, v, pos)
                else:
                    o = attend(q_nope, q_rope, k_nope, k_rope_all, v, pos, k_pos)
                mix = o.reshape(b, T, MLA_HEADS * V_HEAD) @ b_w_o[j]
            h = h + mix
            h = h + 0.5 * swiglu(rmsnorm(h, ln_ffn2[i]), w2_gate[i], w2_up[i], w2_down[i])
            h = h + (p[i] @ w_ple_in[i]) * jax.nn.sigmoid(rmsnorm(h, ln_ple[i]) @ w_ple_gate[i])
            if i == N_A - 1:
                ckv_new, kr_new = mla_kv_side(h, pos, ln_kv, w_kv_a, kv_norm, kr_norm)
                if past_ckv is None:
                    ckv_all, k_rope_all, k_pos = ckv_new, kr_new, pos
                else:
                    ckv_all = jnp.concatenate([past_ckv.astype(ckv_new.dtype), ckv_new], axis=1)
                    k_rope_all = jnp.concatenate([past_kr.astype(kr_new.dtype), kr_new], axis=1)
                    k_pos = jnp.arange(past_ckv.shape[1] + T, dtype=jnp.int32)
                k_nope, v = mla_expand(ckv_all, w_kv_b, k_norm)
        return h, jnp.stack(convs), jnp.stack(ssms), ckv_new, kr_new

    pos_p = jnp.arange(x_prompt.shape[1], dtype=jnp.int32)
    conv0 = jnp.zeros((N_A, x_prompt.shape[0], CONV_W - 1, CONV_DIM), x_prompt.dtype)
    ssm0 = jnp.zeros((N_A, x_prompt.shape[0], SSM_HEADS, SSM_HEAD_DIM, D_STATE), jnp.float32)
    y_prompt, conv_p, ssm_p, kv_p, kr_p = run_group(x_prompt, p_prompt, pos_p, conv0, ssm0, None, None)

    past_len = cache_kv_latent.shape[1]
    pos_s = past_len + jnp.arange(x_sample.shape[1], dtype=jnp.int32)
    y_sample, conv_s, ssm_s, kv_s, kr_s = run_group(x_sample, p_sample, pos_s, state_conv, state_ssm,
                                                    cache_kv_latent, cache_k_rope)

    return (y_prompt, y_sample, conv_p, ssm_p, kv_p, kr_p, conv_s, ssm_s, kv_s, kr_s)


_drawn_inputs = setup_inputs


def setup_inputs(seed=0):
    import zlib

    import numpy as np

    out = dict(_drawn_inputs(seed))
    spreads = {}
    factors = {'ln_ffn2': 2.973,
     'ln_ple': 6.21,
     'a_conv_b': 3.724,
     'k_norm': 8.0,
     'b_q_norm': 8.0,
     'b_qn_nope': 8.0,
     'b_qn_rope': 42.633}
    for name, (base, spread) in spreads.items():
        noise = np.random.default_rng([zlib.crc32(name.encode()), seed]).standard_normal(out[name].shape)
        drawn = base * np.exp(spread * noise) if base else spread * noise
        out[name] = __import__('jax').numpy.asarray(drawn.astype(out[name].dtype))
    for name, factor in factors.items():
        out[name] = (out[name] * factor).astype(out[name].dtype)
    return out
```

```python
import concourse.bass as bass
from concourse import mybir
from contextlib import ExitStack
import numpy as np

F32 = mybir.dt.float32
F32R = mybir.dt.float32r
ALU = mybir.AluOpType
ACT = mybir.ActivationFunctionType
AX = mybir.AxisListType

P = 128
D_MODEL = 1024
SEQ, STREAMS, STEPS = 256, 8, 16
TOK = SEQ + STREAMS * STEPS
TT = TOK // P
KD = D_MODEL // P
D_FF = 2816
KF = D_FF // P
PLE = 256
D_INNER = 2048
HEADS, HD, GROUPS, N = 32, 64, 4, 128
HPG = HEADS // GROUPS
CONV_W = 4
CONV_DIM = D_INNER + 2 * GROUPS * N
KC = CONV_DIM // P
PAST = 512
MH, NOPE, ROPE, VH = 16, 64, 32, 64
QD = NOPE + ROPE
Q_LORA, KV_LORA = 512, 256
SCALE = (NOPE + ROPE) ** -0.5
EPS = 1e-6

SLOTS = 4
AHEAD = 3
STAGES = [("gu0", 44), ("dn0", 24), ("mix", 57), ("gu1", 44), ("dn1", 24), ("pi0", 2), ("pg0", 8),
          ("kv", 3), ("gu2", 44), ("dn2", 24), ("dq", 4), ("qb", 8), ("wo", 8), ("gu3", 44),
          ("dn3", 24), ("pi1", 2), ("pg1", 8)]
DN_TILES = (8, 7, 7)
BASE, WIDTH = {}, []
for _name, _n in STAGES:
    BASE[_name] = len(WIDTH)
    for _b in range(_n):
        WIDTH.append(DN_TILES[_b % 3] * P if _name[:2] == "dn" else
                     (864, 864, 576)[_b] if _name == "kv" else 2 * 384 if _name == "qb" else 1024)
NBLK = len(WIDTH)
NORMS = 8


def build(nc, T):
    ctx = ExitStack()
    with ctx:
        def sb(name, shape, dt=F32, c=ctx):
            return c.enter_context(nc.sbuf_tensor(name, shape, dt))

        def sem(name):
            return ctx.enter_context(nc.semaphore(name))

        h = sb("h", [P, KD, TOK])
        xh = sb("xh", [P, KD, TOK], F32R)
        xl = sb("xl", [P, KD, TOK], F32R)
        raw = sb("raw", [P, SLOTS, 1024])
        whi = sb("whi", [P, SLOTS, 1024], F32R)
        wlo = sb("wlo", [P, SLOTS, 1024], F32R)
        gains = sb("gains", [P, NORMS + 1, KD])
        ident = sb("ident", [P, P])
        ones = sb("ones", [P, P])
        std = sb("std", [P, TOK])
        rstd = sb("rstd", [P, 2, TOK])
        sqt = sb("sqt", [P, TOK])
        sqacc = sb("sqacc", [P, 2, TOK])
        rows = sb("rows", [P, 2, TT])
        bank = [ctx.enter_context(nc.psum_tensor(f"bank{i}", [P, 512], F32)) for i in range(8)]

        with ExitStack() as ffn:
            ah = sb("ah", [P, KF, TOK], F32R, ffn)
            al = sb("al", [P, KF, TOK], F32R, ffn)
            tg = sb("tg", [P, 2, TOK], F32, ffn)
            tu = sb("tu", [P, 2, TOK], F32, ffn)
        XPW = 3 + SEQ + STREAMS * (3 + STEPS)
        CW = XPW - 3
        SAMP0 = 3 + SEQ
        with ExitStack() as ssd:
            yh = sb("yh", [P, 4, TOK], F32R, ssd)
            yl = sb("yl", [P, 4, TOK], F32R, ssd)
            facc = sb("facc", [P, KD, TOK], F32, ssd)
            zs = sb("zs", [P, 4, TOK], F32, ssd)
            xsT = sb("xsT", [P, 4, TOK], F32, ssd)
            BC = sb("BC", [P, 2, TOK], F32, ssd)
            xdt = sb("xdt", [P, TT, 512], F32, ssd)
            xw = sb("xw", [P, TT, 512], F32, ssd)
            seg = sb("seg", [P, 2, 1024], F32, ssd)
            Gm = sb("Gm", [P, TOK], F32, ssd)
            Brow = sb("Brow", [P, TT, P], F32, ssd)
            Bm = sb("Bm", [P, STREAMS, P], F32, ssd)
            Cm = sb("Cm", [P, STREAMS, P], F32, ssd)
            S = sb("S", [P, STREAMS, 512], F32, ssd)
            S1 = sb("S1", [P, 512], F32, ssd)
            yoff = sb("yoff", [P, 2, 512], F32, ssd)
            xp = sb("xp", [P, 2, XPW + 1], F32, ssd)
            cy = sb("cy", [P, 2, XPW + 1], F32, ssd)
            cstate = sb("cstate", [P, KC, STREAMS * 3], F32, ssd)
            cout = sb("cout", [P, KC, 3 + STREAMS * 3], F32, ssd)
            cw = sb("cw", [P, KC, CONV_W + 1], F32, ssd)
            dcol = sb("dcol", [P, 16], F32, ssd)
            ang = sb("ang", [P, 16], F32, ssd)
            mask = sb("mask", [P, TT, P], F32, ssd)
            same = sb("same", [P, P], F32, ssd)
            ind = sb("ind", [P, STREAMS], F32, ssd)
            dtR = sb("dtR", [P, TT, HEADS], F32, ssd)
            aR = sb("aR", [P, TT, HEADS], F32, ssd)
            acs = sb("acs", [P, TT, HEADS], F32, ssd)
            toend = sb("toend", [P, TT, HEADS], F32, ssd)
            eacs = sb("eacs", [P, TT, HEADS], F32, ssd)
            dec = sb("dec", [P, STREAMS + 1, HEADS], F32, ssd)
            dts = sb("dts", [HEADS, 2], F32, ssd)
        am = Bm[:, 0:2, :].rearrange("p a b -> p (a b)").rearrange("p (s h) -> p s h", s=STREAMS)
        dv = [seg[0:HEADS, i // 2, (i % 2) * TOK:(i % 2 + 1) * TOK] for i in range(4)] + \
             [xdt[0:HEADS, i, 0:TOK] for i in range(3)]
        with ExitStack() as ple:
            phi = sb("phi", [P, 2, TOK], F32R, ple)
            plo = sb("plo", [P, 2, TOK], F32R, ple)
            pin = sb("pin", [P, KD, TOK], F32, ple)
            tp = sb("tp", [P, 2, TOK], F32, ple)
            kxh = sb("kxh", [P, KD, TOK], F32R, ple)
            kxl = sb("kxl", [P, KD, TOK], F32R, ple)
            kvr = sb("kvr", [P, TT, KV_LORA + ROPE], F32, ple)
            krot = sb("krot", [P, TT, 2, ROPE], F32, ple)
        with ExitStack() as mla:
            lowA = sb("lowA", [P, 4096], F32, mla)
            lowB = sb("lowB", [P, 4096], F32, mla)
            lowC = sb("lowC", [P, 2048], F32, mla)
            QRTs = sb("QRTs", [P, STREAMS, MH, STEPS], F32, mla)
            QTs = sb("QTs", [P, MH // 2, P], F32, mla)
            wk = sb("wk", [P, 2, MH * NOPE], F32, mla)
            wv = sb("wv", [P, 2, MH * VH], F32, mla)
            Qbd = sb("Qbd", [P, MH // 2, P], F32, mla)
            KTn = sb("KTn", [P, MH // 2, P], F32, mla)
            ckv = sb("ckv", [P, TT, KV_LORA], F32, mla)
            cT = sb("cT", [P, 2, TOK], F32, mla)
            krT = sb("krT", [P, TOK], F32, mla)
            krow = sb("krow", [P, TT, ROPE], F32, mla)
            rsc = sb("rsc", [P, TT, 8], F32, mla)
            cosr = sb("cosr", [P, TT, ROPE // 2], F32, mla)
            sinr = sb("sinr", [P, TT, ROPE // 2], F32, mla)
            cTb = sb("cTb", [P, 2, 2, PAST], F32, mla)
            krTb = sb("krTb", [P, PAST], F32, mla)
            sq5 = sb("sq5", [P, 512], F32, mla)
            kn = sb("kn", [P, 2, 8 * QD], F32, mla)
            Pb = sb("Pb", [P, 2, 640], F32, mla)
            PT = sb("PT", [P, 640], F32, mla)
            ol = sb("ol", [P, KV_LORA], F32, mla)
            qg96 = sb("qg96", [P, 2, QD], F32, mla)
            sm = sb("sm", [P, 96], F32, mla)
        OLT = lowA[:, :].rearrange("p (k h t) -> p k h t", k=2, h=MH)
        Kp = lowA[:, :].rearrange("p (h t) -> p h t", h=MH)
        KT = lowB[:, :].rearrange("p (s j t) -> p s j t", s=2, j=4)
        Qp = lowB[:, :].rearrange("p (h t) -> p h t", h=MH)
        cnat = lowC[:, :].rearrange("p (s k c) -> p s k c", s=2, k=4)
        Vp = lowC[:, :].rearrange("p (k c) -> p k c", k=2)
        cqr = lowC[:, 0:TT * Q_LORA].rearrange("p (t c) -> p t c", t=TT)
        qgr = Pb[:, 0, 0:Q_LORA]
        mk = krTb[:, 0:TOK]
        praw = cTb[:, 0, :, 0:TOK]
        kvg = kn[:, 0, 0:KV_LORA + ROPE]

        raw_loaded = [sem(f"raw_loaded{i}") for i in range(4)]
        hi_ready = sem("hi_ready")
        lo_ready = sem("lo_ready")
        blk = sem("blk")
        x_ld = sem("x_ld")
        const_ld = sem("const_ld")
        ones_ready = sem("ones_ready")
        h_new = sem("h_new")
        sq_done = sem("sq_done")
        sq_step = sem("sq_step")
        ms_ready = sem("ms_ready")
        std_ready = sem("std_ready")
        rstd_ready = sem("rstd_ready")
        xh_ready = sem("xh_ready")
        xl_ready = sem("xl_ready")
        gu_evac = sem("gu_evac")
        sg_ready = sem("sg_ready")
        a_ready = sem("a_ready")
        ah_ready = sem("ah_ready")
        al_ready = sem("al_ready")
        dve_chain = sem("dve_chain")
        act_chain = sem("act_chain")
        in_evac = sem("in_evac")
        c0_ready = sem("c0_ready")
        conv_ready = sem("conv_ready")
        conv_done = sem("conv_done")
        z_done = sem("z_done")
        dt_v = sem("dt_v")
        dt_a = sem("dt_a")
        dt_ready = sem("dt_ready")
        dtT_ps = sem("dtT_ps")
        dtR_ready = sem("dtR_ready")
        ac_ps = sem("ac_ps")
        acs_ready = sem("acs_ready")
        da_ready = sem("da_ready")
        xt_ps = sem("xt_ps")
        bt_ps = sem("bt_ps")
        xdt_ready = sem("xdt_ready")
        xw_ready = sem("xw_ready")
        brow_ready = sem("brow_ready")
        bm_ready = sem("bm_ready")
        g_ps = sem("g_ps")
        gm_ready = sem("gm_ready")
        ab_ps = sem("ab_ps")
        d_ready = sem("d_ready")
        mn_ready = sem("mn_ready")
        e_ready = sem("e_ready")
        m_ready = sem("m_ready")
        u_ps = sem("u_ps")
        s1_ready = sem("s1_ready")
        s1_store = sem("s1_store")
        s_ld = sem("s_ld")
        s_store = sem("s_store")
        cm_zero = sem("cm_zero")
        yo_ps = sem("yo_ps")
        yo_ready = sem("yo_ready")
        ym_done = sem("ym_done")
        su_done = sem("su_done")
        y_evac = sem("y_evac")
        y_ready = sem("y_ready")
        yh_ready = sem("yh_ready")
        yl_ready = sem("yl_ready")
        sqy = sem("sqy")
        f_evac = sem("f_evac")
        yms = sem("yms")
        ystd = sem("ystd")
        cout_ready = sem("cout_ready")
        p_ld = sem("p_ld")
        ph_ready = sem("ph_ready")
        pl_ready = sem("pl_ready")
        pin_ready = sem("pin_ready")
        pg_evac = sem("pg_evac")
        sgm_ready = sem("sgm_ready")
        kxh_ready = sem("kxh_ready")
        kxl_ready = sem("kxl_ready")
        rt_ps = sem("rt_ps")
        rows_ready = sem("rows_ready")
        kvr_ready = sem("kvr_ready")
        kvs = sem("kvs")
        kv_done = sem("kv_done")
        cT_ps = sem("cT_ps")
        cT_ready = sem("cT_ready")
        kr_zero = sem("kr_zero")
        cq_ready = sem("cq_ready")
        cqs = sem("cqs")
        cqn_ready = sem("cqn_ready")
        cqT_ps = sem("cqT_ps")
        cqh = sem("cqh")
        cql = sem("cql")
        qs1 = sem("qs1")
        qs2 = sem("qs2")
        qs3 = sem("qs3")
        qb_evac = sem("qb_evac")
        qr_ready = sem("qr_ready")
        qt_ps = sem("qt_ps")
        qe = sem("qe")
        w_ld = sem("w_ld")
        mla_zero = sem("mla_zero")
        ex_ps = sem("ex_ps")
        ks1 = sem("ks1")
        ks2 = sem("ks2")
        ks3 = sem("ks3")
        ks4 = sem("ks4")
        kt_ps = sem("kt_ps")
        kt_ev = sem("kt_ev")
        vp_ps = sem("vp_ps")
        vp_ev = sem("vp_ev")
        qk_ps = sem("qk_ps")
        pa1 = sem("pa1")
        pa2 = sem("pa2")
        pa3 = sem("pa3")
        pa4 = sem("pa4")
        pt_ps = sem("pt_ps")
        pt_ev = sem("pt_ev")
        po_ps = sem("po_ps")
        oh_ready = sem("oh_ready")
        ol_ready = sem("ol_ready")
        c_ld = [sem(f"c_ld{i}") for i in range(2)]
        kr_ld = sem("kr_ld")
        cn_ld = [sem(f"cn_ld{i}") for i in range(2)]
        qbd_ready = sem("qbd_ready")
        sc_ps = sem("sc_ps")
        sa2 = sem("sa2")
        sa3 = sem("sa3")
        olr = sem("olr")
        ot_ps = sem("ot_ps")
        olt = sem("olt")
        os_ps = sem("os_ps")
        out_st = sem("out_st")
        qg_ready = sem("qg_ready")
        mk_ld = sem("mk_ld")

        block = ctx.enter_context(nc.Block())
        MIX, PI, PG, KV, DQ, QB, WO = (BASE[x] for x in ("mix", "pi0", "pg0", "kv", "dq", "qb", "wo"))
        ITEMS = 6
        CRED = SLOTS

        def group0(g):
            return MIX + 1 + 14 * g

        def tiles(t, w=P):
            return slice(t * w, (t + 1) * w)

        def bc(ap, shape, axis):
            return ap.unsqueeze(axis).broadcast_to(shape)

        def samp(t):
            return t[:, SAMP0:XPW].rearrange("p (s t) -> p s t", s=STREAMS)

        @block.sync
        def _(sp):
            sp.dma_start(h[:, :, :], T["x"]).then_inc(x_ld, 16)
            for r in range(SLOTS):
                sp.dma_start(raw[:, r, :], T["stream"][r]).then_inc(raw_loaded[r], 16)
            with sp.Fori(1, NBLK // SLOTS) as i:
                for r in range(SLOTS):
                    sp.wait_ge(lo_ready, i * SLOTS + (r - SLOTS + 1))
                    sp.dma_start(raw[:, r, :], T["stream"][i * SLOTS + r]).then_inc(raw_loaded[r], 16)

        @block.gpsimd
        def _(pool):
            c = [0]

            def step(ins):
                c[0] += 1
                ins.then_inc(sq_step, 1)
                pool.wait_ge(sq_step, c[0])

            def squares(m):
                acc = sqacc[:, m % 2, :]
                for k in range(KD):
                    pool.wait_ge(h_new, 8 * m + k + 1)
                    if k == 0:
                        step(pool.tensor_tensor(acc, h[:, k, :], h[:, k, :], ALU.mult))
                    else:
                        step(pool.tensor_tensor(sqt[:, :], h[:, k, :], h[:, k, :], ALU.mult))
                        step(pool.tensor_tensor(acc, acc, sqt[:, :], ALU.add))
                pool.sem_inc(sq_done, 1)

            pool.dma_start(gains[:, :, :], T["gains"]).then_inc(const_ld, 16)
            pool.dma_start(ident[:, :], T["ident"]).then_inc(const_ld, 16)
            for t, name in ((cstate, "cstate"), (cw, "cw"), (dcol, "dcol"), (ang, "ang"), (mask, "mask"),
                            (same, "same"), (ind, "ind"), (dts, "dts")):
                pool.dma_start(t[:], T[name]).then_inc(const_ld, 16)
            pool.memset(ones[:, :], 1.0).then_inc(ones_ready, 1)
            pool.memset(xp[:, :, :], 0.0).then_inc(ones_ready, 1)
            squares(0)
            squares(1)
            pool.wait_ge(blk, CRED + MIX)
            pool.dma_start(S[:, :, :], T["ssm"][0]).then_inc(s_ld, 16)
            pool.memset(Cm[:, :, :], 0.0).then_inc(cm_zero, 1)
            for g in range(GROUPS):
                pool.wait_ge(s1_ready, 2 * g + 2)
                pool.dma_start(T["ssm_p"][g], S1[:, :]).then_inc(s1_store, 16)
                pool.wait_ge(su_done, 8 * g + 8)
                pool.dma_start(T["ssm_s"][g], S[:, :, :]).then_inc(s_store, 16)
                for i in range(4):
                    pool.wait_ge(y_ready, 4 * g + i + 1)
                    if g == 0 and i == 0:
                        step(pool.tensor_tensor(sqacc[:, 0, :], zs[:, i, :], zs[:, i, :], ALU.mult))
                    else:
                        step(pool.tensor_tensor(sqt[:, :], zs[:, i, :], zs[:, i, :], ALU.mult))
                        step(pool.tensor_tensor(sqacc[:, 0, :], sqacc[:, 0, :], sqt[:, :], ALU.add))
                    pool.sem_inc(sqy, 1)
                pool.wait_ge(s_store, 16 * (g + 1))
                if g < GROUPS - 1:
                    pool.dma_start(S[:, :, :], T["ssm"][g + 1]).then_inc(s_ld, 16)
            pool.wait_ge(cout_ready, KC)
            pool.dma_start(T["conv"], cout[:, :, :]).then_inc(out_st, 16)
            pool.wait_ge(out_st, 16)
            pool.wait_ge(s1_store, 16 * GROUPS)
            squares(2)
            pool.dma_start(praw, T["p"][0]).then_inc(p_ld, 16)
            pool.dma_start(kvg, T["kvg"]).then_inc(p_ld, 16)
            pool.dma_start(cosr[:], T["cos"]).then_inc(p_ld, 16)
            pool.dma_start(sinr[:], T["sin"]).then_inc(p_ld, 16)
            pool.memset(krT[:, :], 0.0).then_inc(kr_zero, 1)
            squares(3)
            squares(4)
            pool.wait_ge(kv_done, TT)
            pool.dma_start(T["kvl"], ckv[:, :, :]).then_inc(out_st, 16)
            pool.dma_start(T["kr"], krow[:, :, :]).then_inc(out_st, 16)
            squares(5)
            pool.wait_ge(blk, CRED + DQ)
            pool.dma_start(qgr, T["qgr"]).then_inc(w_ld, 16)
            pool.dma_start(qg96[:], T["qg96"]).then_inc(w_ld, 16)
            pool.dma_start(wk[:], T["wk"]).then_inc(w_ld, 16)
            pool.dma_start(wv[:], T["wv"]).then_inc(w_ld, 16)
            pool.dma_start(mk, T["mk"]).then_inc(mk_ld, 16)
            pool.memset(QRTs[:, :, :, :], 0.0).then_inc(mla_zero, 1)
            pool.memset(Qbd[:, :, :], 0.0).then_inc(mla_zero, 1)
            for b in range(STREAMS):
                if b >= 2:
                    pool.wait_ge(ex_ps, ITEMS + 8 * (b - 1))
                pool.dma_start(cTb[:, b % 2, :, :], T["cacheT"][b]).then_inc(c_ld[b % 2], 16)
                if b == 0:
                    pool.wait_ge(pa1, MH)
                    pool.memset(krTb[:, :], 0.0).then_inc(mla_zero, 1)
                    pool.wait_ge(mla_zero, 3)
                    pool.wait_ge(po_ps, MH)
                else:
                    pool.wait_ge(sc_ps, 2 * b)
                pool.dma_start(krTb[0:ROPE, :], T["krcT"][b]).then_inc(kr_ld, 16)
                if b >= 2:
                    pool.wait_ge(po_ps, MH + 2 * (b - 1))
                pool.dma_start(cnat[:, b % 2], T["cache"][b]).then_inc(cn_ld[b % 2], 16)
            pool.wait_ge(cn_ld[1], 16 * 4)
            squares(6)
            pool.dma_start(praw, T["p"][1]).then_inc(p_ld, 16)
            squares(7)
            for k in range(KD):
                pool.wait_ge(h_new, 8 * NORMS + k + 1)
                pool.dma_start(T["y"][:, k, :], h[:, k, :]).then_inc(out_st, 16)
            pool.wait_ge(out_st, 16 * (3 + KD))

        @block.scalar
        def _(act):
            A = nc.scalar.activation
            c = [0]

            def step(ins):
                c[0] += 1
                ins.then_inc(act_chain, 1)
                act.wait_ge(act_chain, c[0])

            def hi_split(n, i=0):
                if n >= NBLK:
                    return
                r = n % SLOTS
                act.wait_ge(raw_loaded[r], i * 16 + 16 * (n // SLOTS + 1))
                act.wait_ge(blk, i * SLOTS + (n + 1))
                w = WIDTH[n]
                A(whi[:, r, 0:w], raw[:, r, 0:w], ACT.Copy).then_inc(hi_ready, 1)

            def norm_std(m):
                act.wait_ge(ms_ready, m + 1)
                A(std[:, :], bank[7][:, 0:TOK], ACT.Sqrt, bias=EPS, scale=1.0 / D_MODEL).then_inc(std_ready, 1)

            def x_hi(m, k):
                act.wait_ge(h_new, 8 * m + k + 1)
                A(xh[:, k, :], h[:, k, :], ACT.Copy, scale=gains[:, m, k:k + 1]).then_inc(xh_ready, 1)

            def gate_up(u):
                base = BASE[f"gu{u}"]

                def pair(i, n0):
                    for j in range(2):
                        n, fs = base + n0 + 2 * j, KF * u + n0 // 2 + j
                        hi_split(n + 3, i)
                        act.wait_ge(gu_evac, i * 2 + (2 + fs + 1))
                        A(tg[:, j, :], tg[:, j, :], ACT.Silu).then_inc(sg_ready, 1)
                        hi_split(n + 4, i)
                        act.wait_ge(a_ready, i * 2 + (fs + 1))
                        A(ah[:, i * 2 + (n0 // 2 + j), :], tu[:, j, :], ACT.Copy).then_inc(ah_ready, 1)
                act.preload_act_table(ACT.Silu)
                with act.Fori(0, KF // 2 - 1) as i:
                    pair(i, 0)
                pair(0, 2 * KF - 4)

            def down(u, m):
                for j in range(KD):
                    for b in range(3):
                        hi_split(BASE[f"dn{u}"] + 3 * j + b + 3)
                    x_hi(m, j)

            def ple_act(l, m):
                act.wait_ge(p_ld, 64 + 16 * l)
                A(phi[:, :, :], praw, ACT.Copy).then_inc(ph_ready, 1)
                norm_std(m)
                for i in range(2):
                    n = BASE[f"pi{l}"] + i
                    hi_split(n + 3)
                    act.wait_ge(blk, CRED + n + 1)
                    for jj in range(4):
                        A(pin[:, 4 * i + jj, :], bank[jj][:, 0:TOK], ACT.Copy).then_inc(pin_ready, 1)
                for j in range(KD):
                    n = BASE[f"pg{l}"] + j
                    hi_split(n + 3)
                    act.wait_ge(pg_evac, 8 * l + j + 1)
                    A(tp[:, j % 2, :], tp[:, j % 2, :], ACT.Sigmoid).then_inc(sgm_ready, 1)

            for r in range(AHEAD):
                act.wait_ge(raw_loaded[r], 16)
                A(whi[:, r, 0:WIDTH[r]], raw[:, r, 0:WIDTH[r]], ACT.Copy).then_inc(hi_ready, 1)
            act.wait_ge(const_ld, 160)
            for k in range(KD):
                x_hi(0, k)
            norm_std(0)
            gate_up(0)
            down(0, 1)

            norm_std(1)
            hi_split(MIX + 3)
            for g in range(GROUPS):
                for b in range(10):
                    n, s, e = group0(g) + b, b % 2, 6 * g + b
                    hi_split(n + 3)
                    if b < 6:
                        ch = 4 * g + b if b < 4 else 16 + 4 * (b - 4) + g
                        step(A(samp(xp[:, s, :])[:, :, 0:3], cstate[:, ch, :].rearrange("p (s t) -> p s t", t=3), ACT.Copy))
                        act.wait_ge(in_evac, 10 * g + b + 1)
                        A(cout[:, ch, 0:3], xp[:, s, SEQ:SEQ + 3], ACT.Copy)
                        A(cout[:, ch, 3:27].rearrange("p (s t) -> p s t", t=3), samp(xp[:, s, :])[:, :, STEPS:STEPS + 3],
                          ACT.Copy).then_inc(cout_ready, 1)
                        A(cy[:, s, 0:CW], xp[:, s, 0:CW], ACT.Identity, bias=cw[:, ch, CONV_W:CONV_W + 1],
                          scale=cw[:, ch, 0:1]).then_inc(c0_ready, 1)
                        act.wait_ge(conv_ready, e + 1)
                        dst = xsT[:, b, :] if b < 4 else BC[:, b - 4, :]
                        A(dst[:, 0:SEQ], cy[:, s, 0:SEQ], ACT.Silu)
                        A(dst[:, SEQ:TOK].rearrange("p (s t) -> p s t", t=STEPS), samp(cy[:, s, :])[:, :, 0:STEPS],
                          ACT.Silu).then_inc(conv_done, 1)
                    else:
                        act.wait_ge(in_evac, 10 * g + b + 1)
                        A(zs[:, b - 6, :], zs[:, b - 6, :], ACT.Silu).then_inc(z_done, 1)
                if g == 0:
                    act.wait_ge(dt_v, 1)
                    step(A(dv[2], dv[1], ACT.Abs))
                    A(dts[:, 1:2], dts[:, 1:2], ACT.Exp)
                    A(dv[3], dv[2], ACT.Exp, scale=-1.0).then_inc(dt_a, 1)
                    act.wait_ge(dt_v, 2)
                    A(dv[5], dv[4], ACT.Ln).then_inc(dt_a, 1)
                    act.wait_ge(acs_ready, 1)
                    A(toend[:], toend[:], ACT.Exp)
                    A(eacs[:], acs[:], ACT.Exp)
                    A(dec[:, 0:STREAMS, :], bank[5][:, 0:STREAMS * HEADS].rearrange("p (s h) -> p s h", h=HEADS), ACT.Exp)
                    A(dec[:, STREAMS, :], bank[6][:, 128:160], ACT.Exp).then_inc(da_ready, 1)
                for t in range(TT):
                    q = 3 * g + t
                    act.wait_ge(mn_ready, q + 1)
                    A(seg[:, q % 2, :], seg[:, q % 2, :], ACT.Exp).then_inc(e_ready, 1)
                for i in range(4):
                    act.wait_ge(y_ready, 4 * g + i + 1)
                    A(yh[:, i, :], zs[:, i, :], ACT.Copy, scale=ang[:, 4 * g + i:4 * g + i + 1]).then_inc(yh_ready, 1)
                for b in range(4):
                    hi_split(group0(g) + 10 + b + 3)
            act.wait_ge(yms, 1)
            A(std[:, :], bank[7][:, 0:TOK], ACT.Sqrt, bias=EPS, scale=1.0 / D_INNER).then_inc(ystd, 1)
            for k in range(KD):
                x_hi(2, k)
            norm_std(2)
            gate_up(1)
            down(1, 3)
            ple_act(0, 3)

            act.wait_ge(blk, CRED + PG + KD)
            for k in range(KD):
                act.wait_ge(h_new, 32 + k + 1)
                A(kxh[:, k, :], h[:, k, :], ACT.Copy, scale=gains[:, NORMS, k:k + 1]).then_inc(kxh_ready, 1)
            for k in range(KD):
                x_hi(4, k)
            norm_std(4)
            for b in range(3):
                hi_split(KV + b + 3)
            for t in range(TT):
                act.wait_ge(kvr_ready, t + 1)
                A(sq5[:, 0:256], kvr[:, t, 0:256], ACT.Square, accum_out=rsc[:, t, 0:1])
                step(A(sq5[:, 256:288], kvr[:, t, 256:288], ACT.Square, accum_out=rsc[:, t, 1:2]))
                A(rsc[:, t, 2:3], rsc[:, t, 0:1], ACT.Sqrt, bias=EPS, scale=1.0 / KV_LORA)
                A(rsc[:, t, 3:4], rsc[:, t, 1:2], ACT.Sqrt, bias=EPS, scale=1.0 / ROPE).then_inc(kvs, 1)
            act.wait_ge(cT_ps, 1)
            act.wait_ge(kr_zero, 1)
            for k in range(2):
                A(cT[:, k, :], bank[5 + k][:, 0:TOK], ACT.Copy)
            A(krT[0:ROPE, :], bank[4][0:ROPE, 0:TOK], ACT.Copy).then_inc(cT_ready, 1)
            gate_up(2)
            down(2, 5)

            norm_std(5)
            for b in range(4):
                hi_split(DQ + b + 3)
            for t in range(TT):
                act.wait_ge(cq_ready, t + 1)
                step(A(sq5[:, :], cqr[:, t, :], ACT.Square, accum_out=rsc[:, t, 0:1]))
                A(rsc[:, t, 2:3], rsc[:, t, 0:1], ACT.Sqrt, bias=EPS, scale=1.0 / Q_LORA).then_inc(cqs, 1)
            act.wait_ge(cqT_ps, 1)
            for k in range(4):
                A(xh[:, k, :], bank[4 + k][:, 0:TOK], ACT.Copy).then_inc(cqh, 1)

            def q_evac(e):
                cg, t = divmod(e, TT)
                act.wait_ge(qt_ps, e + 1)
                if t < 2:
                    A(Qp[0:QD, 4 * cg:4 * cg + 4, tiles(t)], bank[6 + t][0:QD, :].rearrange("p (h t) -> p h t", h=4),
                      ACT.Copy).then_inc(qe, 1)
                else:
                    A(QTs[:, 2 * cg:2 * cg + 2, :], bank[6][:, 0:256].rearrange("p (h t) -> p h t", h=2), ACT.Copy)
                    A(QRTs[0:ROPE, :, 4 * cg:4 * cg + 4, :], bank[7][0:ROPE, :].rearrange("p (h b q) -> p b h q", h=4, q=STEPS),
                      ACT.Copy).then_inc(qe, 1)
            act.wait_ge(mla_zero, 2)
            for cg in range(4):
                for b in range(2):
                    hi_split(QB + 2 * cg + b + 3)
                for t in range(TT):
                    e = 3 * cg + t
                    act.wait_ge(blk, CRED + QB + 2 * cg + 2)
                    A(sq5[:, 0:384], bank[3 * (cg % 2) + t][:, 0:384], ACT.Square).then_inc(qs1, 1)
                    act.wait_ge(qs2, e + 1)
                    A(sm[:, 8:12], sm[:, 0:4], ACT.Sqrt, bias=EPS, scale=1.0 / NOPE)
                    A(sm[:, 12:16], sm[:, 4:8], ACT.Sqrt, bias=EPS, scale=1.0 / ROPE).then_inc(qs3, 1)
                    q_evac(e)

            def key_stats(w):
                act.wait_ge(ex_ps, w + 1)
                A(sq5[:, :], bank[w % 2][:, :], ACT.Square).then_inc(ks1, 1)
                act.wait_ge(ks2, w + 1)
                A(sm[:, 32:40], sm[:, 24:32], ACT.Sqrt, bias=EPS, scale=1.0 / NOPE).then_inc(ks3, 1)

            def key_evac(w):
                act.wait_ge(kt_ps, w + 1)
                if w < 4:
                    t, g = divmod(w, 2)
                    for x in range(2):
                        last = A(Kp[0:QD, 8 * g + 4 * x:8 * g + 4 * x + 4, tiles(t)],
                                 bank[2 + x][0:QD, :].rearrange("p (h t) -> p h t", h=4), ACT.Copy)
                elif w < ITEMS:
                    last = A(KTn[:, 4 * (w - 4):4 * (w - 4) + 4, :], bank[2 + w % 2][:, :].rearrange("p (h t) -> p h t", h=4), ACT.Copy)
                else:
                    u, st = divmod(w - ITEMS, 4)
                    if u >= 2 and st == 0:
                        act.wait_ge(sc_ps, u - 1)
                    last = A(KT[:, u % 2, :, tiles(st)], bank[2 + w % 2][:, :].rearrange("p (h t) -> p h t", h=4), ACT.Copy)
                last.then_inc(kt_ev, 1)

            for w in range(ITEMS):
                key_stats(w)
                key_evac(w)
            for v in range(4):
                act.wait_ge(vp_ps, v + 1)
                A(Vp[:, v // 2, 512 * (v % 2):512 * (v % 2) + 512], bank[4 + v][:, :], ACT.Copy).then_inc(vp_ev, 1)

            def p_exp(x):
                s, o = x % 2, 48 + 8 * (x % 2)
                act.wait_ge(pa2, x + 1)
                A(Pb[:, s, 0:128], Pb[:, s, 0:128], ACT.Exp, bias=sm[:, o + 2:o + 3], scale=SCALE, accum_out=sm[:, o + 4:o + 5])
                A(Pb[:, s, 128:384], Pb[:, s, 128:384], ACT.Exp, bias=sm[:, o + 3:o + 4], scale=SCALE,
                  accum_out=sm[:, o + 5:o + 6]).then_inc(pa3, 1)

            p_exp(0)
            for x in range(MH):
                if x + 1 < MH:
                    p_exp(x + 1)
                act.wait_ge(pt_ps, x + 1)
                A(PT[:, 0:384], bank[6][:, 0:384], ACT.Copy).then_inc(pt_ev, 1)
                if x % 2:
                    act.wait_ge(po_ps, x + 1)
                    A(xh[:, x // 2, 0:SEQ], bank[7 if x // 2 % 2 else 1][:, 0:SEQ], ACT.Copy).then_inc(oh_ready, 1)

            def key_pipe(w):
                key_stats(w)
                key_evac(w)

            for st in range(4):
                key_pipe(ITEMS + st)
            for u in range(2 * STREAMS):
                b, g = divmod(u, 2)
                if g == 0:
                    if b:
                        act.wait_ge(sc_ps, 2 * b)
                    src = QTs[:, :, 16 * b:16 * b + 16].rearrange("p (g j) q -> p g j q", g=2)
                    row = (MH // 2) * P
                    A(bass.AP(Qbd, 0, [[row, 64], [512, 2], [160, 4], [1, 16]]), src[0:64], ACT.Copy)
                    A(bass.AP(Qbd, 64 * row + 16, [[row, 64], [512, 2], [160, 4], [1, 16]]), src[64:128],
                      ACT.Copy).then_inc(qbd_ready, 1)
                act.wait_ge(sa2, u + 1)
                s, o = u % 2, 64 + 8 * (u % 2)
                A(Pb[:, s, 0:PAST], bank[4][:, :], ACT.Exp, bias=sm[:, o + 2:o + 3], scale=SCALE, accum_out=sm[:, o + 4:o + 5])
                A(Pb[:, s, PAST + 16 * b:PAST + 16 * b + 16], bank[5][:, 16 * b:16 * b + 16], ACT.Exp,
                  bias=sm[:, o + 2:o + 3], scale=SCALE, accum_out=sm[:, o + 5:o + 6]).then_inc(sa3, 1)
                nxt = ITEMS + 4 * (u + 1)
                more = u + 1 < 2 * STREAMS
                if more:
                    key_pipe(nxt)
                    key_pipe(nxt + 1)
                act.wait_ge(pt_ps, MH + u + 1)
                A(PT[:, 0:512], bank[6][:, :], ACT.Copy)
                A(PT[:, 512:640], bank[7][:, 0:128], ACT.Copy).then_inc(pt_ev, 1)
                if more:
                    key_pipe(nxt + 2)
                    key_pipe(nxt + 3)
            for x in range(MH // 2):
                act.wait_ge(os_ps, x + 1)
                A(xh[:, x, SEQ:TOK], bank[x % 2][:, 0:P], ACT.Copy).then_inc(oh_ready, 1)
            for b in range(8):
                hi_split(WO + b + 3)
            act.wait_ge(blk, CRED + WO + 8)
            for k in range(KD):
                x_hi(6, k)
            norm_std(6)
            gate_up(3)
            down(3, 7)
            ple_act(1, 7)

        @block.vector
        def _(dve):
            V = nc.vector
            c = [0]

            def step(ins):
                c[0] += 1
                ins.then_inc(dve_chain, 1)
                dve.wait_ge(dve_chain, c[0])

            def lo_split(n, i=0):
                if n >= NBLK:
                    return
                r, w = n % SLOTS, WIDTH[n]
                dve.wait_ge(hi_ready, i * SLOTS + (n + 1))
                V.tensor_tensor(wlo[:, r, 0:w], raw[:, r, 0:w], whi[:, r, 0:w].bitcast(F32),
                                ALU.subtract).then_inc(lo_ready, 1)

            def norm_rstd(m):
                dve.wait_ge(std_ready, m + 1)
                V.reciprocal(rstd[:, m % 2, :], std[:, :]).then_inc(rstd_ready, 1)
                dve.wait_ge(rstd_ready, m + 1)

            def x_lo(m, k):
                dve.wait_ge(xh_ready, 8 * m + k + 1)
                V.scalar_tensor_tensor(out=xl[:, k, :], in0=h[:, k, :], scalar=gains[:, m, k:k + 1],
                                       in1=xh[:, k, :].bitcast(F32), op0=ALU.mult, op1=ALU.subtract).then_inc(xl_ready, 1)

            def gate_up(u, m):
                base, r = BASE[f"gu{u}"], rstd[:, m % 2, :]

                def pair(i, n0):
                    for j in range(2):
                        n, fs = base + n0 + 2 * j, KF * u + n0 // 2 + j
                        dve.wait_ge(blk, i * SLOTS + (CRED + n + 2))
                        V.tensor_tensor(tg[:, j, :], bank[2 * j][:, 0:TOK], r, ALU.mult)
                        V.tensor_tensor(tu[:, j, :], bank[2 * j + 1][:, 0:TOK], r, ALU.mult).then_inc(gu_evac, 1)
                        lo_split(n + 3, i)
                        dve.wait_ge(sg_ready, i * 2 + (fs + 1))
                        V.tensor_tensor(tu[:, j, :], tg[:, j, :], tu[:, j, :], ALU.mult).then_inc(a_ready, 1)
                        lo_split(n + 4, i)
                        dve.wait_ge(ah_ready, i * 2 + (fs + 1))
                        f = i * 2 + (n0 // 2 + j)
                        V.tensor_tensor(al[:, f, :], tu[:, j, :], ah[:, f, :].bitcast(F32), ALU.subtract).then_inc(al_ready, 1)
                with dve.Fori(0, KF // 2 - 1) as i:
                    pair(i, 0)
                pair(0, 2 * KF - 4)

            def down(u, m):
                for j in range(KD):
                    n = BASE[f"dn{u}"] + 3 * j
                    for b in range(3):
                        lo_split(n + b + 3)
                    dve.wait_ge(blk, CRED + n + 3)
                    V.scalar_tensor_tensor(out=h[:, j, :], in0=bank[j % 4][:, 0:TOK], scalar=0.5, in1=h[:, j, :],
                                           op0=ALU.mult, op1=ALU.add).then_inc(h_new, 1)
                    x_lo(m, j)

            def ple_dve(l, m):
                dve.wait_ge(ph_ready, l + 1)
                V.tensor_tensor(plo[:, :, :], praw, phi[:, :, :].bitcast(F32), ALU.subtract).then_inc(pl_ready, 1)
                norm_rstd(m)
                for i in range(2):
                    lo_split(BASE[f"pi{l}"] + i + 3)
                for j in range(KD):
                    n = BASE[f"pg{l}"] + j
                    lo_split(n + 3)
                    dve.wait_ge(blk, CRED + n + 1)
                    V.tensor_tensor(tp[:, j % 2, :], bank[j % 4][:, 0:TOK], rstd[:, m % 2, :], ALU.mult).then_inc(pg_evac, 1)
                    dve.wait_ge(sgm_ready, 8 * l + j + 1)
                    dve.wait_ge(pin_ready, 8 * l + 8)
                    step(V.tensor_tensor(tp[:, j % 2, :], tp[:, j % 2, :], pin[:, j, :], ALU.mult))
                    V.tensor_tensor(h[:, j, :], h[:, j, :], tp[:, j % 2, :], ALU.add).then_inc(h_new, 1)

            dve.sem_inc(gu_evac, 2)
            dve.sem_inc(blk, CRED)
            for r in range(AHEAD):
                lo_split(r)
            dve.wait_ge(x_ld, 16)
            dve.sem_inc(h_new, KD)
            dve.wait_ge(const_ld, 160)
            for k in range(KD):
                x_lo(0, k)
            norm_rstd(0)
            gate_up(0, 0)
            down(0, 1)

            norm_rstd(1)
            r = rstd[:, 1, :]
            lo_split(MIX + 3)
            dve.wait_ge(ones_ready, 2)
            for g in range(GROUPS):
                hs = slice(HPG * g, HPG * g + HPG)
                for b in range(10):
                    n, s, e = group0(g) + b, b % 2, 6 * g + b
                    lo_split(n + 3)
                    dve.wait_ge(blk, CRED + n + 1)
                    src = bank[b % 4]
                    if b < 6:
                        ch = 4 * g + b if b < 4 else 16 + 4 * (b - 4) + g
                        V.tensor_tensor(xp[:, s, 3:3 + SEQ], src[:, 0:SEQ], r[:, 0:SEQ], ALU.mult)
                        V.tensor_tensor(samp(xp[:, s, :])[:, :, 3:3 + STEPS],
                                        src[:, SEQ:TOK].rearrange("p (s t) -> p s t", t=STEPS),
                                        r[:, SEQ:TOK].rearrange("p (s t) -> p s t", t=STEPS), ALU.mult).then_inc(in_evac, 1)
                        dve.wait_ge(c0_ready, e + 1)
                        for k in range(1, CONV_W):
                            ins = V.scalar_tensor_tensor(out=cy[:, s, 0:CW], in0=xp[:, s, k:k + CW], scalar=cw[:, ch, k:k + 1],
                                                         in1=cy[:, s, 0:CW], op0=ALU.mult, op1=ALU.add)
                            if k < CONV_W - 1:
                                step(ins)
                            else:
                                ins.then_inc(conv_ready, 1)
                    else:
                        if g:
                            dve.wait_ge(sqy, 4 * g)
                        V.tensor_tensor(zs[:, b - 6, :], src[:, 0:TOK], r, ALU.mult).then_inc(in_evac, 1)
                if g == 0:
                    step(V.tensor_tensor(dv[0], bank[4][0:HEADS, 0:TOK], r[0:HEADS, :], ALU.mult))
                    V.tensor_scalar(dv[1], dv[0], dts[:, 0:1], None, ALU.add).then_inc(dt_v, 1)
                    dve.wait_ge(dt_a, 1)
                    V.tensor_scalar(dv[4], dv[3], 1.0, None, ALU.add).then_inc(dt_v, 1)
                    dve.wait_ge(dt_v, 2)
                    V.reciprocal(dv[6], dv[4])
                    step(V.tensor_scalar(dv[0], dv[4], -1.0, None, ALU.add))
                    step(V.tensor_tensor(dv[0], dv[3], dv[0], ALU.subtract))
                    step(V.tensor_tensor(dv[0], dv[0], dv[6], ALU.mult))
                    dve.wait_ge(dt_a, 2)
                    step(V.tensor_scalar(dv[2], dv[1], 0.0, None, ALU.max))
                    step(V.tensor_tensor(dv[2], dv[2], dv[5], ALU.add))
                    step(V.tensor_tensor(dv[2], dv[2], dv[0], ALU.add))
                    V.tensor_scalar(dv[1], dv[2], dts[:, 1:2], -1.0, ALU.mult, ALU.mult).then_inc(dt_ready, 1)
                    dve.wait_ge(dtT_ps, 1)
                    V.tensor_copy(dtR[:, :, :], bank[5][:, 0:96].rearrange("p (t h) -> p t h", t=TT))
                    step(V.tensor_copy(aR[:, :, :], bank[5][:, 96:192].rearrange("p (t h) -> p t h", t=TT)))
                    V.tensor_tensor(am, bc(aR[:, 2, :], (P, STREAMS, HEADS), 1), bc(ind[:, :], (P, STREAMS, HEADS), 2),
                                    ALU.mult).then_inc(dtR_ready, 1)
                    dve.wait_ge(ac_ps, 1)
                    step(V.tensor_copy(acs[:, :, :], bank[6][:, 0:96].rearrange("p (t h) -> p t h", t=TT)))
                    V.tensor_tensor(toend[:, :, :], bank[6][:, 96:192].rearrange("p (t h) -> p t h", t=TT), acs[:, :, :],
                                    ALU.subtract).then_inc(acs_ready, 1)
                    dve.wait_ge(da_ready, 1)
                hd = (P, HPG, HD)
                for t in range(TT):
                    dve.wait_ge(xt_ps, 3 * g + t + 1)
                    v3 = xdt[:, t, :].rearrange("p (h d) -> p h d", h=HPG)
                    V.tensor_tensor(v3, bank[4 + t][:, :].rearrange("p (h d) -> p h d", h=HPG), bc(dtR[:, t, hs], hd, 2),
                                    ALU.mult).then_inc(xdt_ready, 1)
                    dve.wait_ge(xdt_ready, 3 * g + t + 1)
                    V.tensor_tensor(xw[:, t, :].rearrange("p (h d) -> p h d", h=HPG), v3, bc(toend[:, t, hs], hd, 2),
                                    ALU.mult).then_inc(xw_ready, 1)
                dve.wait_ge(bt_ps, g + 1)
                V.tensor_copy(Brow[:, :, :], bank[7][:, 0:TOK].rearrange("p (t n) -> p t n", t=TT)).then_inc(brow_ready, 1)
                dve.wait_ge(brow_ready, g + 1)
                V.tensor_tensor(Bm[:, :, :], bc(Brow[:, 2, :], (P, STREAMS, P), 1), bc(ind[:, :], (P, STREAMS, P), 2), ALU.mult)
                dve.wait_ge(cm_zero, 1)
                V.tensor_copy(bass.AP(Cm, 0, [[STREAMS * P, P], [P + STEPS, STREAMS], [1, STEPS]]),
                              BC[:, 1, SEQ:TOK].rearrange("p (s t) -> p s t", t=STEPS)).then_inc(bm_ready, 1)
                dve.wait_ge(g_ps, g + 1)
                V.tensor_tensor(Gm[:, :], bank[7][:, 0:TOK], mask[:, :, :].rearrange("p t l -> p (t l)"),
                                ALU.mult).then_inc(gm_ready, 1)

                def decay(t):
                    q, s = 3 * g + t, (3 * g + t) % 2
                    dve.wait_ge(ab_ps, q + 1)
                    if q >= 2:
                        dve.wait_ge(ym_done, q - 1)
                    for x in range(2):
                        ins = V.tensor_tensor(seg[:, s, 512 * x:512 * x + 512].rearrange("p (h l) -> p h l", h=4),
                                              bank[4 + x][:, :].rearrange("p (h l) -> p h l", h=4),
                                              bc(acs[:, t, HPG * g + 4 * x:HPG * g + 4 * x + 4], (P, 4, P), 2), ALU.subtract)
                    ins.then_inc(d_ready, 1)
                    dve.wait_ge(d_ready, q + 1)
                    V.tensor_scalar(seg[:, s, :], seg[:, s, :], 0.0, None, ALU.min).then_inc(mn_ready, 1)

                def decay_cb(t):
                    q, s = 3 * g + t, (3 * g + t) % 2
                    dve.wait_ge(e_ready, q + 1)
                    dve.wait_ge(gm_ready, g + 1)
                    v = seg[:, s, :].rearrange("p (h l) -> p h l", h=HPG)
                    V.tensor_tensor(v, v, bc(Gm[:, tiles(t)], (P, HPG, P), 1), ALU.mult).then_inc(m_ready, 1)

                def y_old(k):
                    dve.wait_ge(yo_ps, 2 * g + k + 1)
                    V.tensor_tensor(yoff[:, k, :].rearrange("p (h d) -> p h d", h=HPG),
                                    bank[7][:, :].rearrange("p (h d) -> p h d", h=HPG), bc(eacs[:, k + 1, hs], hd, 2),
                                    ALU.mult).then_inc(yo_ready, 1)

                decay(0)
                dve.wait_ge(u_ps, 10 * g + 1)
                if g:
                    dve.wait_ge(s1_store, 16 * g)
                V.tensor_copy(S1[:, :], bank[6][:, :]).then_inc(s1_ready, 1)
                decay_cb(0)
                y_old(0)
                s1v = S1[:, :].rearrange("p (h d) -> p h d", h=HPG)
                step(V.tensor_tensor(s1v, s1v, bc(dec[:, STREAMS, hs], hd, 2), ALU.mult))
                dve.wait_ge(u_ps, 10 * g + 2)
                V.tensor_tensor(S1[:, :], S1[:, :], bank[6][:, :], ALU.add).then_inc(s1_ready, 1)
                decay(1)
                decay_cb(1)
                y_old(1)
                decay(2)
                for b in range(STREAMS):
                    sv = S[:, b, :].rearrange("p (h d) -> p h d", h=HPG)
                    step(V.tensor_tensor(sv, sv, bc(dec[:, b, hs], hd, 2), ALU.mult))
                    if b == 0:
                        decay_cb(2)
                    dve.wait_ge(u_ps, 10 * g + 3 + b)
                    V.tensor_tensor(S[:, b, :], S[:, b, :], bank[6 + b % 2][:, :], ALU.add).then_inc(su_done, 1)
                dve.wait_ge(ym_done, 3 * g + 3)
                for i in range(4):
                    dve.wait_ge(z_done, 4 * g + i + 1)
                    V.scalar_tensor_tensor(out=xsT[:, i, :], in0=xsT[:, i, :], scalar=dcol[:, 4 * g + i:4 * g + i + 1],
                                           in1=bank[i][:, 0:TOK], op0=ALU.mult, op1=ALU.add).then_inc(y_evac, 1)
                    dve.wait_ge(y_evac, 4 * g + i + 1)
                    V.tensor_tensor(zs[:, i, :], zs[:, i, :], xsT[:, i, :], ALU.mult).then_inc(y_ready, 1)
                for i in range(4):
                    dve.wait_ge(yh_ready, 4 * g + i + 1)
                    V.scalar_tensor_tensor(out=yl[:, i, :], in0=zs[:, i, :], scalar=ang[:, 4 * g + i:4 * g + i + 1],
                                           in1=yh[:, i, :].bitcast(F32), op0=ALU.mult, op1=ALU.subtract).then_inc(yl_ready, 1)
                for b in range(4):
                    n = group0(g) + 10 + b
                    lo_split(n + 3)
                    dve.wait_ge(blk, CRED + n + 1)
                    for j in (2 * b, 2 * b + 1):
                        src = bank[4 + j % 4][:, 0:TOK]
                        if g == 0:
                            V.tensor_copy(facc[:, j, :], src).then_inc(f_evac, 1)
                        else:
                            V.tensor_tensor(facc[:, j, :], facc[:, j, :], src, ALU.add).then_inc(f_evac, 1)
            dve.wait_ge(ystd, 1)
            step(V.reciprocal(rstd[:, 0, :], std[:, :]))
            for j in range(KD):
                step(V.tensor_tensor(facc[:, j, :], facc[:, j, :], rstd[:, 0, :], ALU.mult))
                V.tensor_tensor(h[:, j, :], h[:, j, :], facc[:, j, :], ALU.add).then_inc(h_new, 1)
            for j in range(KD):
                x_lo(2, j)
            norm_rstd(2)
            gate_up(1, 2)
            down(1, 3)
            ple_dve(0, 3)

            for k in range(KD):
                dve.wait_ge(kxh_ready, k + 1)
                V.scalar_tensor_tensor(out=kxl[:, k, :], in0=h[:, k, :], scalar=gains[:, NORMS, k:k + 1],
                                       in1=kxh[:, k, :].bitcast(F32), op0=ALU.mult, op1=ALU.subtract).then_inc(kxl_ready, 1)
            for k in range(KD):
                x_lo(4, k)
            norm_rstd(4)
            for b in range(3):
                lo_split(KV + b + 3)

            def token_rows(x):
                dve.wait_ge(rt_ps, x + 1)
                V.tensor_copy(rows[:, x, :], bank[4][:, 0:TOK].rearrange("p (t c) -> p t c", t=TT)[:, :, 0]).then_inc(rows_ready, 1)
                dve.wait_ge(rows_ready, x + 1)

            token_rows(0)
            dve.wait_ge(blk, CRED + KV + 3)
            for t in range(TT):
                V.tensor_scalar(kvr[:, t, :], bank[t][:, 0:KV_LORA + ROPE], rows[:, 0, t:t + 1], None,
                                ALU.mult).then_inc(kvr_ready, 1)
            H2 = ROPE // 2
            for t in range(TT):
                dve.wait_ge(kvs, t + 1)
                step(V.reciprocal(rsc[:, t, 4:6], rsc[:, t, 2:4]))
                V.scalar_tensor_tensor(out=ckv[:, t, :], in0=kvr[:, t, 0:256], scalar=rsc[:, t, 4:5], in1=kvg[:, 0:256],
                                       op0=ALU.mult, op1=ALU.mult)
                x = krot[:, t, 0, :]
                step(V.scalar_tensor_tensor(out=x, in0=kvr[:, t, 256:288], scalar=rsc[:, t, 5:6], in1=kvg[:, 256:288],
                                            op0=ALU.mult, op1=ALU.mult))
                V.tensor_tensor(krot[:, t, 1, 0:H2], x[:, 0:H2], sinr[:, t, :], ALU.mult)
                V.tensor_tensor(krot[:, t, 1, H2:ROPE], x[:, H2:ROPE], sinr[:, t, :], ALU.mult)
                V.tensor_tensor(krow[:, t, 0:H2], x[:, 0:H2], cosr[:, t, :], ALU.mult)
                step(V.tensor_tensor(krow[:, t, H2:ROPE], x[:, H2:ROPE], cosr[:, t, :], ALU.mult))
                V.tensor_tensor(krow[:, t, 0:H2], krow[:, t, 0:H2], krot[:, t, 1, H2:ROPE], ALU.subtract)
                V.tensor_tensor(krow[:, t, H2:ROPE], krow[:, t, H2:ROPE], krot[:, t, 1, 0:H2], ALU.add).then_inc(kv_done, 1)
            gate_up(2, 4)
            down(2, 5)

            norm_rstd(5)
            for b in range(4):
                lo_split(DQ + b + 3)
            token_rows(1)
            dve.wait_ge(blk, CRED + DQ + 4)
            for t in range(TT):
                V.tensor_scalar(cqr[:, t, :], bank[t][:, :], rows[:, 1, t:t + 1], None, ALU.mult).then_inc(cq_ready, 1)
            dve.wait_ge(w_ld, 64)
            for t in range(TT):
                dve.wait_ge(cqs, t + 1)
                step(V.reciprocal(rsc[:, t, 4:5], rsc[:, t, 2:3]))
                V.scalar_tensor_tensor(out=cqr[:, t, :], in0=cqr[:, t, :], scalar=rsc[:, t, 4:5], in1=qgr,
                                       op0=ALU.mult, op1=ALU.mult).then_inc(cqn_ready, 1)
            step(V.tensor_tensor(qg96[:, 0, 0:NOPE], qg96[:, 0, 0:NOPE], qg96[:, 1, 0:NOPE], ALU.mult))
            for k in range(4):
                dve.wait_ge(cqh, k + 1)
                V.tensor_tensor(xl[:, k, :], bank[4 + k][:, 0:TOK], xh[:, k, :].bitcast(F32), ALU.subtract).then_inc(cql, 1)
            for cg in range(4):
                for b in range(2):
                    lo_split(QB + 2 * cg + b + 3)
                for t in range(TT):
                    e, s = 3 * cg + t, (3 * cg + t) % 2
                    dve.wait_ge(qs1, e + 1)
                    v = sq5[:, 0:384].rearrange("p (h d) -> p h d", h=4)
                    V.reduce_sum(sm[:, 0:4], v[:, :, 0:NOPE], axis=AX.X)
                    V.reduce_sum(sm[:, 4:8], v[:, :, NOPE:QD], axis=AX.X).then_inc(qs2, 1)
                    dve.wait_ge(qs3, e + 1)
                    step(V.reciprocal(sm[:, 16:24], sm[:, 8:16]))
                    if e >= 2:
                        dve.wait_ge(qt_ps, e - 1)
                    src = bank[3 * (cg % 2) + t][:, 0:384].rearrange("p (h d) -> p h d", h=4)
                    if t < 2:
                        q = kn[:, s, 0:384].rearrange("p (h d) -> p h d", h=4)
                        qn, qr = q[:, :, 0:NOPE], q[:, :, NOPE:QD]
                    else:
                        qn = kn[:, s, 0:4 * NOPE].rearrange("p (h d) -> p h d", h=4)
                        qr = kn[:, s, 4 * NOPE:384].rearrange("p (h d) -> p h d", h=4)
                    V.tensor_tensor(qn, src[:, :, 0:NOPE], bc(sm[:, 16:20], (P, 4, NOPE), 2), ALU.mult)
                    V.tensor_tensor(qr, src[:, :, NOPE:QD], bc(sm[:, 20:24], (P, 4, ROPE), 2),
                                    ALU.mult).then_inc(qb_evac, 1)
                    dve.wait_ge(qb_evac, e + 1)
                    V.tensor_tensor(qn, qn, bc(qg96[:, 0, 0:NOPE], (P, 4, NOPE), 1), ALU.mult)
                    step(V.tensor_tensor(qr, qr, bc(qg96[:, 0, NOPE:QD], (P, 4, ROPE), 1), ALU.mult))
                    xs_ = kn[:, s, 384:512].rearrange("p (h d) -> p h d", h=4)
                    xc = kn[:, s, 512:640].rearrange("p (h d) -> p h d", h=4)
                    for half in range(2):
                        src = qr[:, :, H2 * half:H2 * half + H2]
                        V.tensor_tensor(xs_[:, :, H2 * half:H2 * half + H2], src, bc(sinr[:, t, :], (P, 4, H2), 1), ALU.mult)
                        ins = V.tensor_tensor(xc[:, :, H2 * half:H2 * half + H2], src, bc(cosr[:, t, :], (P, 4, H2), 1), ALU.mult)
                    step(ins)
                    V.tensor_tensor(qr[:, :, 0:H2], xc[:, :, 0:H2], xs_[:, :, H2:ROPE], ALU.subtract)
                    V.tensor_tensor(qr[:, :, H2:ROPE], xs_[:, :, 0:H2], xc[:, :, H2:ROPE], ALU.add).then_inc(qr_ready, 1)

            def key_rows(w):
                dve.wait_ge(ks1, w + 1)
                V.reduce_sum(sm[:, 24:32], sq5[:, :].rearrange("p (h d) -> p h d", h=8), axis=AX.X).then_inc(ks2, 1)
                dve.wait_ge(ks3, w + 1)
                step(V.reciprocal(sm[:, 40:48], sm[:, 32:40]))
                if w >= 2:
                    dve.wait_ge(kt_ps, w - 1)
                else:
                    dve.wait_ge(qt_ps, 12)
                src = bank[w % 2][:, :].rearrange("p (h d) -> p h d", h=8)
                if w < 4:
                    kv_ = kn[:, w % 2, :].rearrange("p (h d) -> p h d", h=8)
                    V.tensor_copy(kv_[:, :, NOPE:QD], bc(krow[:, w // 2, :], (P, 8, ROPE), 1))
                    dst = kv_[:, :, 0:NOPE]
                else:
                    dst = kn[:, w % 2, 0:512].rearrange("p (h d) -> p h d", h=8)
                V.tensor_tensor(dst, src, bc(sm[:, 40:48], (P, 8, NOPE), 2), ALU.mult).then_inc(ks4, 1)

            for w in range(ITEMS):
                key_rows(w)

            def p_max(x):
                s, o = x % 2, 48 + 8 * (x % 2)
                dve.wait_ge(qk_ps, x + 1)
                if x >= 2:
                    dve.wait_ge(pt_ps, x - 1)
                V.tensor_tensor(Pb[:, s, 0:384], bank[4 + s][:, 0:384], mk, ALU.add).then_inc(pa1, 1)
                dve.wait_ge(pa1, x + 1)
                V.reduce_max(sm[:, o:o + 1], Pb[:, s, 0:128], axis=AX.X)
                step(V.reduce_max(sm[:, o + 1:o + 2], Pb[:, s, 128:384], axis=AX.X))
                V.tensor_scalar(sm[:, o + 2:o + 4], sm[:, o:o + 2], -SCALE, None, ALU.mult).then_inc(pa2, 1)

            dve.wait_ge(mk_ld, 16)
            p_max(0)
            for x in range(MH):
                s, o = x % 2, 48 + 8 * (x % 2)
                if x + 1 < MH:
                    p_max(x + 1)
                dve.wait_ge(pa3, x + 1)
                step(V.reciprocal(sm[:, o + 6:o + 8], sm[:, o + 4:o + 6]))
                V.tensor_scalar(Pb[:, s, 0:128], Pb[:, s, 0:128], sm[:, o + 6:o + 7], None, ALU.mult)
                V.tensor_scalar(Pb[:, s, 128:384], Pb[:, s, 128:384], sm[:, o + 7:o + 8], None, ALU.mult).then_inc(pa4, 1)
                if x % 2:
                    dve.wait_ge(oh_ready, x // 2 + 1)
                    V.tensor_tensor(xl[:, x // 2, 0:SEQ], bank[7 if x // 2 % 2 else 1][:, 0:SEQ],
                                    xh[:, x // 2, 0:SEQ].bitcast(F32), ALU.subtract).then_inc(ol_ready, 1)

            for st in range(4):
                key_rows(ITEMS + st)
            for u in range(2 * STREAMS):
                b, g = divmod(u, 2)
                s, o = u % 2, 64 + 8 * (u % 2)
                dve.wait_ge(sc_ps, u + 1)
                if u >= 2:
                    dve.wait_ge(pt_ps, MH + u - 1)
                else:
                    dve.wait_ge(pt_ps, MH)
                V.memset(Pb[:, s, PAST:640], 0.0)
                V.reduce_max(sm[:, o:o + 1], bank[4][:, :], axis=AX.X)
                step(V.reduce_max(sm[:, o + 1:o + 2], bank[5][:, 16 * b:16 * b + 16], axis=AX.X))
                step(V.tensor_tensor(sm[:, o + 3:o + 4], sm[:, o:o + 1], sm[:, o + 1:o + 2], ALU.max))
                V.tensor_scalar(sm[:, o + 2:o + 3], sm[:, o + 3:o + 4], -SCALE, None, ALU.mult).then_inc(sa2, 1)
                nxt = ITEMS + 4 * (u + 1)
                more = u + 1 < 2 * STREAMS
                if more:
                    key_rows(nxt)
                    key_rows(nxt + 1)
                dve.wait_ge(sa3, u + 1)
                step(V.tensor_tensor(sm[:, o + 6:o + 7], sm[:, o + 4:o + 5], sm[:, o + 5:o + 6], ALU.add))
                step(V.reciprocal(sm[:, o + 7:o + 8], sm[:, o + 6:o + 7]))
                if more:
                    key_rows(nxt + 2)
                    key_rows(nxt + 3)
                dve.wait_ge(po_ps, MH + u + 1)
                V.tensor_scalar(ol[:, :], bank[7][:, 256:512], sm[:, o + 7:o + 8], None, ALU.mult).then_inc(olr, 1)
                dve.wait_ge(ot_ps, u + 1)
                V.tensor_copy(OLT[:, :, 8 * g:8 * g + 8, 16 * b:16 * b + 16],
                              bank[7][:, 0:256].rearrange("p (k h q) -> p k h q", k=2, h=8)).then_inc(olt, 1)
            for x in range(MH // 2):
                dve.wait_ge(oh_ready, MH // 2 + x + 1)
                V.tensor_tensor(xl[:, x, SEQ:TOK], bank[x % 2][:, 0:P], xh[:, x, SEQ:TOK].bitcast(F32),
                                ALU.subtract).then_inc(ol_ready, 1)
            for b in range(8):
                lo_split(WO + b + 3)
                dve.wait_ge(blk, CRED + WO + b + 1)
                V.tensor_tensor(h[:, b, :], h[:, b, :], bank[2 + b % 4][:, 0:TOK], ALU.add).then_inc(h_new, 1)
            for k in range(KD):
                x_lo(6, k)
            norm_rstd(6)
            gate_up(3, 6)
            down(3, 7)
            ple_dve(1, 7)

        @block.tensor
        def _(pe):
            M = nc.tensor.matmul

            def product(out, r, k0, k1, mh_, ml_, first, last):
                for k in range(k0, k1):
                    ws = slice(k * P, (k + 1) * P)
                    M(out, whi[:, r, ws], mh_(k), start=first and k == k0, stop=False)
                    M(out, whi[:, r, ws], ml_(k), start=False, stop=False)
                    ins = M(out, wlo[:, r, ws], mh_(k), start=False, stop=last and k == k1 - 1)
                return ins

            def row_product(out, r, w0, w, xh_, xl_, first, last):
                M(out, xh_, whi[:, r, w0:w0 + w], start=first, stop=False)
                M(out, xh_, wlo[:, r, w0:w0 + w], start=False, stop=False)
                return M(out, xl_, whi[:, r, w0:w0 + w], start=False, stop=last)

            def weights(n, i=0):
                pe.wait_ge(lo_ready, i * SLOTS + (n + 1))

            def norm_sum(m):
                pe.wait_ge(sq_done, m + 1)
                M(bank[7][:, 0:TOK], ones[:, :], sqacc[:, m % 2, :], start=True, stop=True).then_inc(ms_ready, 1)

            X = (lambda k: xh[:, k, :], lambda k: xl[:, k, :])

            def gate_up(u, m):
                base = BASE[f"gu{u}"]
                pe.wait_ge(xl_ready, 8 * (m + 1))

                def pair(i, first):
                    for j in range(2):
                        pe.wait_ge(gu_evac, i * 2 + (KF * u + j + 1))
                        for half in range(2):
                            n = base + 2 * j + half
                            weights(n, i)
                            product(bank[2 * j + half][:, 0:TOK], n % SLOTS, 0, KD, *X, True, True).then_inc(blk, 1)
                            if first and j == 0 and half == 0 and m != 4:
                                norm_sum(m)
                pair(0, True)
                with pe.Fori(1, KF // 2) as i:
                    pair(i, False)

            def down(u, m):
                pe.wait_ge(gu_evac, 2 + KF * (u + 1))
                for j in range(KD):
                    k0 = 0
                    if j >= 4:
                        pe.wait_ge(h_new, 8 * m + j - 3)
                    for b, w in enumerate(DN_TILES):
                        n = BASE[f"dn{u}"] + 3 * j + b
                        if j == 0:
                            pe.wait_ge(al_ready, KF * u + k0 + w)
                        weights(n)
                        product(bank[j % 4][:, 0:TOK], n % SLOTS, 0, w, lambda k: ah[:, k0 + k, :],
                                lambda k: al[:, k0 + k, :], b == 0, b == 2).then_inc(blk, 1)
                        k0 += w

            def ple_pe(l, m):
                pe.wait_ge(pl_ready, l + 1)
                pe.wait_ge(xl_ready, 8 * (m + 1))
                for i in range(2):
                    n = BASE[f"pi{l}"] + i
                    weights(n)
                    for jj in range(4):
                        if i:
                            pe.wait_ge(pin_ready, 8 * l + jj + 1)
                        ins = product(bank[jj][:, 0:TOK], n % SLOTS, 2 * jj, 2 * jj + 2, lambda k: phi[:, k % 2, :],
                                      lambda k: plo[:, k % 2, :], True, True)
                    ins.then_inc(blk, 1)
                    if i == 0:
                        norm_sum(m)
                pe.wait_ge(pin_ready, 8 * l + 8)
                for j in range(KD):
                    n = BASE[f"pg{l}"] + j
                    weights(n)
                    if j >= 4:
                        pe.wait_ge(pg_evac, 8 * l + j - 3)
                    product(bank[j % 4][:, 0:TOK], n % SLOTS, 0, KD, *X, True, True).then_inc(blk, 1)

            pe.wait_ge(ones_ready, 1)
            gate_up(0, 0)
            down(0, 1)

            pe.wait_ge(xl_ready, 16)
            weights(MIX)
            product(bank[4][:, 0:TOK], MIX % SLOTS, 0, KD, *X, True, True).then_inc(blk, 1)
            norm_sum(1)
            for g in range(GROUPS):
                for b in range(10):
                    n = group0(g) + b
                    weights(n)
                    if b >= 4:
                        pe.wait_ge(in_evac, 10 * g + b - 3)
                    elif g:
                        pe.wait_ge(y_evac, 4 * g)
                    else:
                        pe.wait_ge(xl_ready, 16)
                    product(bank[b % 4][:, 0:TOK], n % SLOTS, 0, KD, *X, True, True).then_inc(blk, 1)
                if g == 0:
                    pe.wait_ge(dt_ready, 1)
                    pe.wait_ge(const_ld, 160)
                    for t in range(TT):
                        for x, v in ((0, dv[2]), (96, dv[1])):
                            ins = nc.tensor.transpose(bank[5][:, x + 32 * t:x + 32 * t + 32], v[:, tiles(t)],
                                                      ident[0:HEADS, 0:HEADS])
                    ins.then_inc(dtT_ps, 1)
                    pe.wait_ge(dtR_ready, 1)
                    for t in range(TT):
                        M(bank[6][:, 32 * t:32 * t + 32], mask[:, t, :], aR[:, t, :], start=True, stop=True)
                        M(bank[6][:, 96 + 32 * t:128 + 32 * t], ones[:, :] if t < 2 else same[:, :], aR[:, t, :],
                          start=True, stop=True)
                    M(bank[5][:, 0:STREAMS * HEADS], ones[:, :], am.rearrange("p s h -> p (s h)"), start=True,
                      stop=True).then_inc(ac_ps, 1)
                    pe.wait_ge(da_ready, 1)
                else:
                    pe.wait_ge(f_evac, 8 * g)
                pe.wait_ge(conv_done, 6 * g + 6)
                for t in range(TT):
                    for i in range(4):
                        ins = nc.tensor.transpose(bank[4 + t][:, tiles(i)], xsT[:, i, tiles(t)], ident[:, :])
                    ins.then_inc(xt_ps, 1)
                for t in range(TT):
                    ins = nc.tensor.transpose(bank[7][:, tiles(t)], BC[:, 0, tiles(t)], ident[:, :])
                ins.then_inc(bt_ps, 1)
                pe.wait_ge(brow_ready, g + 1)
                for t in range(TT):
                    ins = M(bank[7][:, tiles(t)], BC[:, 0, tiles(t)], BC[:, 1, tiles(t)], start=True, stop=True)
                ins.then_inc(g_ps, 1)

                def running(t):
                    if t:
                        pe.wait_ge(d_ready, 3 * g + t)
                    for hh in range(HPG):
                        a = aR[:, t, HPG * g + hh:HPG * g + hh + 1].broadcast_to((P, P))
                        ins = M(bank[4 + hh // 4][:, tiles(hh % 4)], a, mask[:, t, :], start=True, stop=True)
                    ins.then_inc(ab_ps, 1)

                def y_tile(t):
                    s = (3 * g + t) % 2
                    pe.wait_ge(m_ready, 3 * g + t + 1)
                    if t:
                        pe.wait_ge(yo_ready, 2 * g + t)
                    for i in range(4):
                        if t:
                            M(bank[i][:, tiles(t)], yoff[:, t - 1, tiles(i)], ident[:, :], start=True, stop=False,
                              skip_group_check=True)
                        for e in range(2):
                            hh = 2 * i + e
                            ins = M(bank[i][HD * e:HD * e + HD, tiles(t)], xdt[:, t, hh * HD:hh * HD + HD],
                                    seg[:, s, tiles(hh)], start=t == 0, stop=True, skip_group_check=True)
                    ins.then_inc(ym_done, 1)

                pe.wait_ge(xdt_ready, 3 * g + 3)
                running(0)
                pe.wait_ge(xw_ready, 3 * g + 3)
                M(bank[6][:, :], Brow[:, 0, :], xw[:, 0, :], start=True, stop=True).then_inc(u_ps, 1)
                pe.wait_ge(s1_ready, 2 * g + 1)
                pe.wait_ge(gm_ready, g + 1)
                M(bank[7][:, :], BC[:, 1, tiles(1)], S1[:, :], start=True, stop=True).then_inc(yo_ps, 1)
                M(bank[6][:, :], Brow[:, 1, :], xw[:, 1, :], start=True, stop=True).then_inc(u_ps, 1)
                pe.wait_ge(in_evac, 10 * g + 10)
                y_tile(0)
                running(1)
                pe.wait_ge(s_ld, 16 * (g + 1))
                pe.wait_ge(bm_ready, g + 1)
                pe.wait_ge(yo_ready, 2 * g + 1)
                for b in range(STREAMS):
                    ins = M(bank[7][:, :], Cm[:, b, :], S[:, b, :], start=b == 0, stop=b == STREAMS - 1)
                ins.then_inc(yo_ps, 1)
                y_tile(1)
                running(2)
                for b in range(STREAMS):
                    if b == 0:
                        pe.wait_ge(s1_ready, 2 * g + 2)
                    elif b == 1:
                        pe.wait_ge(yo_ready, 2 * g + 2)
                    else:
                        pe.wait_ge(su_done, 8 * g + b - 1)
                    M(bank[6 + b % 2][:, :], Bm[:, b, :], xw[:, 2, :], start=True, stop=True).then_inc(u_ps, 1)
                y_tile(2)
                pe.wait_ge(yl_ready, 4 * g + 4)
                pe.wait_ge(su_done, 8 * g + 8)
                for b in range(4):
                    n = group0(g) + 10 + b
                    weights(n)
                    for x in range(2):
                        j = 2 * b + x
                        if b >= 2:
                            pe.wait_ge(f_evac, 8 * g + j - 3)
                        ins = product(bank[4 + j % 4][:, 0:TOK], n % SLOTS, 4 * x, 4 * x + 4, lambda k: yh[:, k % 4, :],
                                      lambda k: yl[:, k % 4, :], True, True)
                    ins.then_inc(blk, 1)
            pe.wait_ge(sqy, 16)
            pe.wait_ge(f_evac, 8 * GROUPS)
            M(bank[7][:, 0:TOK], ones[:, :], sqacc[:, 0, :], start=True, stop=True).then_inc(yms, 1)
            gate_up(1, 2)
            down(1, 3)
            ple_pe(0, 3)

            def token_rows(m, x):
                pe.wait_ge(rstd_ready, m + 1)
                for t in range(TT):
                    ins = nc.tensor.transpose(bank[4][:, tiles(t)], rstd[:, m % 2, tiles(t)], ident[:, :])
                ins.then_inc(rt_ps, 1)

            pe.wait_ge(kxl_ready, KD)
            k = 0
            for b in range(3):
                weights(KV + b)
                for kk in range(WIDTH[KV + b] // 288):
                    for t in range(TT):
                        ins = row_product(bank[t][:, 0:288], (KV + b) % SLOTS, 288 * kk, 288, kxh[:, k, tiles(t)],
                                          kxl[:, k, tiles(t)], k == 0, k == KD - 1)
                    k += 1
                ins.then_inc(blk, 1)
            norm_sum(4)
            token_rows(4, 0)
            pe.wait_ge(kv_done, TT)
            for t in range(TT):
                for k in range(2):
                    nc.tensor.transpose(bank[5 + k][:, tiles(t)], ckv[:, t, tiles(k)], ident[:, :])
                ins = nc.tensor.transpose(bank[4][0:ROPE, tiles(t)], krow[:, t, :], ident[:, :])
            ins.then_inc(cT_ps, 1)
            gate_up(2, 4)
            down(2, 5)

            pe.wait_ge(xl_ready, 48)
            for b in range(4):
                weights(DQ + b)
                for kk in range(2):
                    k = 2 * b + kk
                    for t in range(TT):
                        ins = row_product(bank[t][:, :], (DQ + b) % SLOTS, 512 * kk, 512, xh[:, k, tiles(t)],
                                          xl[:, k, tiles(t)], k == 0, k == KD - 1)
                ins.then_inc(blk, 1)
                if b == 0:
                    norm_sum(5)
            pe.wait_ge(cT_ready, 1)
            token_rows(5, 1)
            for t in range(TT):
                pe.wait_ge(cqn_ready, t + 1)
                for k in range(4):
                    ins = nc.tensor.transpose(bank[4 + k][:, tiles(t)], cqr[:, t, tiles(k)], ident[:, :])
            ins.then_inc(cqT_ps, 1)
            pe.wait_ge(cql, 4)

            def q_transpose(e):
                cg, t = divmod(e, TT)
                s = e % 2
                pe.wait_ge(qr_ready, e + 1)
                if e:
                    pe.wait_ge(qe, e)
                if t < 2:
                    for hh in range(4):
                        ins = nc.tensor.transpose(bank[6 + t][0:QD, tiles(hh)], kn[:, s, QD * hh:QD * hh + QD], ident[:, :])
                else:
                    for pp in range(2):
                        nc.tensor.transpose(bank[6][:, tiles(pp)], kn[:, s, tiles(pp)], ident[:, :])
                    for hh in range(4):
                        ins = nc.tensor.transpose(bank[7][0:ROPE, tiles(hh)], kn[:, s, 256 + 32 * hh:288 + 32 * hh], ident[:, :])
                ins.then_inc(qt_ps, 1)

            for cg in range(4):
                if cg >= 2:
                    pe.wait_ge(qb_evac, 3 * (cg - 1))
                for b in range(2):
                    n = QB + 2 * cg + b
                    weights(n)
                    for kk in range(2):
                        k = 2 * b + kk
                        for t in range(TT):
                            ins = row_product(bank[3 * (cg % 2) + t][:, 0:384], n % SLOTS, 384 * kk, 384, xh[:, k, tiles(t)],
                                              xl[:, k, tiles(t)], k == 0, k == 3)
                    ins.then_inc(blk, 1)
                if cg:
                    for t in range(TT):
                        q_transpose(3 * (cg - 1) + t)
            for t in range(TT):
                q_transpose(9 + t)

            def expand(w):
                if w < ITEMS:
                    t, g = divmod(w, 2)
                    src = cT[:, :, tiles(t)]
                else:
                    u, st = divmod(w - ITEMS, 4)
                    b, g = divmod(u, 2)
                    if g == 0 and st == 0:
                        pe.wait_ge(c_ld[b % 2], 16 * (b // 2 + 1))
                    src = cTb[:, b % 2, :, tiles(st)]
                if w >= 2:
                    pe.wait_ge(ks4, w - 1)
                for k in range(2):
                    ins = M(bank[w % 2][:, :], src[:, k, :], wk[:, k, 512 * g:512 * g + 512], start=k == 0, stop=k == 1)
                ins.then_inc(ex_ps, 1)

            def key_transpose(w):
                pe.wait_ge(ks4, w + 1)
                if w:
                    pe.wait_ge(kt_ev, w if w < ITEMS + 1 else w - 1)
                if w < 4:
                    for hh in range(8):
                        ins = nc.tensor.transpose(bank[2 + hh // 4][0:QD, tiles(hh % 4)], kn[:, w % 2, QD * hh:QD * hh + QD], ident[:, :])
                else:
                    for j in range(4):
                        ins = nc.tensor.transpose(bank[2 + w % 2][:, tiles(j)], kn[:, w % 2, tiles(j)], ident[:, :])
                ins.then_inc(kt_ps, 1)

            pe.wait_ge(w_ld, 64)
            pe.wait_ge(qb_evac, 12)
            expand(0)
            for w in range(ITEMS):
                if w + 1 < ITEMS:
                    expand(w + 1)
                key_transpose(w)
            pe.wait_ge(qe, 12)
            for v in range(4):
                for k in range(2):
                    ins = M(bank[4 + v][:, :], cT[:, k, tiles(v // 2)], wv[:, k, 512 * (v % 2):512 * (v % 2) + 512],
                            start=k == 0, stop=k == 1)
                ins.then_inc(vp_ps, 1)
            pe.wait_ge(vp_ev, 4)
            pe.wait_ge(kt_ev, ITEMS)

            def p_scores(x):
                if x >= 2:
                    pe.wait_ge(pa1, x - 1)
                out = bank[4 + x % 2]
                M(out[:, 0:128], Qp[0:QD, x, 0:128], Kp[0:QD, x, 0:128], start=True, stop=True)
                M(out[:, 128:384], Qp[0:QD, x, 128:256], Kp[0:QD, x, 0:256], start=True, stop=True).then_inc(qk_ps, 1)

            p_scores(0)
            for x in range(MH):
                if x + 1 < MH:
                    p_scores(x + 1)
                pe.wait_ge(pa4, x + 1)
                for j in range(3):
                    ins = nc.tensor.transpose(bank[6][:, tiles(j)], Pb[:, x % 2, tiles(j)], ident[:, :])
                ins.then_inc(pt_ps, 1)
                pe.wait_ge(pt_ev, x + 1)
                if x % 2 == 0 and x >= 4:
                    pe.wait_ge(ol_ready, x // 2 - 1)
                o = bank[7 if x // 2 % 2 else 1][VH * (x % 2):VH * (x % 2) + VH, :]
                v0, v1 = (Vp[:, k, VH * x:VH * x + VH] for k in range(2))
                M(o[:, 0:128], v0, PT[:, 0:128], start=True, stop=True)
                M(o[:, 128:256], v0, PT[:, 128:256], start=True, stop=False)
                M(o[:, 128:256], v1, PT[:, 256:384], start=False, stop=True).then_inc(po_ps, 1)
            pe.wait_ge(ol_ready, MH // 2)

            def s_scores(u):
                b, g = divmod(u, 2)
                pe.wait_ge(qbd_ready, b + 1)
                pe.wait_ge(kt_ev, ITEMS + 4 * (u + 1))
                if u:
                    pe.wait_ge(sa3, u)
                if g == 0:
                    pe.wait_ge(kr_ld, 16 * (b + 1))
                qr = QRTs[:, b, 8 * g:8 * g + 8, :].rearrange("p h q -> p (h q)")
                for out, keys, kr in ((bank[4][:, :], KT[:, u % 2], krTb[:, :]),
                                      (bank[5][:, 0:P], KTn[:, 4 * g:4 * g + 4], krT[:, SEQ:TOK])):
                    for j in range(4):
                        M(out, Qbd[:, 4 * g + j, :], keys[:, j, :], start=j == 0, stop=False)
                    ins = M(out, qr, kr, start=False, stop=True)
                ins.then_inc(sc_ps, 1)

            def s_transpose(u):
                pe.wait_ge(sa3, u + 1)
                if u:
                    pe.wait_ge(olt, u)
                for j in range(5):
                    ins = nc.tensor.transpose(bank[6][:, tiles(j)] if j < 4 else bank[7][:, 0:128], Pb[:, u % 2, tiles(j)], ident[:, :])
                ins.then_inc(pt_ps, 1)

            def s_latent(u):
                b = u // 2
                pe.wait_ge(pt_ev, MH + u + 1)
                if u % 2 == 0:
                    pe.wait_ge(cn_ld[b % 2], 16 * (b // 2 + 1))
                for j in range(5):
                    ins = M(bank[7][:, 256:512], PT[:, tiles(j)], cnat[:, b % 2, j, :] if j < 4 else ckv[:, 2, :],
                            start=j == 0, stop=j == 4)
                ins.then_inc(po_ps, 1)

            expand(ITEMS)
            for st in range(4):
                if st < 3:
                    expand(ITEMS + st + 1)
                key_transpose(ITEMS + st)
            for u in range(2 * STREAMS):
                nxt = ITEMS + 4 * (u + 1)
                more = u + 1 < 2 * STREAMS
                s_scores(u)
                if more:
                    expand(nxt)
                    expand(nxt + 1)
                    key_transpose(nxt)
                    key_transpose(nxt + 1)
                s_transpose(u)
                if more:
                    expand(nxt + 2)
                s_latent(u)
                if more:
                    expand(nxt + 3)
                    key_transpose(nxt + 2)
                    key_transpose(nxt + 3)
                pe.wait_ge(olr, u + 1)
                for k in range(2):
                    ins = nc.tensor.transpose(bank[7][:, tiles(k)], ol[:, tiles(k)], ident[:, :])
                ins.then_inc(ot_ps, 1)
            pe.wait_ge(olt, 2 * STREAMS)
            for x in range(MH):
                if x % 2 == 0 and x >= 4:
                    pe.wait_ge(ol_ready, MH // 2 + x // 2 - 1)
                o = bank[x // 2 % 2][VH * (x % 2):VH * (x % 2) + VH, 0:P]
                for k in range(2):
                    ins = M(o, wv[:, k, VH * x:VH * x + VH], OLT[:, k, x, :], start=k == 0, stop=k == 1)
                if x % 2:
                    ins.then_inc(os_ps, 1)
            pe.wait_ge(ol_ready, MH)
            for b in range(8):
                weights(WO + b)
                if b >= 4:
                    pe.wait_ge(h_new, 48 + b - 3)
                product(bank[2 + b % 4][:, 0:TOK], (WO + b) % SLOTS, 0, KD, *X, True, True).then_inc(blk, 1)
            gate_up(3, 6)
            down(3, 7)
            ple_pe(1, 7)


def tile_blocks(w, cols=P):
    k, m = w.shape
    return w.reshape(k // P, P, m // cols, cols).transpose(2, 1, 0, 3).reshape(m // cols, P, -1)


def kernel(**inp):
    import concourse.bacc as bacc
    from concourse.bass_utils import run_bass_kernel_spmd
    A = {k: np.asarray(v) for k, v in inp.items()}
    f32 = np.float32

    stream = np.zeros((NBLK, P, 1024), f32)

    def put(stage, blocks, first=0):
        b0 = BASE[stage] + first
        for j, w in enumerate(blocks):
            stream[b0 + j, :, :w.shape[-1]] = w

    for u, (l, s) in enumerate(((0, 1), (0, 2), (1, 1), (1, 2))):
        gate, up = (tile_blocks(A[f"w{s}_{x}"][l]) for x in ("gate", "up"))
        put(f"gu{u}", np.stack([gate, up], 1).reshape(2 * KF, P, 1024))
        down, at = tile_blocks(A[f"w{s}_down"][l]), [0, 8, 15, 22]
        put(f"dn{u}", [down[j][:, at[b] * P:at[b + 1] * P] for j in range(KD) for b in range(3)])
    w_in = A["a_in_proj"][0]
    w_dt = np.zeros((D_MODEL, P), f32)
    w_dt[:, :HEADS] = w_in[:, D_INNER + CONV_DIM:]
    put("mix", tile_blocks(w_dt))
    zt, ct = tile_blocks(w_in[:, :D_INNER]), tile_blocks(w_in[:, D_INNER:D_INNER + CONV_DIM])
    w_out = A["a_out_proj"][0]
    for g in range(GROUPS):
        put("mix", [ct[4 * g + i] for i in range(4)] + [ct[16 + g], ct[20 + g]] + [zt[4 * g + i] for i in range(4)], 1 + 14 * g)
        o = tile_blocks(w_out[512 * g:512 * g + 512])
        put("mix", o.reshape(4, 2, P, 512).transpose(0, 2, 1, 3).reshape(4, P, 1024), 1 + 14 * g + 10)
    for l in range(2):
        o = tile_blocks(A["w_ple_in"][l])
        put(f"pi{l}", o.reshape(2, 4, P, 256).transpose(0, 2, 1, 3).reshape(2, P, 1024))
        put(f"pg{l}", tile_blocks(A["w_ple_gate"][l]))

    def row_blocks(w, per):
        k = w.reshape(KD if w.shape[0] == D_MODEL else w.shape[0] // P, P, -1)
        return [k[i:i + per].transpose(1, 0, 2).reshape(P, -1) for i in range(0, k.shape[0], per)]

    put("kv", row_blocks(A["w_kv_a"], 3))
    put("dq", row_blocks(A["b_w_dq"][0], 2))
    for cg in range(4):
        put("qb", row_blocks(np.ascontiguousarray(A["b_w_q_b"][0][:, 384 * cg:384 * cg + 384]), 2), 2 * cg)
    put("wo", tile_blocks(A["b_w_o"][0]))

    def feat(x):
        return np.ascontiguousarray(x.reshape(x.shape[0], -1, P).transpose(2, 1, 0))

    def both(a, b):
        return np.concatenate([a.reshape(SEQ, -1), b.reshape(TOK - SEQ, -1)])

    def col(v):
        return v.reshape(-1, P).T

    def every(v):
        return np.ascontiguousarray(np.broadcast_to(v, (P,) + v.shape))

    arr = {"stream": stream, "x": feat(both(A["x_prompt"], A["x_sample"]))}
    arr["p"] = np.stack([feat(both(A["p_prompt"][l], A["p_sample"][l])) for l in range(2)])
    norm_gains = [A["ln_ffn1"][0], A["ln_mix"][0], A["ln_ffn2"][0], A["ln_ple"][0], A["ln_ffn1"][1], A["ln_mix"][1],
                  A["ln_ffn2"][1], A["ln_ple"][1], A["ln_kv"]]
    arr["gains"] = np.stack([col(v) for v in norm_gains], 1)
    arr["ident"] = np.eye(P, dtype=f32)
    arr["cstate"] = A["state_conv"][0].reshape(STREAMS, 3, KC, P).transpose(3, 2, 0, 1).reshape(P, KC, STREAMS * 3)
    arr["cw"] = np.concatenate([A["a_conv_w"][0], A["a_conv_b"]], 0).reshape(CONV_W + 1, KC, P).transpose(2, 1, 0)
    arr["dcol"] = col(np.repeat(A["a_D"][0], HD))
    arr["ang"] = col(A["a_norm"][0])
    row, cl = np.arange(P)[:, None], np.arange(P)[None, :]
    tri, blk16 = (row <= cl), (row // STEPS == cl // STEPS)
    arr["mask"] = np.stack([tri, tri, tri & blk16], 1).astype(f32)
    arr["same"] = blk16.astype(f32)
    arr["ind"] = (row // STEPS == np.arange(STREAMS)[None, :]).astype(f32)
    arr["dts"] = np.stack([A["a_dt_bias"][0], A["a_A_log"][0]], 1)
    arr["ssm"] = A["state_ssm"][0].reshape(STREAMS, GROUPS, 512, N).transpose(1, 3, 0, 2)
    arr["kvg"] = every(np.concatenate([A["kv_norm"], A["kr_norm"]]))
    inv = f32(10000.0) ** (-np.arange(ROPE // 2, dtype=f32) / f32(ROPE // 2))
    pos = np.concatenate([np.arange(SEQ), np.tile(PAST + np.arange(STEPS), STREAMS)]).astype(f32)
    ang_ = pos[:, None] * inv[None, :]
    arr["cos"] = np.cos(ang_).astype(f32).reshape(TT, P, -1).transpose(1, 0, 2)
    arr["sin"] = np.sin(ang_).astype(f32).reshape(TT, P, -1).transpose(1, 0, 2)
    arr["qgr"] = every(A["b_q_norm"][0])
    arr["qg96"] = every(np.stack([np.concatenate([A["b_qn_nope"][0], A["b_qn_rope"][0]]),
                                  np.concatenate([A["k_norm"], np.zeros(ROPE, f32)])]))
    wkv = A["w_kv_b"].reshape(2, P, MH, NOPE + VH)
    arr["wk"] = wkv[..., :NOPE].transpose(1, 0, 2, 3).reshape(P, 2, -1)
    arr["wv"] = wkv[..., NOPE:].transpose(1, 0, 2, 3).reshape(P, 2, -1)
    diag = np.where((cl // 64) <= (row // 64), 0.0, -1e30).astype(f32)
    arr["mk"] = np.concatenate([diag, np.zeros((P, P), f32), diag], 1)
    cache = A["cache_kv_latent"]
    arr["cache"] = cache.reshape(STREAMS, 4, P, KV_LORA).transpose(0, 2, 1, 3)
    arr["cacheT"] = cache.reshape(STREAMS, PAST, 2, P).transpose(0, 3, 2, 1)
    arr["krcT"] = A["cache_k_rope"].transpose(0, 2, 1)
    outs = {"y": (P, KD, TOK), "ssm_p": (GROUPS, P, 512), "ssm_s": (GROUPS, P, STREAMS, 512),
            "conv": (P, KC, 27), "kvl": (P, TT, KV_LORA), "kr": (P, TT, ROPE)}

    nc = bacc.Bacc("TRN2", target_bir_lowering=False, num_devices=1)
    T = {}
    sent = {}
    for name, a in arr.items():
        sent[f"in_{name}"] = np.ascontiguousarray(a)
        T[name] = nc.dram_tensor(f"in_{name}", a.shape, F32, kind="ExternalInput").ap()
    for name, shape in outs.items():
        T[name] = nc.dram_tensor(f"out_{name}", shape, F32, kind="ExternalOutput").ap()
    build(nc, T)
    got = run_bass_kernel_spmd(nc, [sent], core_ids=[0]).results[0]
    got = {name: np.asarray(got[f"out_{name}"]) for name in outs}

    y = got["y"].transpose(2, 1, 0).reshape(TOK, D_MODEL)
    kvl = got["kvl"].transpose(1, 0, 2).reshape(TOK, KV_LORA)
    kr = got["kr"].transpose(1, 0, 2).reshape(TOK, ROPE)
    conv = got["conv"].transpose(2, 1, 0).reshape(27, CONV_DIM)
    ssm_p = got["ssm_p"].reshape(GROUPS, N, HPG, HD).transpose(0, 2, 3, 1).reshape(1, 1, HEADS, HD, N)
    ssm_s = got["ssm_s"].reshape(GROUPS, N, STREAMS, HPG, HD).transpose(2, 0, 3, 4, 1).reshape(1, STREAMS, HEADS, HD, N)
    outs_ = (y[:SEQ].reshape(1, SEQ, D_MODEL), y[SEQ:].reshape(STREAMS, STEPS, D_MODEL),
             conv[:3].reshape(1, 1, 3, CONV_DIM), ssm_p,
             kvl[:SEQ].reshape(1, SEQ, KV_LORA), kr[:SEQ].reshape(1, SEQ, ROPE),
             conv[3:].reshape(1, STREAMS, 3, CONV_DIM), ssm_s,
             kvl[SEQ:].reshape(STREAMS, STEPS, KV_LORA), kr[SEQ:].reshape(STREAMS, STEPS, ROPE))
    return tuple(np.ascontiguousarray(o) for o in outs_)
```

```python
import concourse.bass as bass
from concourse import mybir
from contextlib import ExitStack
import numpy as np

F32 = mybir.dt.float32
F32R = mybir.dt.float32r
ALU = mybir.AluOpType
ACT = mybir.ActivationFunctionType
AX = mybir.AxisListType

P = 128
D_MODEL = 1024
SEQ, STREAMS, STEPS = 256, 8, 16
TOK = SEQ + STREAMS * STEPS
TT = TOK // P
KD = D_MODEL // P
D_FF = 2816
KF = D_FF // P
PLE = 256
D_INNER = 2048
HEADS, HD, GROUPS, N = 32, 64, 4, 128
HPG = HEADS // GROUPS
CONV_W = 4
CONV_DIM = D_INNER + 2 * GROUPS * N
KC = CONV_DIM // P
PAST = 512
MH, NOPE, ROPE, VH = 16, 64, 32, 64
QD = NOPE + ROPE
Q_LORA, KV_LORA = 512, 256
SCALE = (NOPE + ROPE) ** -0.5
EPS = 1e-6

SLOTS = 4
AHEAD = 3
STAGES = [("gu0", 44), ("dn0", 24), ("mix", 57), ("gu1", 44), ("dn1", 24), ("pi0", 2), ("pg0", 8),
          ("kv", 3), ("gu2", 44), ("dn2", 24), ("dq", 4), ("qb", 8), ("wo", 8), ("gu3", 44),
          ("dn3", 24), ("pi1", 2), ("pg1", 8)]
DN_TILES = (8, 7, 7)
BASE, WIDTH = {}, []
for _name, _n in STAGES:
    BASE[_name] = len(WIDTH)
    for _b in range(_n):
        WIDTH.append(DN_TILES[_b % 3] * P if _name[:2] == "dn" else
                     (864, 864, 576)[_b] if _name == "kv" else 2 * 384 if _name == "qb" else 1024)
NBLK = len(WIDTH)
NORMS = 8


def build(nc, T):
    ctx = ExitStack()
    with ctx:
        def sb(name, shape, dt=F32, c=ctx):
            return c.enter_context(nc.sbuf_tensor(name, shape, dt))

        def sem(name):
            return ctx.enter_context(nc.semaphore(name))

        h = sb("h", [P, KD, TOK])
        xh = sb("xh", [P, KD, TOK], F32R)
        xl = sb("xl", [P, KD, TOK], F32R)
        raw = sb("raw", [P, SLOTS, 1024])
        whi = sb("whi", [P, SLOTS, 1024], F32R)
        wlo = sb("wlo", [P, SLOTS, 1024], F32R)
        gains = sb("gains", [P, NORMS + 1, KD])
        ident = sb("ident", [P, P])
        ones = sb("ones", [P, P])
        std = sb("std", [P, TOK])
        rstd = sb("rstd", [P, 2, TOK])
        sqt = sb("sqt", [P, TOK])
        sqacc = sb("sqacc", [P, 2, TOK])
        rows = sb("rows", [P, 2, TT])
        bank = [ctx.enter_context(nc.psum_tensor(f"bank{i}", [P, 512], F32)) for i in range(8)]

        with ExitStack() as ffn:
            ah = sb("ah", [P, KF, TOK], F32R, ffn)
            al = sb("al", [P, KF, TOK], F32R, ffn)
            tg = sb("tg", [P, 2, TOK], F32, ffn)
            tu = sb("tu", [P, 2, TOK], F32, ffn)
        XPW = 3 + SEQ + STREAMS * (3 + STEPS)
        CW = XPW - 3
        SAMP0 = 3 + SEQ
        with ExitStack() as ssd:
            yh = sb("yh", [P, 4, TOK], F32R, ssd)
            yl = sb("yl", [P, 4, TOK], F32R, ssd)
            facc = sb("facc", [P, KD, TOK], F32, ssd)
            zs = sb("zs", [P, 4, TOK], F32, ssd)
            xsT = sb("xsT", [P, 4, TOK], F32, ssd)
            BC = sb("BC", [P, 2, TOK], F32, ssd)
            xdt = sb("xdt", [P, TT, 512], F32, ssd)
            xw = sb("xw", [P, TT, 512], F32, ssd)
            seg = sb("seg", [P, 2, 1024], F32, ssd)
            Gm = sb("Gm", [P, TOK], F32, ssd)
            Brow = sb("Brow", [P, TT, P], F32, ssd)
            Bm = sb("Bm", [P, STREAMS, P], F32, ssd)
            Cm = sb("Cm", [P, STREAMS, P], F32, ssd)
            S = sb("S", [P, STREAMS, 512], F32, ssd)
            S1 = sb("S1", [P, 512], F32, ssd)
            yoff = sb("yoff", [P, 2, 512], F32, ssd)
            xp = sb("xp", [P, 2, XPW + 1], F32, ssd)
            cy = sb("cy", [P, 2, XPW + 1], F32, ssd)
            cstate = sb("cstate", [P, KC, STREAMS * 3], F32, ssd)
            cout = sb("cout", [P, KC, 3 + STREAMS * 3], F32, ssd)
            cw = sb("cw", [P, KC, CONV_W + 1], F32, ssd)
            dcol = sb("dcol", [P, 16], F32, ssd)
            ang = sb("ang", [P, 16], F32, ssd)
            mask = sb("mask", [P, TT, P], F32, ssd)
            same = sb("same", [P, P], F32, ssd)
            ind = sb("ind", [P, STREAMS], F32, ssd)
            dtR = sb("dtR", [P, TT, HEADS], F32, ssd)
            aR = sb("aR", [P, TT, HEADS], F32, ssd)
            acs = sb("acs", [P, TT, HEADS], F32, ssd)
            toend = sb("toend", [P, TT, HEADS], F32, ssd)
            eacs = sb("eacs", [P, TT, HEADS], F32, ssd)
            dec = sb("dec", [P, STREAMS + 1, HEADS], F32, ssd)
            dts = sb("dts", [HEADS, 2], F32, ssd)
        am = Bm[:, 0:2, :].rearrange("p a b -> p (a b)").rearrange("p (s h) -> p s h", s=STREAMS)
        dv = [seg[0:HEADS, i // 2, (i % 2) * TOK:(i % 2 + 1) * TOK] for i in range(4)] + \
             [xdt[0:HEADS, i, 0:TOK] for i in range(3)]
        with ExitStack() as ple:
            phi = sb("phi", [P, 2, TOK], F32R, ple)
            plo = sb("plo", [P, 2, TOK], F32R, ple)
            pin = sb("pin", [P, KD, TOK], F32, ple)
            tp = sb("tp", [P, 2, TOK], F32, ple)
            kxh = sb("kxh", [P, KD, TOK], F32R, ple)
            kxl = sb("kxl", [P, KD, TOK], F32R, ple)
            kvr = sb("kvr", [P, TT, KV_LORA + ROPE], F32, ple)
            krot = sb("krot", [P, TT, 2, ROPE], F32, ple)
        with ExitStack() as mla:
            lowA = sb("lowA", [P, 4096], F32, mla)
            lowB = sb("lowB", [P, 4096], F32, mla)
            lowC = sb("lowC", [P, 2048], F32, mla)
            Qs = sb("Qs", [P, STREAMS, MH, STEPS], F32, mla)
            with ExitStack() as split:
                wk = sb("wk", [P, 2, MH * NOPE], F32, split)
            wkl = sb("wkl", [P, 2, MH * NOPE], F32R, mla)
            wkh = sb("wkh", [P, 2, MH * NOPE], F32R, mla)
            wv = sb("wv", [P, 2, MH * VH], F32, mla)
            cTh = sb("cTh", [P, 2, 2, PAST], F32R, mla)
            ckv = sb("ckv", [P, TT, KV_LORA], F32, mla)
            cT = sb("cT", [P, 2, TOK], F32, mla)
            krT = sb("krT", [P, TOK], F32, mla)
            krow = sb("krow", [P, TT, QD], F32, mla)
            rsc = sb("rsc", [P, TT, 8], F32, mla)
            cosr = sb("cosr", [P, TT, ROPE], F32, mla)
            sinr = sb("sinr", [P, TT, ROPE], F32, mla)
            with ExitStack() as split:
                cTb = sb("cTb", [P, 2, 2, PAST], F32, split)
            cTl = sb("cTl", [P, 2, 2, PAST], F32R, mla)
            sq5 = sb("sq5", [P, 2, 512], F32, mla)
            rsn = sb("rsn", [P, MH], F32, mla)
            kn = sb("kn", [P, 2, 8 * QD], F32, mla)
            Pb = sb("Pb", [P, 2, 640], F32, mla)
            gq = sb("gq", [P, 3], F32, mla)
            gr = sb("gr", [P, ROPE], F32, mla)
            sm = sb("sm", [P, 128], F32, mla)
        Kp = lowA[:, :].rearrange("p (h t) -> p h t", h=MH)
        wkT = lowA[:, :].rearrange("p (h c) -> p h c", h=MH)
        QC = lowB[:, :].rearrange("p (k b h q) -> p k b h q", k=2, b=STREAMS, h=MH)
        Qp = lowB[:, :].rearrange("p (h t) -> p h t", h=MH)
        cnat = lowC[:, :].rearrange("p (s k c) -> p s k c", s=2, k=4)
        Vp = lowC[:, :].rearrange("p (k c) -> p k c", k=2)
        PT = rstd[:, :, :].rearrange("p a t -> p (a t)")[:, 0:640]
        ol = std[:, 0:KV_LORA]
        rbn = sqt[:, 0:2 * P].rearrange("p (g t) -> p g t", g=2)
        ksq = sqacc[:, :, :].rearrange("p a t -> p (a t)")[:, 0:STREAMS * 4 * MH].rearrange(
            "p (b s h) -> p b s h", b=STREAMS, s=4)
        krTb = ckv[:, 0:2, :].rearrange("p a c -> p (a c)")
        cqr = lowC[:, 0:TT * Q_LORA].rearrange("p (t c) -> p t c", t=TT)
        qgr = Pb[:, 0, 0:Q_LORA]
        mk = krTb[:, 0:TOK]
        praw = cTb[:, 0, :, 0:TOK]
        kvg = kn[:, 0, 0:KV_LORA + ROPE]
        rq = sq5
        rk = kn

        raw_loaded = [sem(f"raw_loaded{i}") for i in range(4)]
        hi_ready = sem("hi_ready")
        lo_ready = sem("lo_ready")
        blk = sem("blk")
        x_ld = sem("x_ld")
        const_ld = sem("const_ld")
        ones_ready = sem("ones_ready")
        h_new = sem("h_new")
        sq_done = sem("sq_done")
        sq_step = sem("sq_step")
        ms_ready = sem("ms_ready")
        std_ready = sem("std_ready")
        rstd_ready = sem("rstd_ready")
        xh_ready = sem("xh_ready")
        xl_ready = sem("xl_ready")
        gu_evac = sem("gu_evac")
        sg_ready = sem("sg_ready")
        a_ready = sem("a_ready")
        ah_ready = sem("ah_ready")
        al_ready = sem("al_ready")
        dve_chain = sem("dve_chain")
        act_chain = sem("act_chain")
        in_evac = sem("in_evac")
        c0_ready = sem("c0_ready")
        conv_ready = sem("conv_ready")
        conv_done = sem("conv_done")
        z_done = sem("z_done")
        dt_v = sem("dt_v")
        dt_a = sem("dt_a")
        dt_ready = sem("dt_ready")
        dtT_ps = sem("dtT_ps")
        dtR_ready = sem("dtR_ready")
        ac_ps = sem("ac_ps")
        acs_ready = sem("acs_ready")
        da_ready = sem("da_ready")
        xt_ps = sem("xt_ps")
        bt_ps = sem("bt_ps")
        xdt_ready = sem("xdt_ready")
        xw_ready = sem("xw_ready")
        brow_ready = sem("brow_ready")
        bm_ready = sem("bm_ready")
        g_ps = sem("g_ps")
        gm_ready = sem("gm_ready")
        ab_ps = sem("ab_ps")
        d_ready = sem("d_ready")
        mn_ready = sem("mn_ready")
        e_ready = sem("e_ready")
        m_ready = sem("m_ready")
        u_ps = sem("u_ps")
        s1_ready = sem("s1_ready")
        s1_store = sem("s1_store")
        s_ld = sem("s_ld")
        s_store = sem("s_store")
        cm_zero = sem("cm_zero")
        yo_ps = sem("yo_ps")
        yo_ready = sem("yo_ready")
        ym_done = sem("ym_done")
        su_done = sem("su_done")
        y_evac = sem("y_evac")
        y_ready = sem("y_ready")
        yh_ready = sem("yh_ready")
        yl_ready = sem("yl_ready")
        sqy = sem("sqy")
        f_evac = sem("f_evac")
        yms = sem("yms")
        ystd = sem("ystd")
        cout_ready = sem("cout_ready")
        p_ld = sem("p_ld")
        ph_ready = sem("ph_ready")
        pl_ready = sem("pl_ready")
        pin_ready = sem("pin_ready")
        pg_evac = sem("pg_evac")
        sgm_ready = sem("sgm_ready")
        kxh_ready = sem("kxh_ready")
        kxl_ready = sem("kxl_ready")
        rt_ps = sem("rt_ps")
        rows_ready = sem("rows_ready")
        kvr_ready = sem("kvr_ready")
        kvs = sem("kvs")
        kv_done = sem("kv_done")
        cT_ps = sem("cT_ps")
        cT_ready = sem("cT_ready")
        kr_zero = sem("kr_zero")
        wk_hi = sem("wk_hi")
        wk_lo = sem("wk_lo")
        past_hi = sem("past_hi")
        past_lo = sem("past_lo")
        past_ps = sem("past_ps")
        past_sq = sem("past_sq")
        past_sum = sem("past_sum")
        past_std = sem("past_std")
        past_rstd = sem("past_rstd")
        wkT_ld = sem("wkT_ld")
        qc_ps = sem("qc_ps")
        qc_ev = sem("qc_ev")
        new_rq = sem("new_rq")
        new_rt = sem("new_rt")
        new_rk = sem("new_rk")
        rq_ready = sem("rq_ready")
        rt_done = sem("rt_done")
        rk_ready = sem("rk_ready")
        sa1 = sem("sa1")
        cq_ready = sem("cq_ready")
        cqs = sem("cqs")
        cqn_ready = sem("cqn_ready")
        cqT_ps = sem("cqT_ps")
        cqh = sem("cqh")
        cql = sem("cql")
        qs1 = sem("qs1")
        qs2 = sem("qs2")
        qs3 = sem("qs3")
        gq_ready = sem("gq_ready")
        qb_evac = sem("qb_evac")
        qr_ready = sem("qr_ready")
        qt_ps = sem("qt_ps")
        qe = sem("qe")
        w_ld = sem("w_ld")
        mla_zero = sem("mla_zero")
        ex_ps = sem("ex_ps")
        ks1 = sem("ks1")
        ks2 = sem("ks2")
        ks3 = sem("ks3")
        ks4 = sem("ks4")
        kt_ps = sem("kt_ps")
        kt_ev = sem("kt_ev")
        vp_ps = sem("vp_ps")
        vp_ev = sem("vp_ev")
        qk_ps = sem("qk_ps")
        pa1 = sem("pa1")
        pa2 = sem("pa2")
        pa3 = sem("pa3")
        pa4 = sem("pa4")
        pt_ps = sem("pt_ps")
        pt_ev = sem("pt_ev")
        po_ps = sem("po_ps")
        oh_ready = sem("oh_ready")
        ol_ready = sem("ol_ready")
        c_ld = [sem(f"c_ld{i}") for i in range(2)]
        kr_ld = sem("kr_ld")
        cn_ld = [sem(f"cn_ld{i}") for i in range(2)]
        sc_ps = sem("sc_ps")
        sa2 = sem("sa2")
        sa3 = sem("sa3")
        olr = sem("olr")
        ot_ps = sem("ot_ps")
        olt = sem("olt")
        os_ps = sem("os_ps")
        out_st = sem("out_st")
        mk_ld = sem("mk_ld")

        block = ctx.enter_context(nc.Block())
        MIX, PI, PG, KV, DQ, QB, WO = (BASE[x] for x in ("mix", "pi0", "pg0", "kv", "dq", "qb", "wo"))
        ITEMS = 6
        UNITS = 2 * STREAMS
        CRED = SLOTS

        def group0(g):
            return MIX + 1 + 14 * g

        def tiles(t, w=P):
            return slice(t * w, (t + 1) * w)

        def bc(ap, shape, axis):
            return ap.unsqueeze(axis).broadcast_to(shape)

        def samp(t):
            return t[:, SAMP0:XPW].rearrange("p (s t) -> p s t", s=STREAMS)

        @block.sync
        def _(sp):
            sp.dma_start(h[:, :, :], T["x"]).then_inc(x_ld, 16)
            for r in range(SLOTS):
                sp.dma_start(raw[:, r, :], T["stream"][r]).then_inc(raw_loaded[r], 16)
            with sp.Fori(1, NBLK // SLOTS) as i:
                for r in range(SLOTS):
                    sp.wait_ge(lo_ready, i * SLOTS + (r - SLOTS + 1))
                    sp.dma_start(raw[:, r, :], T["stream"][i * SLOTS + r]).then_inc(raw_loaded[r], 16)

        @block.gpsimd
        def _(pool):
            c = [0]

            def step(ins):
                c[0] += 1
                ins.then_inc(sq_step, 1)
                pool.wait_ge(sq_step, c[0])

            def squares(m):
                acc = sqacc[:, m % 2, :]
                for k in range(KD):
                    pool.wait_ge(h_new, 8 * m + k + 1)
                    if k == 0:
                        step(pool.tensor_tensor(acc, h[:, k, :], h[:, k, :], ALU.mult))
                    else:
                        step(pool.tensor_tensor(sqt[:, :], h[:, k, :], h[:, k, :], ALU.mult))
                        step(pool.tensor_tensor(acc, acc, sqt[:, :], ALU.add))
                pool.sem_inc(sq_done, 1)

            pool.dma_start(gains[:, :, :], T["gains"]).then_inc(const_ld, 16)
            pool.dma_start(ident[:, :], T["ident"]).then_inc(const_ld, 16)
            for t, name in ((cstate, "cstate"), (cw, "cw"), (dcol, "dcol"), (ang, "ang"), (mask, "mask"),
                            (same, "same"), (ind, "ind"), (dts, "dts")):
                pool.dma_start(t[:], T[name]).then_inc(const_ld, 16)
            pool.memset(ones[:, :], 1.0).then_inc(ones_ready, 1)
            pool.memset(xp[:, :, :], 0.0).then_inc(ones_ready, 1)
            squares(0)
            squares(1)
            pool.wait_ge(blk, CRED + MIX)
            pool.dma_start(S[:, :, :], T["ssm"][0]).then_inc(s_ld, 16)
            pool.memset(Cm[:, :, :], 0.0).then_inc(cm_zero, 1)
            for g in range(GROUPS):
                pool.wait_ge(s1_ready, 2 * g + 2)
                pool.dma_start(T["ssm_p"][g], S1[:, :]).then_inc(s1_store, 16)
                pool.wait_ge(su_done, 8 * g + 8)
                pool.dma_start(T["ssm_s"][g], S[:, :, :]).then_inc(s_store, 16)
                for i in range(4):
                    pool.wait_ge(y_ready, 4 * g + i + 1)
                    if g == 0 and i == 0:
                        step(pool.tensor_tensor(sqacc[:, 0, :], zs[:, i, :], zs[:, i, :], ALU.mult))
                    else:
                        step(pool.tensor_tensor(sqt[:, :], zs[:, i, :], zs[:, i, :], ALU.mult))
                        step(pool.tensor_tensor(sqacc[:, 0, :], sqacc[:, 0, :], sqt[:, :], ALU.add))
                    pool.sem_inc(sqy, 1)
                pool.wait_ge(s_store, 16 * (g + 1))
                if g < GROUPS - 1:
                    pool.dma_start(S[:, :, :], T["ssm"][g + 1]).then_inc(s_ld, 16)
            pool.wait_ge(cout_ready, KC)
            pool.dma_start(T["conv"], cout[:, :, :]).then_inc(out_st, 16)
            pool.wait_ge(out_st, 16)
            pool.wait_ge(s1_store, 16 * GROUPS)
            squares(2)
            pool.dma_start(praw, T["p"][0]).then_inc(p_ld, 16)
            pool.dma_start(kvg, T["kvg"]).then_inc(p_ld, 16)
            pool.dma_start(cosr[:], T["cos"]).then_inc(p_ld, 16)
            pool.dma_start(sinr[:], T["sin"]).then_inc(p_ld, 16)
            pool.memset(krow[:, :, :], 0.0).then_inc(kr_zero, 1)
            squares(3)
            squares(4)
            pool.wait_ge(kv_done, TT)
            pool.dma_start(T["kvl"], ckv[:, :, :]).then_inc(out_st, 16)
            pool.dma_start(T["kr"], krow[:, :, NOPE:QD]).then_inc(out_st, 16)
            squares(5)
            pool.wait_ge(blk, CRED + DQ)
            pool.dma_start(qgr, T["qgr"]).then_inc(w_ld, 16)
            pool.dma_start(gr[:], T["gr"]).then_inc(w_ld, 16)
            pool.dma_start(gq[:, 0:2], T["gq"]).then_inc(w_ld, 16)
            pool.dma_start(wk[:], T["wk"]).then_inc(w_ld, 16)
            pool.dma_start(wv[:], T["wv"]).then_inc(w_ld, 16)
            pool.wait_ge(out_st, 16 * 3)
            pool.wait_ge(cT_ready, 1)
            pool.dma_start(mk, T["mk"]).then_inc(mk_ld, 16)
            for b in range(STREAMS):
                if b >= 2:
                    pool.wait_ge(past_ps, 8 * (b - 1))
                pool.dma_start(cTb[:, b % 2, :, :], T["cacheT"][b]).then_inc(c_ld[b % 2], 16)
            pool.wait_ge(qk_ps, MH)
            pool.dma_start(wkT[0:QD], T["wkT"]).then_inc(wkT_ld, 16)

            def past_latent(b):
                if b < 2:
                    pool.wait_ge(past_ps, 8 * (STREAMS - 1 + b))
                else:
                    pool.wait_ge(sc_ps, 2 * (b - 1))
                pool.dma_start(cTb[:, b % 2, :, :], T["cacheT"][b]).then_inc(c_ld[b % 2], 16)
                if b < 2:
                    pool.wait_ge(po_ps, MH)
                else:
                    pool.wait_ge(po_ps, MH + 2 * (b - 1))
                pool.dma_start(cnat[:, b % 2], T["cache"][b]).then_inc(cn_ld[b % 2], 16)

            def past_rope(b):
                if b == 0:
                    pool.wait_ge(pa1, MH)
                    pool.memset(krTb[:, :], 0.0).then_inc(mla_zero, 1)
                    pool.wait_ge(mla_zero, 1)
                else:
                    pool.wait_ge(sc_ps, 2 * b)
                pool.dma_start(krTb[NOPE:QD], T["krcT"][b]).then_inc(kr_ld, 16)

            past_latent(0)
            past_rope(0)
            pool.wait_ge(ks4, ITEMS)
            for g in range(2):
                pool.tensor_copy(rq[:, 0, tiles(g)].rearrange("p (h q) -> p h q", h=8),
                                 bc(rsn[:, 8 * g:8 * g + 8], (P, 8, STEPS), 2)).then_inc(new_rq, 1)
            pool.wait_ge(past_rstd, 1)
            for u in range(UNITS):
                b, g = divmod(u, 2)
                if u == 0:
                    pool.wait_ge(new_rt, 1)
                if u >= 2:
                    pool.wait_ge(rt_done, u - 1)
                for st in range(4):
                    ins = pool.tensor_copy(rq[:, u % 2, tiles(st)].rearrange("p (h q) -> p h q", h=8),
                                           bc(ksq[:, b, st, 8 * g:8 * g + 8], (P, 8, STEPS), 2))
                ins.then_inc(rq_ready, 1)
                if b + 1 < STREAMS:
                    if g == 0:
                        past_latent(b + 1)
                    else:
                        past_rope(b + 1)
            pool.wait_ge(cn_ld[1], 16 * 4)
            squares(6)
            pool.dma_start(praw, T["p"][1]).then_inc(p_ld, 16)
            squares(7)
            for k in range(KD):
                pool.wait_ge(h_new, 8 * NORMS + k + 1)
                pool.dma_start(T["y"][:, k, :], h[:, k, :]).then_inc(out_st, 16)
            pool.wait_ge(out_st, 16 * (3 + KD))

        @block.scalar
        def _(act):
            A = nc.scalar.activation
            c = [0]

            def step(ins):
                c[0] += 1
                ins.then_inc(act_chain, 1)
                act.wait_ge(act_chain, c[0])

            def hi_split(n, i=0):
                if n >= NBLK:
                    return
                r = n % SLOTS
                act.wait_ge(raw_loaded[r], i * 16 + 16 * (n // SLOTS + 1))
                act.wait_ge(blk, i * SLOTS + (n + 1))
                w = WIDTH[n]
                A(whi[:, r, 0:w], raw[:, r, 0:w], ACT.Copy).then_inc(hi_ready, 1)

            def norm_std(m):
                act.wait_ge(ms_ready, m + 1)
                A(std[:, :], bank[7][:, 0:TOK], ACT.Sqrt, bias=EPS, scale=1.0 / D_MODEL).then_inc(std_ready, 1)

            def x_hi(m, k):
                act.wait_ge(h_new, 8 * m + k + 1)
                A(xh[:, k, :], h[:, k, :], ACT.Copy, scale=gains[:, m, k:k + 1]).then_inc(xh_ready, 1)

            def gate_up(u):
                base = BASE[f"gu{u}"]

                def pair(i, n0):
                    for j in range(2):
                        n, fs = base + n0 + 2 * j, KF * u + n0 // 2 + j
                        hi_split(n + 3, i)
                        act.wait_ge(gu_evac, i * 2 + (2 + fs + 1))
                        A(tg[:, j, :], tg[:, j, :], ACT.Silu).then_inc(sg_ready, 1)
                        hi_split(n + 4, i)
                        act.wait_ge(a_ready, i * 2 + (fs + 1))
                        A(ah[:, i * 2 + (n0 // 2 + j), :], tu[:, j, :], ACT.Copy).then_inc(ah_ready, 1)
                act.preload_act_table(ACT.Silu)
                with act.Fori(0, KF // 2 - 1) as i:
                    pair(i, 0)
                pair(0, 2 * KF - 4)

            def down(u, m):
                for j in range(KD):
                    for b in range(3):
                        hi_split(BASE[f"dn{u}"] + 3 * j + b + 3)
                    x_hi(m, j)

            def ple_act(l, m):
                act.wait_ge(p_ld, 64 + 16 * l)
                A(phi[:, :, :], praw, ACT.Copy).then_inc(ph_ready, 1)
                norm_std(m)
                for i in range(2):
                    n = BASE[f"pi{l}"] + i
                    hi_split(n + 3)
                    act.wait_ge(blk, CRED + n + 1)
                    for jj in range(4):
                        A(pin[:, 4 * i + jj, :], bank[jj][:, 0:TOK], ACT.Copy).then_inc(pin_ready, 1)
                for j in range(KD):
                    n = BASE[f"pg{l}"] + j
                    hi_split(n + 3)
                    act.wait_ge(pg_evac, 8 * l + j + 1)
                    A(tp[:, j % 2, :], tp[:, j % 2, :], ACT.Sigmoid).then_inc(sgm_ready, 1)

            for r in range(AHEAD):
                act.wait_ge(raw_loaded[r], 16)
                A(whi[:, r, 0:WIDTH[r]], raw[:, r, 0:WIDTH[r]], ACT.Copy).then_inc(hi_ready, 1)
            act.wait_ge(const_ld, 160)
            for k in range(KD):
                x_hi(0, k)
            norm_std(0)
            gate_up(0)
            down(0, 1)

            norm_std(1)
            hi_split(MIX + 3)
            for g in range(GROUPS):
                for b in range(10):
                    n, s, e = group0(g) + b, b % 2, 6 * g + b
                    hi_split(n + 3)
                    if b < 6:
                        ch = 4 * g + b if b < 4 else 16 + 4 * (b - 4) + g
                        step(A(samp(xp[:, s, :])[:, :, 0:3], cstate[:, ch, :].rearrange("p (s t) -> p s t", t=3), ACT.Copy))
                        act.wait_ge(in_evac, 10 * g + b + 1)
                        A(cout[:, ch, 0:3], xp[:, s, SEQ:SEQ + 3], ACT.Copy)
                        A(cout[:, ch, 3:27].rearrange("p (s t) -> p s t", t=3), samp(xp[:, s, :])[:, :, STEPS:STEPS + 3],
                          ACT.Copy).then_inc(cout_ready, 1)
                        A(cy[:, s, 0:CW], xp[:, s, 0:CW], ACT.Identity, bias=cw[:, ch, CONV_W:CONV_W + 1],
                          scale=cw[:, ch, 0:1]).then_inc(c0_ready, 1)
                        act.wait_ge(conv_ready, e + 1)
                        dst = xsT[:, b, :] if b < 4 else BC[:, b - 4, :]
                        A(dst[:, 0:SEQ], cy[:, s, 0:SEQ], ACT.Silu)
                        A(dst[:, SEQ:TOK].rearrange("p (s t) -> p s t", t=STEPS), samp(cy[:, s, :])[:, :, 0:STEPS],
                          ACT.Silu).then_inc(conv_done, 1)
                    else:
                        act.wait_ge(in_evac, 10 * g + b + 1)
                        A(zs[:, b - 6, :], zs[:, b - 6, :], ACT.Silu).then_inc(z_done, 1)
                if g == 0:
                    act.wait_ge(dt_v, 1)
                    step(A(dv[2], dv[1], ACT.Abs))
                    A(dts[:, 1:2], dts[:, 1:2], ACT.Exp)
                    A(dv[3], dv[2], ACT.Exp, scale=-1.0).then_inc(dt_a, 1)
                    act.wait_ge(dt_v, 2)
                    A(dv[5], dv[4], ACT.Ln).then_inc(dt_a, 1)
                    act.wait_ge(acs_ready, 1)
                    A(toend[:], toend[:], ACT.Exp)
                    A(eacs[:], acs[:], ACT.Exp)
                    A(dec[:, 0:STREAMS, :], bank[5][:, 0:STREAMS * HEADS].rearrange("p (s h) -> p s h", h=HEADS), ACT.Exp)
                    A(dec[:, STREAMS, :], bank[6][:, 128:160], ACT.Exp).then_inc(da_ready, 1)
                for t in range(TT):
                    q = 3 * g + t
                    act.wait_ge(mn_ready, q + 1)
                    A(seg[:, q % 2, :], seg[:, q % 2, :], ACT.Exp).then_inc(e_ready, 1)
                for i in range(4):
                    act.wait_ge(y_ready, 4 * g + i + 1)
                    A(yh[:, i, :], zs[:, i, :], ACT.Copy, scale=ang[:, 4 * g + i:4 * g + i + 1]).then_inc(yh_ready, 1)
                for b in range(4):
                    hi_split(group0(g) + 10 + b + 3)
            act.wait_ge(yms, 1)
            A(std[:, :], bank[7][:, 0:TOK], ACT.Sqrt, bias=EPS, scale=1.0 / D_INNER).then_inc(ystd, 1)
            for k in range(KD):
                x_hi(2, k)
            norm_std(2)
            gate_up(1)
            down(1, 3)
            ple_act(0, 3)

            act.wait_ge(blk, CRED + PG + KD)
            for k in range(KD):
                act.wait_ge(h_new, 32 + k + 1)
                A(kxh[:, k, :], h[:, k, :], ACT.Copy, scale=gains[:, NORMS, k:k + 1]).then_inc(kxh_ready, 1)
            for k in range(KD):
                x_hi(4, k)
            norm_std(4)
            for b in range(3):
                hi_split(KV + b + 3)
            for t in range(TT):
                act.wait_ge(kvr_ready, t + 1)
                A(sq5[:, 0, 0:256], kvr[:, t, 0:256], ACT.Square, accum_out=rsc[:, t, 0:1])
                step(A(sq5[:, 0, 256:288], kvr[:, t, 256:288], ACT.Square, accum_out=rsc[:, t, 1:2]))
                A(rsc[:, t, 2:3], rsc[:, t, 0:1], ACT.Sqrt, bias=EPS, scale=1.0 / KV_LORA)
                A(rsc[:, t, 3:4], rsc[:, t, 1:2], ACT.Sqrt, bias=EPS, scale=1.0 / ROPE).then_inc(kvs, 1)
            act.wait_ge(cT_ps, 1)
            for k in range(2):
                A(cT[:, k, :], bank[5 + k][:, 0:TOK], ACT.Copy)
            A(krT[0:QD, :], bank[4][0:QD, 0:TOK], ACT.Copy).then_inc(cT_ready, 1)
            gate_up(2)
            down(2, 5)

            norm_std(5)
            for b in range(4):
                hi_split(DQ + b + 3)
            for t in range(TT):
                act.wait_ge(cq_ready, t + 1)
                step(A(sq5[:, 0, :], cqr[:, t, :], ACT.Square, accum_out=rsc[:, t, 0:1]))
                A(rsc[:, t, 2:3], rsc[:, t, 0:1], ACT.Sqrt, bias=EPS, scale=1.0 / Q_LORA).then_inc(cqs, 1)
            act.wait_ge(cqT_ps, 1)
            for k in range(4):
                A(xh[:, k, :], bank[4 + k][:, 0:TOK], ACT.Copy).then_inc(cqh, 1)

            def q_square(e):
                cg, t = divmod(e, TT)
                act.wait_ge(blk, CRED + QB + 2 * cg + 2)
                if e >= 2:
                    act.wait_ge(qs2, e - 1)
                A(sq5[:, e % 2, 0:384], bank[3 * (cg % 2) + t][:, 0:384], ACT.Square).then_inc(qs1, 1)

            def q_evac(e):
                cg, t = divmod(e, TT)
                act.wait_ge(qt_ps, e + 1)
                src = bank[6 + e % 2][0:QD, :].rearrange("p (h t) -> p h t", h=4)
                if t < 2:
                    A(Qp[0:QD, 4 * cg:4 * cg + 4, tiles(t)], src, ACT.Copy, scale=gq[0:QD, 2:3]).then_inc(qe, 1)
                else:
                    A(Qs[0:QD, :, 4 * cg:4 * cg + 4, :],
                      bank[6 + e % 2][0:QD, :].rearrange("p (h b q) -> p b h q", h=4, q=STEPS),
                      ACT.Copy, scale=gq[0:QD, 2:3]).then_inc(qe, 1)
            act.wait_ge(gq_ready, 1)
            for cg in range(4):
                for b in range(2):
                    hi_split(QB + 2 * cg + b + 3)
                for t in range(TT):
                    e = 3 * cg + t
                    if e == 0:
                        q_square(0)
                    if e + 1 < 12:
                        q_square(e + 1)
                    o = 24 * (e % 2)
                    act.wait_ge(qs2, e + 1)
                    A(sm[:, o + 8:o + 12], sm[:, o:o + 4], ACT.Sqrt, bias=EPS, scale=1.0 / NOPE)
                    A(sm[:, o + 12:o + 16], sm[:, o + 4:o + 8], ACT.Sqrt, bias=EPS, scale=1.0 / ROPE).then_inc(qs3, 1)
                    if e:
                        q_evac(e - 1)
            q_evac(11)

            def key_square(w):
                act.wait_ge(ex_ps, w + 1)
                act.wait_ge(qs2, 12)
                if w >= 2:
                    act.wait_ge(ks2, w - 1)
                A(sq5[:, w % 2, :], bank[w % 2][:, :], ACT.Square).then_inc(ks1, 1)

            def key_evac(w):
                t, g = divmod(w, 2)
                act.wait_ge(kt_ps, w + 1)
                for x in range(2):
                    last = A(Kp[0:QD, 8 * g + 4 * x:8 * g + 4 * x + 4, tiles(t)],
                             bank[2 + x][0:QD, :].rearrange("p (h t) -> p h t", h=4), ACT.Copy)
                last.then_inc(kt_ev, 1)

            key_square(0)
            for w in range(ITEMS):
                if w + 1 < ITEMS:
                    key_square(w + 1)
                o = 48 + 24 * (w % 2)
                act.wait_ge(ks2, w + 1)
                A(sm[:, o + 8:o + 16], sm[:, o:o + 8], ACT.Sqrt, bias=EPS, scale=1.0 / NOPE).then_inc(ks3, 1)
                if 1 <= w <= 4:
                    key_evac(w - 1)
            act.wait_ge(w_ld, 16 * 5)
            for k in range(2):
                A(wkh[:, k, :], wk[:, k, :], ACT.Copy).then_inc(wk_hi, 1)
            for v in range(4):
                act.wait_ge(vp_ps, v + 1)
                A(Vp[:, v // 2, 512 * (v % 2):512 * (v % 2) + 512], bank[4 + v][:, :], ACT.Copy).then_inc(vp_ev, 1)

            def past_split(b):
                act.wait_ge(c_ld[b % 2], 16 * (b // 2 + 1))
                A(cTh[:, b % 2], cTb[:, b % 2], ACT.Copy).then_inc(past_hi, 1)

            def past_square(w):
                act.wait_ge(past_ps, w + 1)
                if w < 2:
                    act.wait_ge(kt_ps, 4)
                else:
                    act.wait_ge(past_sum, w - 1)
                A(kn[:, w % 2, 0:512], bank[w % 2][:, :], ACT.Square).then_inc(past_sq, 1)

            def p_exp(x):
                s, o = x % 2, 48 + 8 * (x % 2)
                act.wait_ge(pa2, x + 1)
                A(Pb[:, s, 0:128], Pb[:, s, 0:128], ACT.Exp, bias=sm[:, o + 2:o + 3], scale=SCALE, accum_out=sm[:, o + 4:o + 5])
                A(Pb[:, s, 128:384], Pb[:, s, 128:384], ACT.Exp, bias=sm[:, o + 3:o + 4], scale=SCALE,
                  accum_out=sm[:, o + 5:o + 6]).then_inc(pa3, 1)

            past_split(0)
            past_split(1)
            p_exp(0)
            for x in range(MH):
                if x + 1 < MH:
                    p_exp(x + 1)
                past_square(4 * x)
                past_square(4 * x + 1)
                act.wait_ge(pt_ps, x + 1)
                A(PT[:, 0:384], bank[6][:, 0:384], ACT.Copy).then_inc(pt_ev, 1)
                past_square(4 * x + 2)
                past_square(4 * x + 3)
                if x % 2 and 2 <= x // 2 + 1 < STREAMS:
                    past_split(x // 2 + 1)
                if x % 2:
                    act.wait_ge(po_ps, x + 1)
                    A(xh[:, x // 2, 0:SEQ], bank[7 if x // 2 % 2 else 3][:, 0:SEQ], ACT.Copy).then_inc(oh_ready, 1)

            act.wait_ge(past_sum, 8 * STREAMS)
            A(ksq[:], ksq[:], ACT.Sqrt, bias=EPS, scale=1.0 / NOPE).then_inc(past_std, 1)
            for j in range(8):
                act.wait_ge(qc_ps, j + 1)
                for k in range(2):
                    ins = A(QC[:, k, :, 2 * j:2 * j + 2, :],
                            bank[j % 4][:, tiles(k, 2 * P)].rearrange("p (h b q) -> p b h q", h=2, b=STREAMS), ACT.Copy)
                ins.then_inc(qc_ev, 1)
            act.wait_ge(new_rt, 1)
            A(rbn[:, :, :], bank[4][:, 0:2 * P].rearrange("p (g t) -> p g t", g=2), ACT.Copy).then_inc(new_rk, 1)

            def s_rstd(u):
                act.wait_ge(rt_done, u + 1)
                if u >= 2:
                    act.wait_ge(sa1, u - 1)
                A(rk[:, u % 2, 0:512], bank[3][:, :], ACT.Copy).then_inc(rk_ready, 1)

            def s_exp(u):
                b = u // 2
                act.wait_ge(sa2, u + 1)
                s, o = u % 2, 64 + 8 * (u % 2)
                A(Pb[:, s, 0:PAST], Pb[:, s, 0:PAST], ACT.Exp, bias=sm[:, o + 2:o + 3], scale=SCALE, accum_out=sm[:, o + 4:o + 5])
                new = Pb[:, s, PAST + 16 * b:PAST + 16 * b + 16]
                A(new, new, ACT.Exp, bias=sm[:, o + 2:o + 3], scale=SCALE, accum_out=sm[:, o + 5:o + 6]).then_inc(sa3, 1)

            s_rstd(0)
            s_exp(0)
            for u in range(UNITS):
                act.wait_ge(pt_ps, MH + u + 1)
                A(PT[:, 0:512], bank[6][:, :], ACT.Copy)
                A(PT[:, 512:640], bank[0][:, 0:P], ACT.Copy).then_inc(pt_ev, 1)
                if u + 1 < UNITS:
                    s_rstd(u + 1)
                    s_exp(u + 1)
            for x in range(MH // 2):
                act.wait_ge(os_ps, x + 1)
                A(xh[:, x, SEQ:TOK], bank[x % 2][:, 0:P], ACT.Copy).then_inc(oh_ready, 1)
            for b in range(8):
                hi_split(WO + b + 3)
            act.wait_ge(blk, CRED + WO + 8)
            for k in range(KD):
                x_hi(6, k)
            norm_std(6)
            gate_up(3)
            down(3, 7)
            ple_act(1, 7)

        @block.vector
        def _(dve):
            V = nc.vector
            c = [0]

            def step(ins):
                c[0] += 1
                ins.then_inc(dve_chain, 1)
                dve.wait_ge(dve_chain, c[0])

            def lo_split(n, i=0):
                if n >= NBLK:
                    return
                r, w = n % SLOTS, WIDTH[n]
                dve.wait_ge(hi_ready, i * SLOTS + (n + 1))
                V.tensor_tensor(wlo[:, r, 0:w], raw[:, r, 0:w], whi[:, r, 0:w].bitcast(F32),
                                ALU.subtract).then_inc(lo_ready, 1)

            def norm_rstd(m):
                dve.wait_ge(std_ready, m + 1)
                V.reciprocal(rstd[:, m % 2, :], std[:, :]).then_inc(rstd_ready, 1)
                dve.wait_ge(rstd_ready, m + 1)

            def x_lo(m, k):
                dve.wait_ge(xh_ready, 8 * m + k + 1)
                V.scalar_tensor_tensor(out=xl[:, k, :], in0=h[:, k, :], scalar=gains[:, m, k:k + 1],
                                       in1=xh[:, k, :].bitcast(F32), op0=ALU.mult, op1=ALU.subtract).then_inc(xl_ready, 1)

            def gate_up(u, m):
                base, r = BASE[f"gu{u}"], rstd[:, m % 2, :]

                def pair(i, n0):
                    for j in range(2):
                        n, fs = base + n0 + 2 * j, KF * u + n0 // 2 + j
                        dve.wait_ge(blk, i * SLOTS + (CRED + n + 2))
                        V.tensor_tensor(tg[:, j, :], bank[2 * j][:, 0:TOK], r, ALU.mult)
                        V.tensor_tensor(tu[:, j, :], bank[2 * j + 1][:, 0:TOK], r, ALU.mult).then_inc(gu_evac, 1)
                        lo_split(n + 3, i)
                        dve.wait_ge(sg_ready, i * 2 + (fs + 1))
                        V.tensor_tensor(tu[:, j, :], tg[:, j, :], tu[:, j, :], ALU.mult).then_inc(a_ready, 1)
                        lo_split(n + 4, i)
                        dve.wait_ge(ah_ready, i * 2 + (fs + 1))
                        f = i * 2 + (n0 // 2 + j)
                        V.tensor_tensor(al[:, f, :], tu[:, j, :], ah[:, f, :].bitcast(F32), ALU.subtract).then_inc(al_ready, 1)
                with dve.Fori(0, KF // 2 - 1) as i:
                    pair(i, 0)
                pair(0, 2 * KF - 4)

            def down(u, m):
                for j in range(KD):
                    n = BASE[f"dn{u}"] + 3 * j
                    for b in range(3):
                        lo_split(n + b + 3)
                    dve.wait_ge(blk, CRED + n + 3)
                    V.scalar_tensor_tensor(out=h[:, j, :], in0=bank[j % 4][:, 0:TOK], scalar=0.5, in1=h[:, j, :],
                                           op0=ALU.mult, op1=ALU.add).then_inc(h_new, 1)
                    x_lo(m, j)

            def ple_dve(l, m):
                dve.wait_ge(ph_ready, l + 1)
                V.tensor_tensor(plo[:, :, :], praw, phi[:, :, :].bitcast(F32), ALU.subtract).then_inc(pl_ready, 1)
                norm_rstd(m)
                for i in range(2):
                    lo_split(BASE[f"pi{l}"] + i + 3)
                for j in range(KD):
                    n = BASE[f"pg{l}"] + j
                    lo_split(n + 3)
                    dve.wait_ge(blk, CRED + n + 1)
                    V.tensor_tensor(tp[:, j % 2, :], bank[j % 4][:, 0:TOK], rstd[:, m % 2, :], ALU.mult).then_inc(pg_evac, 1)
                    dve.wait_ge(sgm_ready, 8 * l + j + 1)
                    dve.wait_ge(pin_ready, 8 * l + 8)
                    step(V.tensor_tensor(tp[:, j % 2, :], tp[:, j % 2, :], pin[:, j, :], ALU.mult))
                    V.tensor_tensor(h[:, j, :], h[:, j, :], tp[:, j % 2, :], ALU.add).then_inc(h_new, 1)

            dve.sem_inc(gu_evac, 2)
            dve.sem_inc(blk, CRED)
            for r in range(AHEAD):
                lo_split(r)
            dve.wait_ge(x_ld, 16)
            dve.sem_inc(h_new, KD)
            dve.wait_ge(const_ld, 160)
            for k in range(KD):
                x_lo(0, k)
            norm_rstd(0)
            gate_up(0, 0)
            down(0, 1)

            norm_rstd(1)
            r = rstd[:, 1, :]
            lo_split(MIX + 3)
            dve.wait_ge(ones_ready, 2)
            for g in range(GROUPS):
                hs = slice(HPG * g, HPG * g + HPG)
                for b in range(10):
                    n, s, e = group0(g) + b, b % 2, 6 * g + b
                    lo_split(n + 3)
                    dve.wait_ge(blk, CRED + n + 1)
                    src = bank[b % 4]
                    if b < 6:
                        ch = 4 * g + b if b < 4 else 16 + 4 * (b - 4) + g
                        V.tensor_tensor(xp[:, s, 3:3 + SEQ], src[:, 0:SEQ], r[:, 0:SEQ], ALU.mult)
                        V.tensor_tensor(samp(xp[:, s, :])[:, :, 3:3 + STEPS],
                                        src[:, SEQ:TOK].rearrange("p (s t) -> p s t", t=STEPS),
                                        r[:, SEQ:TOK].rearrange("p (s t) -> p s t", t=STEPS), ALU.mult).then_inc(in_evac, 1)
                        dve.wait_ge(c0_ready, e + 1)
                        for k in range(1, CONV_W):
                            ins = V.scalar_tensor_tensor(out=cy[:, s, 0:CW], in0=xp[:, s, k:k + CW], scalar=cw[:, ch, k:k + 1],
                                                         in1=cy[:, s, 0:CW], op0=ALU.mult, op1=ALU.add)
                            if k < CONV_W - 1:
                                step(ins)
                            else:
                                ins.then_inc(conv_ready, 1)
                    else:
                        if g:
                            dve.wait_ge(sqy, 4 * g)
                        V.tensor_tensor(zs[:, b - 6, :], src[:, 0:TOK], r, ALU.mult).then_inc(in_evac, 1)
                if g == 0:
                    step(V.tensor_tensor(dv[0], bank[4][0:HEADS, 0:TOK], r[0:HEADS, :], ALU.mult))
                    V.tensor_scalar(dv[1], dv[0], dts[:, 0:1], None, ALU.add).then_inc(dt_v, 1)
                    dve.wait_ge(dt_a, 1)
                    V.tensor_scalar(dv[4], dv[3], 1.0, None, ALU.add).then_inc(dt_v, 1)
                    dve.wait_ge(dt_v, 2)
                    V.reciprocal(dv[6], dv[4])
                    step(V.tensor_scalar(dv[0], dv[4], -1.0, None, ALU.add))
                    step(V.tensor_tensor(dv[0], dv[3], dv[0], ALU.subtract))
                    step(V.tensor_tensor(dv[0], dv[0], dv[6], ALU.mult))
                    dve.wait_ge(dt_a, 2)
                    step(V.tensor_scalar(dv[2], dv[1], 0.0, None, ALU.max))
                    step(V.tensor_tensor(dv[2], dv[2], dv[5], ALU.add))
                    step(V.tensor_tensor(dv[2], dv[2], dv[0], ALU.add))
                    V.tensor_scalar(dv[1], dv[2], dts[:, 1:2], -1.0, ALU.mult, ALU.mult).then_inc(dt_ready, 1)
                    dve.wait_ge(dtT_ps, 1)
                    V.tensor_copy(dtR[:, :, :], bank[5][:, 0:96].rearrange("p (t h) -> p t h", t=TT))
                    step(V.tensor_copy(aR[:, :, :], bank[5][:, 96:192].rearrange("p (t h) -> p t h", t=TT)))
                    V.tensor_tensor(am, bc(aR[:, 2, :], (P, STREAMS, HEADS), 1), bc(ind[:, :], (P, STREAMS, HEADS), 2),
                                    ALU.mult).then_inc(dtR_ready, 1)
                    dve.wait_ge(ac_ps, 1)
                    step(V.tensor_copy(acs[:, :, :], bank[6][:, 0:96].rearrange("p (t h) -> p t h", t=TT)))
                    V.tensor_tensor(toend[:, :, :], bank[6][:, 96:192].rearrange("p (t h) -> p t h", t=TT), acs[:, :, :],
                                    ALU.subtract).then_inc(acs_ready, 1)
                    dve.wait_ge(da_ready, 1)
                hd = (P, HPG, HD)
                for t in range(TT):
                    dve.wait_ge(xt_ps, 3 * g + t + 1)
                    v3 = xdt[:, t, :].rearrange("p (h d) -> p h d", h=HPG)
                    V.tensor_tensor(v3, bank[4 + t][:, :].rearrange("p (h d) -> p h d", h=HPG), bc(dtR[:, t, hs], hd, 2),
                                    ALU.mult).then_inc(xdt_ready, 1)
                    dve.wait_ge(xdt_ready, 3 * g + t + 1)
                    V.tensor_tensor(xw[:, t, :].rearrange("p (h d) -> p h d", h=HPG), v3, bc(toend[:, t, hs], hd, 2),
                                    ALU.mult).then_inc(xw_ready, 1)
                dve.wait_ge(bt_ps, g + 1)
                V.tensor_copy(Brow[:, :, :], bank[7][:, 0:TOK].rearrange("p (t n) -> p t n", t=TT)).then_inc(brow_ready, 1)
                dve.wait_ge(brow_ready, g + 1)
                V.tensor_tensor(Bm[:, :, :], bc(Brow[:, 2, :], (P, STREAMS, P), 1), bc(ind[:, :], (P, STREAMS, P), 2), ALU.mult)
                dve.wait_ge(cm_zero, 1)
                V.tensor_copy(bass.AP(Cm, 0, [[STREAMS * P, P], [P + STEPS, STREAMS], [1, STEPS]]),
                              BC[:, 1, SEQ:TOK].rearrange("p (s t) -> p s t", t=STEPS)).then_inc(bm_ready, 1)
                dve.wait_ge(g_ps, g + 1)
                V.tensor_tensor(Gm[:, :], bank[7][:, 0:TOK], mask[:, :, :].rearrange("p t l -> p (t l)"),
                                ALU.mult).then_inc(gm_ready, 1)

                def decay(t):
                    q, s = 3 * g + t, (3 * g + t) % 2
                    dve.wait_ge(ab_ps, q + 1)
                    if q >= 2:
                        dve.wait_ge(ym_done, q - 1)
                    for x in range(2):
                        ins = V.tensor_tensor(seg[:, s, 512 * x:512 * x + 512].rearrange("p (h l) -> p h l", h=4),
                                              bank[4 + x][:, :].rearrange("p (h l) -> p h l", h=4),
                                              bc(acs[:, t, HPG * g + 4 * x:HPG * g + 4 * x + 4], (P, 4, P), 2), ALU.subtract)
                    ins.then_inc(d_ready, 1)
                    dve.wait_ge(d_ready, q + 1)
                    V.tensor_scalar(seg[:, s, :], seg[:, s, :], 0.0, None, ALU.min).then_inc(mn_ready, 1)

                def decay_cb(t):
                    q, s = 3 * g + t, (3 * g + t) % 2
                    dve.wait_ge(e_ready, q + 1)
                    dve.wait_ge(gm_ready, g + 1)
                    v = seg[:, s, :].rearrange("p (h l) -> p h l", h=HPG)
                    V.tensor_tensor(v, v, bc(Gm[:, tiles(t)], (P, HPG, P), 1), ALU.mult).then_inc(m_ready, 1)

                def y_old(k):
                    dve.wait_ge(yo_ps, 2 * g + k + 1)
                    V.tensor_tensor(yoff[:, k, :].rearrange("p (h d) -> p h d", h=HPG),
                                    bank[7][:, :].rearrange("p (h d) -> p h d", h=HPG), bc(eacs[:, k + 1, hs], hd, 2),
                                    ALU.mult).then_inc(yo_ready, 1)

                decay(0)
                dve.wait_ge(u_ps, 10 * g + 1)
                if g:
                    dve.wait_ge(s1_store, 16 * g)
                V.tensor_copy(S1[:, :], bank[6][:, :]).then_inc(s1_ready, 1)
                decay_cb(0)
                y_old(0)
                s1v = S1[:, :].rearrange("p (h d) -> p h d", h=HPG)
                step(V.tensor_tensor(s1v, s1v, bc(dec[:, STREAMS, hs], hd, 2), ALU.mult))
                dve.wait_ge(u_ps, 10 * g + 2)
                V.tensor_tensor(S1[:, :], S1[:, :], bank[6][:, :], ALU.add).then_inc(s1_ready, 1)
                decay(1)
                decay_cb(1)
                y_old(1)
                decay(2)
                for b in range(STREAMS):
                    sv = S[:, b, :].rearrange("p (h d) -> p h d", h=HPG)
                    step(V.tensor_tensor(sv, sv, bc(dec[:, b, hs], hd, 2), ALU.mult))
                    if b == 0:
                        decay_cb(2)
                    dve.wait_ge(u_ps, 10 * g + 3 + b)
                    V.tensor_tensor(S[:, b, :], S[:, b, :], bank[6 + b % 2][:, :], ALU.add).then_inc(su_done, 1)
                dve.wait_ge(ym_done, 3 * g + 3)
                for i in range(4):
                    dve.wait_ge(z_done, 4 * g + i + 1)
                    V.scalar_tensor_tensor(out=xsT[:, i, :], in0=xsT[:, i, :], scalar=dcol[:, 4 * g + i:4 * g + i + 1],
                                           in1=bank[i][:, 0:TOK], op0=ALU.mult, op1=ALU.add).then_inc(y_evac, 1)
                    dve.wait_ge(y_evac, 4 * g + i + 1)
                    V.tensor_tensor(zs[:, i, :], zs[:, i, :], xsT[:, i, :], ALU.mult).then_inc(y_ready, 1)
                for i in range(4):
                    dve.wait_ge(yh_ready, 4 * g + i + 1)
                    V.scalar_tensor_tensor(out=yl[:, i, :], in0=zs[:, i, :], scalar=ang[:, 4 * g + i:4 * g + i + 1],
                                           in1=yh[:, i, :].bitcast(F32), op0=ALU.mult, op1=ALU.subtract).then_inc(yl_ready, 1)
                for b in range(4):
                    n = group0(g) + 10 + b
                    lo_split(n + 3)
                    dve.wait_ge(blk, CRED + n + 1)
                    for j in (2 * b, 2 * b + 1):
                        src = bank[4 + j % 4][:, 0:TOK]
                        if g == 0:
                            V.tensor_copy(facc[:, j, :], src).then_inc(f_evac, 1)
                        else:
                            V.tensor_tensor(facc[:, j, :], facc[:, j, :], src, ALU.add).then_inc(f_evac, 1)
            dve.wait_ge(ystd, 1)
            step(V.reciprocal(rstd[:, 0, :], std[:, :]))
            for j in range(KD):
                step(V.tensor_tensor(facc[:, j, :], facc[:, j, :], rstd[:, 0, :], ALU.mult))
                V.tensor_tensor(h[:, j, :], h[:, j, :], facc[:, j, :], ALU.add).then_inc(h_new, 1)
            for j in range(KD):
                x_lo(2, j)
            norm_rstd(2)
            gate_up(1, 2)
            down(1, 3)
            ple_dve(0, 3)

            for k in range(KD):
                dve.wait_ge(kxh_ready, k + 1)
                V.scalar_tensor_tensor(out=kxl[:, k, :], in0=h[:, k, :], scalar=gains[:, NORMS, k:k + 1],
                                       in1=kxh[:, k, :].bitcast(F32), op0=ALU.mult, op1=ALU.subtract).then_inc(kxl_ready, 1)
            for k in range(KD):
                x_lo(4, k)
            norm_rstd(4)
            for b in range(3):
                lo_split(KV + b + 3)

            def token_rows(x):
                dve.wait_ge(rt_ps, x + 1)
                V.tensor_copy(rows[:, x, :], bank[4][:, 0:TOK].rearrange("p (t c) -> p t c", t=TT)[:, :, 0]).then_inc(rows_ready, 1)
                dve.wait_ge(rows_ready, x + 1)

            token_rows(0)
            dve.wait_ge(blk, CRED + KV + 3)
            for t in range(TT):
                V.tensor_scalar(kvr[:, t, :], bank[t][:, 0:KV_LORA + ROPE], rows[:, 0, t:t + 1], None,
                                ALU.mult).then_inc(kvr_ready, 1)
            H2 = ROPE // 2
            dve.wait_ge(kr_zero, 1)
            for t in range(TT):
                dve.wait_ge(kvs, t + 1)
                step(V.reciprocal(rsc[:, t, 4:6], rsc[:, t, 2:4]))
                V.scalar_tensor_tensor(out=ckv[:, t, :], in0=kvr[:, t, 0:256], scalar=rsc[:, t, 4:5], in1=kvg[:, 0:256],
                                       op0=ALU.mult, op1=ALU.mult)
                x = krot[:, t, 0, :]
                step(V.scalar_tensor_tensor(out=x, in0=kvr[:, t, 256:288], scalar=rsc[:, t, 5:6], in1=kvg[:, 256:288],
                                            op0=ALU.mult, op1=ALU.mult))
                kr = krow[:, t, NOPE:QD]
                V.tensor_tensor(krot[:, t, 1, :], x, sinr[:, t, :], ALU.mult)
                step(V.tensor_tensor(kr, x, cosr[:, t, :], ALU.mult))
                V.tensor_tensor(kr[:, 0:H2], kr[:, 0:H2], krot[:, t, 1, H2:ROPE], ALU.subtract)
                V.tensor_tensor(kr[:, H2:ROPE], kr[:, H2:ROPE], krot[:, t, 1, 0:H2], ALU.add).then_inc(kv_done, 1)
            gate_up(2, 4)
            down(2, 5)

            norm_rstd(5)
            for b in range(4):
                lo_split(DQ + b + 3)
            token_rows(1)
            dve.wait_ge(blk, CRED + DQ + 4)
            for t in range(TT):
                V.tensor_scalar(cqr[:, t, :], bank[t][:, :], rows[:, 1, t:t + 1], None, ALU.mult).then_inc(cq_ready, 1)
            dve.wait_ge(w_ld, 16 * 5)
            for t in range(TT):
                dve.wait_ge(cqs, t + 1)
                step(V.reciprocal(rsc[:, t, 4:5], rsc[:, t, 2:3]))
                V.scalar_tensor_tensor(out=cqr[:, t, :], in0=cqr[:, t, :], scalar=rsc[:, t, 4:5], in1=qgr,
                                       op0=ALU.mult, op1=ALU.mult).then_inc(cqn_ready, 1)
            V.tensor_tensor(gq[:, 2:3], gq[:, 0:1], gq[:, 1:2], ALU.mult).then_inc(gq_ready, 1)
            V.tensor_tensor(cosr[:], cosr[:], bc(gr[:], (P, TT, ROPE), 1), ALU.mult)
            V.tensor_tensor(sinr[:], sinr[:], bc(gr[:], (P, TT, ROPE), 1), ALU.mult).then_inc(gq_ready, 1)
            dve.wait_ge(gq_ready, 2)
            for k in range(4):
                dve.wait_ge(cqh, k + 1)
                V.tensor_tensor(xl[:, k, :], bank[4 + k][:, 0:TOK], xh[:, k, :].bitcast(F32), ALU.subtract).then_inc(cql, 1)
            def q_sums(e):
                o = 24 * (e % 2)
                dve.wait_ge(qs1, e + 1)
                v = sq5[:, e % 2, 0:384].rearrange("p (h d) -> p h d", h=4)
                V.reduce_sum(sm[:, o:o + 4], v[:, :, 0:NOPE], axis=AX.X)
                V.reduce_sum(sm[:, o + 4:o + 8], v[:, :, NOPE:QD], axis=AX.X).then_inc(qs2, 1)

            for cg in range(4):
                for b in range(2):
                    lo_split(QB + 2 * cg + b + 3)
                for t in range(TT):
                    e, s = 3 * cg + t, (3 * cg + t) % 2
                    o = 24 * s
                    if e == 0:
                        q_sums(0)
                    if e + 1 < 12:
                        q_sums(e + 1)
                    dve.wait_ge(qs3, e + 1)
                    step(V.reciprocal(sm[:, o + 16:o + 24], sm[:, o + 8:o + 16]))
                    if e >= 2:
                        dve.wait_ge(qt_ps, e - 1)
                    src = bank[3 * (cg % 2) + t][:, 0:384].rearrange("p (h d) -> p h d", h=4)
                    q = kn[:, s, 0:384].rearrange("p (h d) -> p h d", h=4)
                    x = kn[:, s, 384:512].rearrange("p (h d) -> p h d", h=4)
                    xs_ = kn[:, s, 512:640].rearrange("p (h d) -> p h d", h=4)
                    qr = q[:, :, NOPE:QD]
                    V.tensor_tensor(x, src[:, :, NOPE:QD], bc(sm[:, o + 20:o + 24], (P, 4, ROPE), 2), ALU.mult)
                    V.tensor_tensor(q[:, :, 0:NOPE], src[:, :, 0:NOPE], bc(sm[:, o + 16:o + 20], (P, 4, NOPE), 2),
                                    ALU.mult).then_inc(qb_evac, 1)
                    dve.wait_ge(qb_evac, e + 1)
                    V.tensor_tensor(xs_, x, bc(sinr[:, t, :], (P, 4, ROPE), 1), ALU.mult)
                    step(V.tensor_tensor(qr, x, bc(cosr[:, t, :], (P, 4, ROPE), 1), ALU.mult))
                    V.tensor_tensor(qr[:, :, 0:H2], qr[:, :, 0:H2], xs_[:, :, H2:ROPE], ALU.subtract)
                    V.tensor_tensor(qr[:, :, H2:ROPE], qr[:, :, H2:ROPE], xs_[:, :, 0:H2], ALU.add).then_inc(qr_ready, 1)

            def key_sums(w):
                o = 48 + 24 * (w % 2)
                dve.wait_ge(ks1, w + 1)
                V.reduce_sum(sm[:, o:o + 8], sq5[:, w % 2, :].rearrange("p (h d) -> p h d", h=8), axis=AX.X).then_inc(ks2, 1)

            key_sums(0)
            for w in range(ITEMS):
                if w + 1 < ITEMS:
                    key_sums(w + 1)
                o = 48 + 24 * (w % 2)
                dve.wait_ge(ks3, w + 1)
                if w >= 4:
                    V.reciprocal(rsn[:, 8 * (w - 4):8 * (w - 4) + 8], sm[:, o + 8:o + 16]).then_inc(ks4, 1)
                    continue
                step(V.reciprocal(sm[:, o + 16:o + 24], sm[:, o + 8:o + 16]))
                if w >= 2:
                    dve.wait_ge(kt_ps, w - 1)
                else:
                    dve.wait_ge(qt_ps, 12)
                src = bank[w % 2][:, :].rearrange("p (h d) -> p h d", h=8)
                kv_ = kn[:, w % 2, :].rearrange("p (h d) -> p h d", h=8)
                V.tensor_copy(kv_[:, :, NOPE:QD], bc(krow[:, w // 2, NOPE:QD], (P, 8, ROPE), 1))
                V.tensor_tensor(kv_[:, :, 0:NOPE], src, bc(sm[:, o + 16:o + 24], (P, 8, NOPE), 2), ALU.mult).then_inc(ks4, 1)
            dve.wait_ge(ex_ps, ITEMS)
            for k in range(2):
                dve.wait_ge(wk_hi, k + 1)
                V.tensor_tensor(wkl[:, k, :], wk[:, k, :], wkh[:, k, :].bitcast(F32), ALU.subtract).then_inc(wk_lo, 1)

            def past_split(b):
                dve.wait_ge(past_hi, b + 1)
                V.tensor_tensor(cTl[:, b % 2], cTb[:, b % 2], cTh[:, b % 2].bitcast(F32), ALU.subtract).then_inc(past_lo, 1)

            def past_sums(w):
                b, st, g = w // 8, w // 2 % 4, w % 2
                dve.wait_ge(past_sq, w + 1)
                V.reduce_sum(ksq[:, b, st, 8 * g:8 * g + 8], kn[:, w % 2, 0:512].rearrange("p (h d) -> p h d", h=8),
                             axis=AX.X).then_inc(past_sum, 1)

            def p_max(x):
                s, o = x % 2, 48 + 8 * (x % 2)
                dve.wait_ge(qk_ps, x + 1)
                if x >= 2:
                    dve.wait_ge(pt_ps, x - 1)
                V.tensor_tensor(Pb[:, s, 0:384], bank[4 + s][:, 0:384], mk, ALU.add).then_inc(pa1, 1)
                dve.wait_ge(pa1, x + 1)
                V.reduce_max(sm[:, o:o + 1], Pb[:, s, 0:128], axis=AX.X)
                step(V.reduce_max(sm[:, o + 1:o + 2], Pb[:, s, 128:384], axis=AX.X))
                V.tensor_scalar(sm[:, o + 2:o + 4], sm[:, o:o + 2], -SCALE, None, ALU.mult).then_inc(pa2, 1)

            past_split(0)
            past_split(1)
            dve.wait_ge(mk_ld, 16)
            p_max(0)
            for x in range(MH):
                s, o = x % 2, 48 + 8 * (x % 2)
                if x + 1 < MH:
                    p_max(x + 1)
                dve.wait_ge(pa3, x + 1)
                step(V.reciprocal(sm[:, o + 6:o + 8], sm[:, o + 4:o + 6]))
                V.tensor_scalar(Pb[:, s, 0:128], Pb[:, s, 0:128], sm[:, o + 6:o + 7], None, ALU.mult)
                V.tensor_scalar(Pb[:, s, 128:384], Pb[:, s, 128:384], sm[:, o + 7:o + 8], None, ALU.mult).then_inc(pa4, 1)
                for i in range(4):
                    past_sums(4 * x + i)
                if x % 2 and 2 <= x // 2 + 1 < STREAMS:
                    past_split(x // 2 + 1)
                if x % 2:
                    dve.wait_ge(oh_ready, x // 2 + 1)
                    V.tensor_tensor(xl[:, x // 2, 0:SEQ], bank[7 if x // 2 % 2 else 3][:, 0:SEQ],
                                    xh[:, x // 2, 0:SEQ].bitcast(F32), ALU.subtract).then_inc(ol_ready, 1)

            dve.wait_ge(past_std, 1)
            V.reciprocal(ksq[:], ksq[:]).then_inc(past_rstd, 1)

            def s_max(u):
                b, g = divmod(u, 2)
                s, o = u % 2, 64 + 8 * (u % 2)
                dve.wait_ge(pt_ps, MH + max(u - 1, 0))
                step(V.memset(Pb[:, s, PAST:640], 0.0))
                new = slice(PAST + 16 * b, PAST + 16 * b + 16)
                nk = slice(16 * b, 16 * b + 16)
                if u == 0:
                    dve.wait_ge(new_rk, 1)
                dve.wait_ge(rk_ready, u + 1)
                dve.wait_ge(sc_ps, u + 1)
                V.tensor_tensor(Pb[:, s, 0:PAST], bank[2][:, :], rk[:, s, 0:512], ALU.mult)
                step(V.tensor_tensor(Pb[:, s, new], bank[5][:, nk], rbn[:, g, nk], ALU.mult))
                V.tensor_tensor(Pb[:, s, 0:PAST], Pb[:, s, 0:PAST], bank[4][:, :], ALU.add)
                V.tensor_tensor(Pb[:, s, new], Pb[:, s, new], bank[5][:, P + 16 * b:P + 16 * b + 16], ALU.add).then_inc(sa1, 1)
                dve.wait_ge(sa1, u + 1)
                V.reduce_max(sm[:, o:o + 1], Pb[:, s, 0:PAST], axis=AX.X)
                step(V.reduce_max(sm[:, o + 1:o + 2], Pb[:, s, new], axis=AX.X))
                step(V.tensor_tensor(sm[:, o + 3:o + 4], sm[:, o:o + 1], sm[:, o + 1:o + 2], ALU.max))
                V.tensor_scalar(sm[:, o + 2:o + 3], sm[:, o + 3:o + 4], -SCALE, None, ALU.mult).then_inc(sa2, 1)

            def s_latent(u):
                b, g = divmod(u, 2)
                dve.wait_ge(ot_ps, u + 1)
                V.tensor_copy(QC[:, :, b, 8 * g:8 * g + 8, :],
                              bank[1][:, 0:256].rearrange("p (k h q) -> p k h q", k=2, h=8)).then_inc(olt, 1)

            s_max(0)
            for u in range(UNITS):
                o = 64 + 8 * (u % 2)
                dve.wait_ge(sa3, u + 1)
                step(V.tensor_tensor(sm[:, o + 6:o + 7], sm[:, o + 4:o + 5], sm[:, o + 5:o + 6], ALU.add))
                step(V.reciprocal(sm[:, o + 7:o + 8], sm[:, o + 6:o + 7]))
                if u:
                    s_latent(u - 1)
                if u + 1 < UNITS:
                    s_max(u + 1)
                dve.wait_ge(po_ps, MH + u + 1)
                V.tensor_scalar(ol[:, :], bank[7][:, 256:512], sm[:, o + 7:o + 8], None, ALU.mult).then_inc(olr, 1)
            s_latent(UNITS - 1)
            for x in range(MH // 2):
                dve.wait_ge(oh_ready, MH // 2 + x + 1)
                V.tensor_tensor(xl[:, x, SEQ:TOK], bank[x % 2][:, 0:P], xh[:, x, SEQ:TOK].bitcast(F32),
                                ALU.subtract).then_inc(ol_ready, 1)
            for b in range(8):
                lo_split(WO + b + 3)
                dve.wait_ge(blk, CRED + WO + b + 1)
                V.tensor_tensor(h[:, b, :], h[:, b, :], bank[2 + b % 4][:, 0:TOK], ALU.add).then_inc(h_new, 1)
            for k in range(KD):
                x_lo(6, k)
            norm_rstd(6)
            gate_up(3, 6)
            down(3, 7)
            ple_dve(1, 7)

        @block.tensor
        def _(pe):
            M = nc.tensor.matmul

            def product(out, r, k0, k1, mh_, ml_, first, last):
                for k in range(k0, k1):
                    ws = slice(k * P, (k + 1) * P)
                    M(out, whi[:, r, ws], mh_(k), start=first and k == k0, stop=False)
                    M(out, whi[:, r, ws], ml_(k), start=False, stop=False)
                    ins = M(out, wlo[:, r, ws], mh_(k), start=False, stop=last and k == k1 - 1)
                return ins

            def row_product(out, r, w0, w, xh_, xl_, first, last):
                M(out, xh_, whi[:, r, w0:w0 + w], start=first, stop=False)
                M(out, xh_, wlo[:, r, w0:w0 + w], start=False, stop=False)
                return M(out, xl_, whi[:, r, w0:w0 + w], start=False, stop=last)

            def weights(n, i=0):
                pe.wait_ge(lo_ready, i * SLOTS + (n + 1))

            def norm_sum(m):
                pe.wait_ge(sq_done, m + 1)
                M(bank[7][:, 0:TOK], ones[:, :], sqacc[:, m % 2, :], start=True, stop=True).then_inc(ms_ready, 1)

            X = (lambda k: xh[:, k, :], lambda k: xl[:, k, :])

            def gate_up(u, m):
                base = BASE[f"gu{u}"]
                pe.wait_ge(xl_ready, 8 * (m + 1))

                def pair(i, first):
                    for j in range(2):
                        pe.wait_ge(gu_evac, i * 2 + (KF * u + j + 1))
                        for half in range(2):
                            n = base + 2 * j + half
                            weights(n, i)
                            product(bank[2 * j + half][:, 0:TOK], n % SLOTS, 0, KD, *X, True, True).then_inc(blk, 1)
                            if first and j == 0 and half == 0 and m != 4:
                                norm_sum(m)
                pair(0, True)
                with pe.Fori(1, KF // 2) as i:
                    pair(i, False)

            def down(u, m):
                pe.wait_ge(gu_evac, 2 + KF * (u + 1))
                for j in range(KD):
                    k0 = 0
                    if j >= 4:
                        pe.wait_ge(h_new, 8 * m + j - 3)
                    for b, w in enumerate(DN_TILES):
                        n = BASE[f"dn{u}"] + 3 * j + b
                        if j == 0:
                            pe.wait_ge(al_ready, KF * u + k0 + w)
                        weights(n)
                        product(bank[j % 4][:, 0:TOK], n % SLOTS, 0, w, lambda k: ah[:, k0 + k, :],
                                lambda k: al[:, k0 + k, :], b == 0, b == 2).then_inc(blk, 1)
                        k0 += w

            def ple_pe(l, m):
                pe.wait_ge(pl_ready, l + 1)
                pe.wait_ge(xl_ready, 8 * (m + 1))
                for i in range(2):
                    n = BASE[f"pi{l}"] + i
                    weights(n)
                    for jj in range(4):
                        if i:
                            pe.wait_ge(pin_ready, 8 * l + jj + 1)
                        ins = product(bank[jj][:, 0:TOK], n % SLOTS, 2 * jj, 2 * jj + 2, lambda k: phi[:, k % 2, :],
                                      lambda k: plo[:, k % 2, :], True, True)
                    ins.then_inc(blk, 1)
                    if i == 0:
                        norm_sum(m)
                pe.wait_ge(pin_ready, 8 * l + 8)
                for j in range(KD):
                    n = BASE[f"pg{l}"] + j
                    weights(n)
                    if j >= 4:
                        pe.wait_ge(pg_evac, 8 * l + j - 3)
                    product(bank[j % 4][:, 0:TOK], n % SLOTS, 0, KD, *X, True, True).then_inc(blk, 1)

            pe.wait_ge(ones_ready, 1)
            gate_up(0, 0)
            down(0, 1)

            pe.wait_ge(xl_ready, 16)
            weights(MIX)
            product(bank[4][:, 0:TOK], MIX % SLOTS, 0, KD, *X, True, True).then_inc(blk, 1)
            norm_sum(1)
            for g in range(GROUPS):
                for b in range(10):
                    n = group0(g) + b
                    weights(n)
                    if b >= 4:
                        pe.wait_ge(in_evac, 10 * g + b - 3)
                    elif g:
                        pe.wait_ge(y_evac, 4 * g)
                    else:
                        pe.wait_ge(xl_ready, 16)
                    product(bank[b % 4][:, 0:TOK], n % SLOTS, 0, KD, *X, True, True).then_inc(blk, 1)
                if g == 0:
                    pe.wait_ge(dt_ready, 1)
                    pe.wait_ge(const_ld, 160)
                    for t in range(TT):
                        for x, v in ((0, dv[2]), (96, dv[1])):
                            ins = nc.tensor.transpose(bank[5][:, x + 32 * t:x + 32 * t + 32], v[:, tiles(t)],
                                                      ident[0:HEADS, 0:HEADS])
                    ins.then_inc(dtT_ps, 1)
                    pe.wait_ge(dtR_ready, 1)
                    for t in range(TT):
                        M(bank[6][:, 32 * t:32 * t + 32], mask[:, t, :], aR[:, t, :], start=True, stop=True)
                        M(bank[6][:, 96 + 32 * t:128 + 32 * t], ones[:, :] if t < 2 else same[:, :], aR[:, t, :],
                          start=True, stop=True)
                    M(bank[5][:, 0:STREAMS * HEADS], ones[:, :], am.rearrange("p s h -> p (s h)"), start=True,
                      stop=True).then_inc(ac_ps, 1)
                    pe.wait_ge(da_ready, 1)
                else:
                    pe.wait_ge(f_evac, 8 * g)
                pe.wait_ge(conv_done, 6 * g + 6)
                for t in range(TT):
                    for i in range(4):
                        ins = nc.tensor.transpose(bank[4 + t][:, tiles(i)], xsT[:, i, tiles(t)], ident[:, :])
                    ins.then_inc(xt_ps, 1)
                for t in range(TT):
                    ins = nc.tensor.transpose(bank[7][:, tiles(t)], BC[:, 0, tiles(t)], ident[:, :])
                ins.then_inc(bt_ps, 1)
                pe.wait_ge(brow_ready, g + 1)
                for t in range(TT):
                    ins = M(bank[7][:, tiles(t)], BC[:, 0, tiles(t)], BC[:, 1, tiles(t)], start=True, stop=True)
                ins.then_inc(g_ps, 1)

                def running(t):
                    if t:
                        pe.wait_ge(d_ready, 3 * g + t)
                    for hh in range(HPG):
                        a = aR[:, t, HPG * g + hh:HPG * g + hh + 1].broadcast_to((P, P))
                        ins = M(bank[4 + hh // 4][:, tiles(hh % 4)], a, mask[:, t, :], start=True, stop=True)
                    ins.then_inc(ab_ps, 1)

                def y_tile(t):
                    s = (3 * g + t) % 2
                    pe.wait_ge(m_ready, 3 * g + t + 1)
                    if t:
                        pe.wait_ge(yo_ready, 2 * g + t)
                    for i in range(4):
                        if t:
                            M(bank[i][:, tiles(t)], yoff[:, t - 1, tiles(i)], ident[:, :], start=True, stop=False,
                              skip_group_check=True)
                        for e in range(2):
                            hh = 2 * i + e
                            ins = M(bank[i][HD * e:HD * e + HD, tiles(t)], xdt[:, t, hh * HD:hh * HD + HD],
                                    seg[:, s, tiles(hh)], start=t == 0, stop=True, skip_group_check=True)
                    ins.then_inc(ym_done, 1)

                pe.wait_ge(xdt_ready, 3 * g + 3)
                running(0)
                pe.wait_ge(xw_ready, 3 * g + 3)
                M(bank[6][:, :], Brow[:, 0, :], xw[:, 0, :], start=True, stop=True).then_inc(u_ps, 1)
                pe.wait_ge(s1_ready, 2 * g + 1)
                pe.wait_ge(gm_ready, g + 1)
                M(bank[7][:, :], BC[:, 1, tiles(1)], S1[:, :], start=True, stop=True).then_inc(yo_ps, 1)
                M(bank[6][:, :], Brow[:, 1, :], xw[:, 1, :], start=True, stop=True).then_inc(u_ps, 1)
                pe.wait_ge(in_evac, 10 * g + 10)
                y_tile(0)
                running(1)
                pe.wait_ge(s_ld, 16 * (g + 1))
                pe.wait_ge(bm_ready, g + 1)
                pe.wait_ge(yo_ready, 2 * g + 1)
                for b in range(STREAMS):
                    ins = M(bank[7][:, :], Cm[:, b, :], S[:, b, :], start=b == 0, stop=b == STREAMS - 1)
                ins.then_inc(yo_ps, 1)
                y_tile(1)
                running(2)
                for b in range(STREAMS):
                    if b == 0:
                        pe.wait_ge(s1_ready, 2 * g + 2)
                    elif b == 1:
                        pe.wait_ge(yo_ready, 2 * g + 2)
                    else:
                        pe.wait_ge(su_done, 8 * g + b - 1)
                    M(bank[6 + b % 2][:, :], Bm[:, b, :], xw[:, 2, :], start=True, stop=True).then_inc(u_ps, 1)
                y_tile(2)
                pe.wait_ge(yl_ready, 4 * g + 4)
                pe.wait_ge(su_done, 8 * g + 8)
                for b in range(4):
                    n = group0(g) + 10 + b
                    weights(n)
                    for x in range(2):
                        j = 2 * b + x
                        if b >= 2:
                            pe.wait_ge(f_evac, 8 * g + j - 3)
                        ins = product(bank[4 + j % 4][:, 0:TOK], n % SLOTS, 4 * x, 4 * x + 4, lambda k: yh[:, k % 4, :],
                                      lambda k: yl[:, k % 4, :], True, True)
                    ins.then_inc(blk, 1)
            pe.wait_ge(sqy, 16)
            pe.wait_ge(f_evac, 8 * GROUPS)
            M(bank[7][:, 0:TOK], ones[:, :], sqacc[:, 0, :], start=True, stop=True).then_inc(yms, 1)
            gate_up(1, 2)
            down(1, 3)
            ple_pe(0, 3)

            def token_rows(m, x):
                pe.wait_ge(rstd_ready, m + 1)
                for t in range(TT):
                    ins = nc.tensor.transpose(bank[4][:, tiles(t)], rstd[:, m % 2, tiles(t)], ident[:, :])
                ins.then_inc(rt_ps, 1)

            pe.wait_ge(kxl_ready, KD)
            k = 0
            for b in range(3):
                weights(KV + b)
                for kk in range(WIDTH[KV + b] // 288):
                    for t in range(TT):
                        ins = row_product(bank[t][:, 0:288], (KV + b) % SLOTS, 288 * kk, 288, kxh[:, k, tiles(t)],
                                          kxl[:, k, tiles(t)], k == 0, k == KD - 1)
                    k += 1
                ins.then_inc(blk, 1)
            norm_sum(4)
            token_rows(4, 0)
            pe.wait_ge(kv_done, TT)
            for t in range(TT):
                for k in range(2):
                    nc.tensor.transpose(bank[5 + k][:, tiles(t)], ckv[:, t, tiles(k)], ident[:, :])
                ins = nc.tensor.transpose(bank[4][0:QD, tiles(t)], krow[:, t, :], ident[:, :])
            ins.then_inc(cT_ps, 1)
            gate_up(2, 4)
            down(2, 5)

            pe.wait_ge(xl_ready, 48)
            for b in range(4):
                weights(DQ + b)
                for kk in range(2):
                    k = 2 * b + kk
                    for t in range(TT):
                        ins = row_product(bank[t][:, :], (DQ + b) % SLOTS, 512 * kk, 512, xh[:, k, tiles(t)],
                                          xl[:, k, tiles(t)], k == 0, k == KD - 1)
                ins.then_inc(blk, 1)
                if b == 0:
                    norm_sum(5)
            pe.wait_ge(cT_ready, 1)
            token_rows(5, 1)
            for t in range(TT):
                pe.wait_ge(cqn_ready, t + 1)
                for k in range(4):
                    ins = nc.tensor.transpose(bank[4 + k][:, tiles(t)], cqr[:, t, tiles(k)], ident[:, :])
            ins.then_inc(cqT_ps, 1)
            pe.wait_ge(cql, 4)

            def q_transpose(e):
                pe.wait_ge(qr_ready, e + 1)
                if e >= 2:
                    pe.wait_ge(qe, e - 1)
                for hh in range(4):
                    ins = nc.tensor.transpose(bank[6 + e % 2][0:QD, tiles(hh)], kn[:, e % 2, QD * hh:QD * hh + QD], ident[:, :])
                ins.then_inc(qt_ps, 1)

            for cg in range(4):
                if cg >= 2:
                    pe.wait_ge(qb_evac, 3 * (cg - 1))
                for b in range(2):
                    n = QB + 2 * cg + b
                    weights(n)
                    for kk in range(2):
                        k = 2 * b + kk
                        for t in range(TT):
                            ins = row_product(bank[3 * (cg % 2) + t][:, 0:384], n % SLOTS, 384 * kk, 384, xh[:, k, tiles(t)],
                                              xl[:, k, tiles(t)], k == 0, k == 3)
                    ins.then_inc(blk, 1)
                if cg:
                    for t in range(TT):
                        q_transpose(3 * (cg - 1) + t)
            for t in range(TT):
                q_transpose(9 + t)

            def expand(w):
                t, g = divmod(w, 2)
                if w >= 2:
                    pe.wait_ge(ks4, w - 1)
                for k in range(2):
                    ins = M(bank[w % 2][:, :], cT[:, k, tiles(t)], wk[:, k, 512 * g:512 * g + 512], start=k == 0, stop=k == 1)
                ins.then_inc(ex_ps, 1)

            pe.wait_ge(w_ld, 16 * 5)
            pe.wait_ge(qb_evac, 12)
            expand(0)
            for w in range(ITEMS):
                if w + 1 < ITEMS:
                    expand(w + 1)
                if w < 4:
                    pe.wait_ge(ks4, w + 1)
                    if w:
                        pe.wait_ge(kt_ev, w)
                    for hh in range(8):
                        ins = nc.tensor.transpose(bank[2 + hh // 4][0:QD, tiles(hh % 4)], kn[:, w % 2, QD * hh:QD * hh + QD], ident[:, :])
                    ins.then_inc(kt_ps, 1)
            pe.wait_ge(qe, 12)
            for v in range(4):
                for k in range(2):
                    ins = M(bank[4 + v][:, :], cT[:, k, tiles(v // 2)], wv[:, k, 512 * (v % 2):512 * (v % 2) + 512],
                            start=k == 0, stop=k == 1)
                ins.then_inc(vp_ps, 1)
            pe.wait_ge(vp_ev, 4)
            pe.wait_ge(kt_ev, 4)
            pe.wait_ge(ks4, ITEMS)

            def p_scores(x):
                if x >= 2:
                    pe.wait_ge(pa1, x - 1)
                out = bank[4 + x % 2]
                M(out[:, 0:128], Qp[0:QD, x, 0:128], Kp[0:QD, x, 0:128], start=True, stop=True)
                M(out[:, 128:384], Qp[0:QD, x, 128:256], Kp[0:QD, x, 0:256], start=True, stop=True).then_inc(qk_ps, 1)

            def past_expand(w):
                b, st, g = w // 8, w // 2 % 4, w % 2
                if w % 8 == 0:
                    pe.wait_ge(past_lo, b + 1)
                if w >= 2:
                    pe.wait_ge(past_sq, w - 1)
                for k in range(2):
                    ch, cl = cTh[:, b % 2, k, tiles(st)], cTl[:, b % 2, k, tiles(st)]
                    half = slice(512 * g, 512 * g + 512)
                    M(bank[w % 2][:, :], ch, wkh[:, k, half], start=k == 0, stop=False)
                    M(bank[w % 2][:, :], ch, wkl[:, k, half], start=False, stop=False)
                    ins = M(bank[w % 2][:, :], cl, wkh[:, k, half], start=False, stop=k == 1)
                ins.then_inc(past_ps, 1)

            pe.wait_ge(wk_lo, 2)
            p_scores(0)
            for x in range(MH):
                if x + 1 < MH:
                    p_scores(x + 1)
                past_expand(4 * x)
                past_expand(4 * x + 1)
                pe.wait_ge(pa4, x + 1)
                for j in range(3):
                    ins = nc.tensor.transpose(bank[6][:, tiles(j)], Pb[:, x % 2, tiles(j)], ident[:, :])
                ins.then_inc(pt_ps, 1)
                past_expand(4 * x + 2)
                pe.wait_ge(pt_ev, x + 1)
                if x % 2 == 0 and x >= 4:
                    pe.wait_ge(ol_ready, x // 2 - 1)
                o = bank[7 if x // 2 % 2 else 3][VH * (x % 2):VH * (x % 2) + VH, :]
                v0, v1 = (Vp[:, k, VH * x:VH * x + VH] for k in range(2))
                M(o[:, 0:128], v0, PT[:, 0:128], start=True, stop=True)
                M(o[:, 128:256], v0, PT[:, 128:256], start=True, stop=False)
                M(o[:, 128:256], v1, PT[:, 256:384], start=False, stop=True).then_inc(po_ps, 1)
                past_expand(4 * x + 3)

            pe.wait_ge(wkT_ld, 16)
            pe.wait_ge(ol_ready, MH // 2)
            pe.wait_ge(past_sq, 8 * STREAMS)
            for j in range(8):
                if j >= 4:
                    pe.wait_ge(qc_ev, j - 3)
                for k in range(2):
                    for hh in range(2):
                        x = 2 * j + hh
                        ins = M(bank[j % 4][:, tiles(2 * k + hh)], wkT[0:QD, x, tiles(k)], Qs[0:QD, :, x, :], start=True, stop=True)
                ins.then_inc(qc_ps, 1)
            pe.wait_ge(new_rq, 2)
            for g in range(2):
                ins = nc.tensor.transpose(bank[4][:, tiles(g)], rq[:, 0, tiles(g)], ident[:, :])
            ins.then_inc(new_rt, 1)
            pe.wait_ge(qc_ev, 8)
            pe.wait_ge(new_rk, 1)

            def s_nope(u):
                b, g = divmod(u, 2)
                if g == 0:
                    pe.wait_ge(c_ld[b % 2], 16 * (STREAMS // 2 + b // 2 + 1))
                if u:
                    pe.wait_ge(sa1, u)
                for k in range(2):
                    q = QC[:, k, b, 8 * g:8 * g + 8, :].rearrange("p h q -> p (h q)")
                    M(bank[2][:, :], q, cTb[:, b % 2, k, :], start=k == 0, stop=k == 1)
                    M(bank[5][:, 0:P], q, cT[:, k, SEQ:TOK], start=k == 0, stop=k == 1)

            def s_rope(u):
                b, g = divmod(u, 2)
                if u:
                    pe.wait_ge(rk_ready, u)
                pe.wait_ge(rq_ready, u + 1)
                for st in range(4):
                    ins = nc.tensor.transpose(bank[3][:, tiles(st)], rq[:, u % 2, tiles(st)], ident[:, :])
                ins.then_inc(rt_done, 1)
                if g == 0:
                    pe.wait_ge(kr_ld, 16 * (b + 1))
                q = Qs[0:QD, b, 8 * g:8 * g + 8, :].rearrange("p h q -> p (h q)")
                M(bank[4][:, :], q, krTb[0:QD, :], start=True, stop=True)
                M(bank[5][:, P:2 * P], q, krT[0:QD, SEQ:TOK], start=True, stop=True).then_inc(sc_ps, 1)

            def s_turn(u):
                pe.wait_ge(olr, u + 1)
                if u:
                    pe.wait_ge(olt, u)
                for k in range(2):
                    ins = nc.tensor.transpose(bank[1][:, tiles(k)], ol[:, tiles(k)], ident[:, :])
                ins.then_inc(ot_ps, 1)

            s_nope(0)
            s_rope(0)
            for u in range(UNITS):
                b = u // 2
                if u + 1 < UNITS:
                    s_nope(u + 1)
                if u:
                    s_turn(u - 1)
                pe.wait_ge(sa3, u + 1)
                for j in range(5):
                    ins = nc.tensor.transpose(bank[6][:, tiles(j)] if j < 4 else bank[0][:, 0:P], Pb[:, u % 2, tiles(j)], ident[:, :])
                ins.then_inc(pt_ps, 1)
                if u + 1 < UNITS:
                    s_rope(u + 1)
                pe.wait_ge(pt_ev, MH + u + 1)
                if u % 2 == 0:
                    pe.wait_ge(cn_ld[b % 2], 16 * (b // 2 + 1))
                for j in range(5):
                    ins = M(bank[7][:, 256:512], PT[:, tiles(j)], cnat[:, b % 2, j, :] if j < 4 else ckv[:, 2, :],
                            start=j == 0, stop=j == 4)
                ins.then_inc(po_ps, 1)
            s_turn(UNITS - 1)
            pe.wait_ge(olt, 2 * STREAMS)
            for x in range(MH):
                if x % 2 == 0 and x >= 4:
                    pe.wait_ge(ol_ready, MH // 2 + x // 2 - 1)
                o = bank[x // 2 % 2][VH * (x % 2):VH * (x % 2) + VH, 0:P]
                for k in range(2):
                    ins = M(o, wv[:, k, VH * x:VH * x + VH], QC[:, k, :, x, :], start=k == 0, stop=k == 1)
                if x % 2:
                    ins.then_inc(os_ps, 1)
            pe.wait_ge(ol_ready, MH)
            for b in range(8):
                weights(WO + b)
                if b >= 4:
                    pe.wait_ge(h_new, 48 + b - 3)
                product(bank[2 + b % 4][:, 0:TOK], (WO + b) % SLOTS, 0, KD, *X, True, True).then_inc(blk, 1)
            gate_up(3, 6)
            down(3, 7)
            ple_pe(1, 7)


def tile_blocks(w, cols=P):
    k, m = w.shape
    return w.reshape(k // P, P, m // cols, cols).transpose(2, 1, 0, 3).reshape(m // cols, P, -1)


def kernel(**inp):
    import concourse.bacc as bacc
    from concourse.bass_utils import run_bass_kernel_spmd
    A = {k: np.asarray(v) for k, v in inp.items()}
    f32 = np.float32

    stream = np.zeros((NBLK, P, 1024), f32)

    def put(stage, blocks, first=0):
        b0 = BASE[stage] + first
        for j, w in enumerate(blocks):
            stream[b0 + j, :, :w.shape[-1]] = w

    for u, (l, s) in enumerate(((0, 1), (0, 2), (1, 1), (1, 2))):
        gate, up = (tile_blocks(A[f"w{s}_{x}"][l]) for x in ("gate", "up"))
        put(f"gu{u}", np.stack([gate, up], 1).reshape(2 * KF, P, 1024))
        down, at = tile_blocks(A[f"w{s}_down"][l]), [0, 8, 15, 22]
        put(f"dn{u}", [down[j][:, at[b] * P:at[b + 1] * P] for j in range(KD) for b in range(3)])
    w_in = A["a_in_proj"][0]
    w_dt = np.zeros((D_MODEL, P), f32)
    w_dt[:, :HEADS] = w_in[:, D_INNER + CONV_DIM:]
    put("mix", tile_blocks(w_dt))
    zt, ct = tile_blocks(w_in[:, :D_INNER]), tile_blocks(w_in[:, D_INNER:D_INNER + CONV_DIM])
    w_out = A["a_out_proj"][0]
    for g in range(GROUPS):
        put("mix", [ct[4 * g + i] for i in range(4)] + [ct[16 + g], ct[20 + g]] + [zt[4 * g + i] for i in range(4)], 1 + 14 * g)
        o = tile_blocks(w_out[512 * g:512 * g + 512])
        put("mix", o.reshape(4, 2, P, 512).transpose(0, 2, 1, 3).reshape(4, P, 1024), 1 + 14 * g + 10)
    for l in range(2):
        o = tile_blocks(A["w_ple_in"][l])
        put(f"pi{l}", o.reshape(2, 4, P, 256).transpose(0, 2, 1, 3).reshape(2, P, 1024))
        put(f"pg{l}", tile_blocks(A["w_ple_gate"][l]))

    def row_blocks(w, per):
        k = w.reshape(KD if w.shape[0] == D_MODEL else w.shape[0] // P, P, -1)
        return [k[i:i + per].transpose(1, 0, 2).reshape(P, -1) for i in range(0, k.shape[0], per)]

    put("kv", row_blocks(A["w_kv_a"], 3))
    put("dq", row_blocks(A["b_w_dq"][0], 2))
    for cg in range(4):
        put("qb", row_blocks(np.ascontiguousarray(A["b_w_q_b"][0][:, 384 * cg:384 * cg + 384]), 2), 2 * cg)
    put("wo", tile_blocks(A["b_w_o"][0]))

    def feat(x):
        return np.ascontiguousarray(x.reshape(x.shape[0], -1, P).transpose(2, 1, 0))

    def both(a, b):
        return np.concatenate([a.reshape(SEQ, -1), b.reshape(TOK - SEQ, -1)])

    def col(v):
        return v.reshape(-1, P).T

    def every(v):
        return np.ascontiguousarray(np.broadcast_to(v, (P,) + v.shape))

    arr = {"stream": stream, "x": feat(both(A["x_prompt"], A["x_sample"]))}
    arr["p"] = np.stack([feat(both(A["p_prompt"][l], A["p_sample"][l])) for l in range(2)])
    norm_gains = [A["ln_ffn1"][0], A["ln_mix"][0], A["ln_ffn2"][0], A["ln_ple"][0], A["ln_ffn1"][1], A["ln_mix"][1],
                  A["ln_ffn2"][1], A["ln_ple"][1], A["ln_kv"]]
    arr["gains"] = np.stack([col(v) for v in norm_gains], 1)
    arr["ident"] = np.eye(P, dtype=f32)
    arr["cstate"] = A["state_conv"][0].reshape(STREAMS, 3, KC, P).transpose(3, 2, 0, 1).reshape(P, KC, STREAMS * 3)
    arr["cw"] = np.concatenate([A["a_conv_w"][0], A["a_conv_b"]], 0).reshape(CONV_W + 1, KC, P).transpose(2, 1, 0)
    arr["dcol"] = col(np.repeat(A["a_D"][0], HD))
    arr["ang"] = col(A["a_norm"][0])
    row, cl = np.arange(P)[:, None], np.arange(P)[None, :]
    tri, blk16 = (row <= cl), (row // STEPS == cl // STEPS)
    arr["mask"] = np.stack([tri, tri, tri & blk16], 1).astype(f32)
    arr["same"] = blk16.astype(f32)
    arr["ind"] = (row // STEPS == np.arange(STREAMS)[None, :]).astype(f32)
    arr["dts"] = np.stack([A["a_dt_bias"][0], A["a_A_log"][0]], 1)
    arr["ssm"] = A["state_ssm"][0].reshape(STREAMS, GROUPS, 512, N).transpose(1, 3, 0, 2)
    arr["kvg"] = every(np.concatenate([A["kv_norm"], A["kr_norm"]]))
    inv = f32(10000.0) ** (-np.arange(ROPE // 2, dtype=f32) / f32(ROPE // 2))
    pos = np.concatenate([np.arange(SEQ), np.tile(PAST + np.arange(STEPS), STREAMS)]).astype(f32)
    ang_ = pos[:, None] * inv[None, :]
    arr["cos"] = np.tile(np.cos(ang_).astype(f32), 2).reshape(TT, P, -1).transpose(1, 0, 2)
    arr["sin"] = np.tile(np.sin(ang_).astype(f32), 2).reshape(TT, P, -1).transpose(1, 0, 2)
    arr["qgr"] = every(A["b_q_norm"][0])
    arr["gr"] = every(A["b_qn_rope"][0])
    pad = np.ones(P - NOPE, f32)
    arr["gq"] = np.stack([np.concatenate([A["b_qn_nope"][0], pad]), np.concatenate([A["k_norm"], pad])], 1)
    wkv = A["w_kv_b"].reshape(2, P, MH, NOPE + VH)
    arr["wk"] = wkv[..., :NOPE].transpose(1, 0, 2, 3).reshape(P, 2, -1)
    arr["wv"] = wkv[..., NOPE:].transpose(1, 0, 2, 3).reshape(P, 2, -1)
    arr["wkT"] = np.zeros((QD, MH, KV_LORA), f32)
    arr["wkT"][:NOPE] = A["w_kv_b"].reshape(KV_LORA, MH, NOPE + VH)[..., :NOPE].transpose(2, 1, 0)
    diag = np.where((cl // 64) <= (row // 64), 0.0, -1e30).astype(f32)
    arr["mk"] = np.concatenate([diag, np.zeros((P, P), f32), diag], 1)
    cache = A["cache_kv_latent"]
    arr["cache"] = cache.reshape(STREAMS, 4, P, KV_LORA).transpose(0, 2, 1, 3)
    arr["cacheT"] = cache.reshape(STREAMS, PAST, 2, P).transpose(0, 3, 2, 1)
    arr["krcT"] = A["cache_k_rope"].transpose(0, 2, 1)
    outs = {"y": (P, KD, TOK), "ssm_p": (GROUPS, P, 512), "ssm_s": (GROUPS, P, STREAMS, 512),
            "conv": (P, KC, 27), "kvl": (P, TT, KV_LORA), "kr": (P, TT, ROPE)}

    nc = bacc.Bacc("TRN2", target_bir_lowering=False, num_devices=1)
    T = {}
    sent = {}
    for name, a in arr.items():
        sent[f"in_{name}"] = np.ascontiguousarray(a)
        T[name] = nc.dram_tensor(f"in_{name}", a.shape, F32, kind="ExternalInput").ap()
    for name, shape in outs.items():
        T[name] = nc.dram_tensor(f"out_{name}", shape, F32, kind="ExternalOutput").ap()
    build(nc, T)
    got = run_bass_kernel_spmd(nc, [sent], core_ids=[0]).results[0]
    got = {name: np.asarray(got[f"out_{name}"]) for name in outs}

    y = got["y"].transpose(2, 1, 0).reshape(TOK, D_MODEL)
    kvl = got["kvl"].transpose(1, 0, 2).reshape(TOK, KV_LORA)
    kr = got["kr"].transpose(1, 0, 2).reshape(TOK, ROPE)
    conv = got["conv"].transpose(2, 1, 0).reshape(27, CONV_DIM)
    ssm_p = got["ssm_p"].reshape(GROUPS, N, HPG, HD).transpose(0, 2, 3, 1).reshape(1, 1, HEADS, HD, N)
    ssm_s = got["ssm_s"].reshape(GROUPS, N, STREAMS, HPG, HD).transpose(2, 0, 3, 4, 1).reshape(1, STREAMS, HEADS, HD, N)
    outs_ = (y[:SEQ].reshape(1, SEQ, D_MODEL), y[SEQ:].reshape(STREAMS, STEPS, D_MODEL),
             conv[:3].reshape(1, 1, 3, CONV_DIM), ssm_p,
             kvl[:SEQ].reshape(1, SEQ, KV_LORA), kr[:SEQ].reshape(1, SEQ, ROPE),
             conv[3:].reshape(1, STREAMS, 3, CONV_DIM), ssm_s,
             kvl[SEQ:].reshape(STREAMS, STEPS, KV_LORA), kr[SEQ:].reshape(STREAMS, STEPS, ROPE))
    return tuple(np.ascontiguousarray(o) for o in outs_)
```

```python
import concourse.bass as bass
from concourse import mybir
from contextlib import ExitStack
import numpy as np

F32 = mybir.dt.float32
F32R = mybir.dt.float32r
ALU = mybir.AluOpType
ACT = mybir.ActivationFunctionType
AX = mybir.AxisListType

P = 128
D_MODEL = 1024
SEQ, STREAMS, STEPS = 256, 8, 16
TOK = SEQ + STREAMS * STEPS
TT = TOK // P
KD = D_MODEL // P
D_FF = 2816
KF = D_FF // P
PLE = 256
D_INNER = 2048
HEADS, HD, GROUPS, N = 32, 64, 4, 128
HPG = HEADS // GROUPS
CONV_W = 4
CONV_DIM = D_INNER + 2 * GROUPS * N
KC = CONV_DIM // P
PAST = 512
MH, NOPE, ROPE, VH = 16, 64, 32, 64
QD = NOPE + ROPE
Q_LORA, KV_LORA = 512, 256
SCALE = (NOPE + ROPE) ** -0.5
EPS = 1e-6

SLOTS = 4
AHEAD = 3
STAGES = [("gu0", 44), ("dn0", 24), ("mix", 57), ("gu1", 44), ("dn1", 24), ("pi0", 2), ("pg0", 8),
          ("kv", 3), ("gu2", 44), ("dn2", 24), ("dq", 4), ("qb", 8), ("wo", 8), ("gu3", 44),
          ("dn3", 24), ("pi1", 2), ("pg1", 8)]
DN_TILES = (8, 7, 7)
BASE, WIDTH = {}, []
for _name, _n in STAGES:
    BASE[_name] = len(WIDTH)
    for _b in range(_n):
        WIDTH.append(DN_TILES[_b % 3] * P if _name[:2] == "dn" else
                     (864, 864, 576)[_b] if _name == "kv" else 2 * 384 if _name == "qb" else 1024)
NBLK = len(WIDTH)
NORMS = 8


def build(nc, T):
    ctx = ExitStack()
    with ctx:
        def sb(name, shape, dt=F32, c=ctx):
            return c.enter_context(nc.sbuf_tensor(name, shape, dt))

        def sem(name):
            return ctx.enter_context(nc.semaphore(name))

        h = sb("h", [P, KD, TOK])
        xh = sb("xh", [P, KD, TOK], F32R)
        xl = sb("xl", [P, KD, TOK], F32R)
        raw = sb("raw", [P, SLOTS, 1024])
        whi = sb("whi", [P, SLOTS, 1024], F32R)
        wlo = sb("wlo", [P, SLOTS, 1024], F32R)
        gains = sb("gains", [P, NORMS + 1, KD])
        ident = sb("ident", [P, P])
        ones = sb("ones", [P, P])
        std = sb("std", [P, TOK])
        rstd = sb("rstd", [P, 2, TOK])
        sqt = sb("sqt", [P, TOK])
        sqacc = sb("sqacc", [P, 2, TOK])
        rows = sb("rows", [P, 2, TT])
        bank = [ctx.enter_context(nc.psum_tensor(f"bank{i}", [P, 512], F32)) for i in range(8)]

        with ExitStack() as ffn:
            ah = sb("ah", [P, KF, TOK], F32R, ffn)
            al = sb("al", [P, KF, TOK], F32R, ffn)
            tg = sb("tg", [P, 2, TOK], F32, ffn)
            tu = sb("tu", [P, 2, TOK], F32, ffn)
        XPW = 3 + SEQ + STREAMS * (3 + STEPS)
        CW = XPW - 3
        SAMP0 = 3 + SEQ
        with ExitStack() as ssd:
            yh = sb("yh", [P, 4, TOK], F32R, ssd)
            yl = sb("yl", [P, 4, TOK], F32R, ssd)
            facc = sb("facc", [P, KD, TOK], F32, ssd)
            zs = sb("zs", [P, 4, TOK], F32, ssd)
            xsT = sb("xsT", [P, 4, TOK], F32, ssd)
            BC = sb("BC", [P, 2, TOK], F32, ssd)
            xdt = sb("xdt", [P, TT, 512], F32, ssd)
            xw = sb("xw", [P, TT, 512], F32, ssd)
            seg = sb("seg", [P, 2, 1024], F32, ssd)
            Gm = sb("Gm", [P, TOK], F32, ssd)
            Brow = sb("Brow", [P, TT, P], F32, ssd)
            Bm = sb("Bm", [P, STREAMS, P], F32, ssd)
            Cm = sb("Cm", [P, STREAMS, P], F32, ssd)
            S = sb("S", [P, STREAMS, 512], F32, ssd)
            S1 = sb("S1", [P, 512], F32, ssd)
            yoff = sb("yoff", [P, 2, 512], F32, ssd)
            xp = sb("xp", [P, 2, XPW + 1], F32, ssd)
            cy = sb("cy", [P, 2, XPW + 1], F32, ssd)
            cstate = sb("cstate", [P, KC, STREAMS * 3], F32, ssd)
            cout = sb("cout", [P, KC, 3 + STREAMS * 3], F32, ssd)
            cw = sb("cw", [P, KC, CONV_W + 1], F32, ssd)
            dcol = sb("dcol", [P, 16], F32, ssd)
            ang = sb("ang", [P, 16], F32, ssd)
            mask = sb("mask", [P, TT, P], F32, ssd)
            same = sb("same", [P, P], F32, ssd)
            ind = sb("ind", [P, STREAMS], F32, ssd)
            dtR = sb("dtR", [P, TT, HEADS], F32, ssd)
            aR = sb("aR", [P, TT, HEADS], F32, ssd)
            acs = sb("acs", [P, TT, HEADS], F32, ssd)
            toend = sb("toend", [P, TT, HEADS], F32, ssd)
            eacs = sb("eacs", [P, TT, HEADS], F32, ssd)
            dec = sb("dec", [P, STREAMS + 1, HEADS], F32, ssd)
            dts = sb("dts", [HEADS, 2], F32, ssd)
        am = Bm[:, 0:2, :].rearrange("p a b -> p (a b)").rearrange("p (s h) -> p s h", s=STREAMS)
        dv = [seg[0:HEADS, i // 2, (i % 2) * TOK:(i % 2 + 1) * TOK] for i in range(4)] + \
             [xdt[0:HEADS, i, 0:TOK] for i in range(3)]
        with ExitStack() as ple:
            pin = sb("pin", [P, KD, TOK], F32, ple)
            tp = sb("tp", [P, 2, TOK], F32, ple)
            kxh = sb("kxh", [P, KD, TOK], F32R, ple)
            kxl = sb("kxl", [P, KD, TOK], F32R, ple)
            kvr = sb("kvr", [P, TT, KV_LORA + ROPE], F32, ple)
            krot = sb("krot", [P, TT, 2, ROPE], F32, ple)
        with ExitStack() as mla:
            lowA = sb("lowA", [P, 4096], F32, mla)
            lowB = sb("lowB", [P, 4096], F32, mla)
            lowC = sb("lowC", [P, 2048], F32, mla)
            Qs = sb("Qs", [P, STREAMS, MH, STEPS], F32, mla)
            with ExitStack() as split:
                wk = sb("wk", [P, 2, MH * NOPE], F32, split)
            wkl = sb("wkl", [P, 2, MH * NOPE], F32R, mla)
            wkh = sb("wkh", [P, 2, MH * NOPE], F32R, mla)
            wv = sb("wv", [P, 2, MH * VH], F32, mla)
            with ExitStack() as emb:
                phi = sb("phi", [P, 2, TOK], F32R, emb)
                plo = sb("plo", [P, 2, TOK], F32R, emb)
            cTh = sb("cTh", [P, 2, 2, PAST], F32R, mla)
            ckv = sb("ckv", [P, TT, KV_LORA], F32, mla)
            cT = sb("cT", [P, 2, TOK], F32, mla)
            krT = sb("krT", [P, TOK], F32, mla)
            krow = sb("krow", [P, TT, QD], F32, mla)
            rsc = sb("rsc", [P, TT, 8], F32, mla)
            cosr = sb("cosr", [P, TT, ROPE], F32, mla)
            sinr = sb("sinr", [P, TT, ROPE], F32, mla)
            with ExitStack() as split:
                cTb = sb("cTb", [P, 2, 2, PAST], F32, split)
            cTl = sb("cTl", [P, 2, 2, PAST], F32R, mla)
            sq5 = sb("sq5", [P, 2, 512], F32, mla)
            rsn = sb("rsn", [P, MH], F32, mla)
            kn = sb("kn", [P, 2, 8 * QD], F32, mla)
            Pb = sb("Pb", [P, 2, 640], F32, mla)
            gq = sb("gq", [P, 3], F32, mla)
            gr = sb("gr", [P, ROPE], F32, mla)
            sm = sb("sm", [P, 128], F32, mla)
        Kp = lowA[:, :].rearrange("p (h t) -> p h t", h=MH)
        wkT = lowA[:, :].rearrange("p (h c) -> p h c", h=MH)
        QC = lowB[:, :].rearrange("p (k b h q) -> p k b h q", k=2, b=STREAMS, h=MH)
        Qp = lowB[:, :].rearrange("p (h t) -> p h t", h=MH)
        cnat = lowC[:, :].rearrange("p (s k c) -> p s k c", s=2, k=4)
        Vp = lowC[:, :].rearrange("p (k c) -> p k c", k=2)
        knf = kn[:, :, :].rearrange("p s c -> p (s c)")

        def q_rows(e):
            return knf[:, 384 * (e % 3):384 * (e % 3) + 384].rearrange("p (h d) -> p h d", h=4)

        def q_rope(e):
            return knf[:, 1152 + 128 * (e % 2):1280 + 128 * (e % 2)].rearrange("p (h d) -> p h d", h=4)

        q_sin = knf[:, 1408:1536].rearrange("p (h d) -> p h d", h=4)
        PT = rstd[:, :, :].rearrange("p a t -> p (a t)")[:, 0:640]
        ol = std[:, 0:KV_LORA]
        rbn = sqt[:, 0:2 * P].rearrange("p (g t) -> p g t", g=2)
        ksq = sqacc[:, :, :].rearrange("p a t -> p (a t)")[:, 0:STREAMS * 4 * MH].rearrange(
            "p (b s h) -> p b s h", b=STREAMS, s=4)
        krTb = ckv[:, 0:2, :].rearrange("p a c -> p (a c)")
        cqr = lowC[:, 0:TT * Q_LORA].rearrange("p (t c) -> p t c", t=TT)
        qgr = Pb[:, 0, 0:Q_LORA]
        mk = krTb[:, 0:TOK]
        praw = cTb[:, 0, :, 0:TOK]
        kvg = kn[:, 0, 0:KV_LORA + ROPE]
        rq = sq5
        rk = kn

        raw_loaded = [sem(f"raw_loaded{i}") for i in range(4)]
        hi_ready = sem("hi_ready")
        lo_ready = sem("lo_ready")
        blk = sem("blk")
        x_ld = [sem(f"x_ld{i}") for i in range(2)]
        row_std = sem("row_std")
        const_ld = sem("const_ld")
        filled = sem("filled")
        h_new = sem("h_new")
        sq_done = sem("sq_done")
        sq_step = sem("sq_step")
        ms_ready = sem("ms_ready")
        std_ready = sem("std_ready")
        rstd_ready = sem("rstd_ready")
        xh_ready = sem("xh_ready")
        xl_ready = sem("xl_ready")
        gu_evac = sem("gu_evac")
        sg_ready = sem("sg_ready")
        a_ready = sem("a_ready")
        ah_ready = sem("ah_ready")
        al_ready = sem("al_ready")
        dve_chain = sem("dve_chain")
        act_chain = sem("act_chain")
        in_evac = sem("in_evac")
        c0_ready = sem("c0_ready")
        conv_ready = sem("conv_ready")
        conv_done = sem("conv_done")
        z_done = sem("z_done")
        dt_dve = sem("dt_dve")
        dt_act = sem("dt_act")
        dt_ready = sem("dt_ready")
        dtT_ps = sem("dtT_ps")
        dtR_ready = sem("dtR_ready")
        ac_ps = sem("ac_ps")
        acs_ready = sem("acs_ready")
        da_ready = sem("da_ready")
        xt_ps = sem("xt_ps")
        bt_ps = sem("bt_ps")
        xdt_ready = sem("xdt_ready")
        xw_ready = sem("xw_ready")
        brow_ready = sem("brow_ready")
        bm_ready = sem("bm_ready")
        g_ps = sem("g_ps")
        gm_ready = sem("gm_ready")
        running_ps = sem("running_ps")
        decay_diff = sem("decay_diff")
        decay_arg = sem("decay_arg")
        decay_ready = sem("decay_ready")
        decay_cb_ready = sem("decay_cb_ready")
        state_ps = sem("state_ps")
        s1_ready = sem("s1_ready")
        s1_store = sem("s1_store")
        s_ld = sem("s_ld")
        s_store = sem("s_store")
        y_old_ps = sem("y_old_ps")
        s_read = sem("s_read")
        s_dec = sem("s_dec")
        conv_pool = sem("conv_pool")
        yo_ready = sem("yo_ready")
        y_tile_ps = sem("y_tile_ps")
        state_ready = sem("state_ready")
        y_evac = sem("y_evac")
        y_ready = sem("y_ready")
        yh_ready = sem("yh_ready")
        yl_ready = sem("yl_ready")
        y_sq = sem("y_sq")
        f_evac = sem("f_evac")
        y_sum_ps = sem("y_sum_ps")
        y_std = sem("y_std")
        cout_ready = sem("cout_ready")
        p_ld = sem("p_ld")
        ph_ready = sem("ph_ready")
        pl_ready = sem("pl_ready")
        pin_ready = sem("pin_ready")
        pg_evac = sem("pg_evac")
        sgm_ready = sem("sgm_ready")
        kxh_ready = sem("kxh_ready")
        kxl_ready = sem("kxl_ready")
        rt_ps = sem("rt_ps")
        rows_ready = sem("rows_ready")
        kvr_ready = sem("kvr_ready")
        kv_std = sem("kv_std")
        kv_done = sem("kv_done")
        cT_ps = sem("cT_ps")
        cT_ready = sem("cT_ready")
        wk_hi = sem("wk_hi")
        wk_lo = sem("wk_lo")
        past_hi = sem("past_hi")
        past_lo = sem("past_lo")
        past_ps = sem("past_ps")
        past_sq = sem("past_sq")
        past_sum = sem("past_sum")
        past_std = sem("past_std")
        past_rstd = sem("past_rstd")
        wkT_ld = sem("wkT_ld")
        qc_ps = sem("qc_ps")
        qc_ev = sem("qc_ev")
        new_rq = sem("new_rq")
        new_rt = sem("new_rt")
        new_rk = sem("new_rk")
        rq_ready = sem("rq_ready")
        rt_done = sem("rt_done")
        rk_ready = sem("rk_ready")
        s_added = sem("s_added")
        cq_ready = sem("cq_ready")
        cq_std = sem("cq_std")
        cqn_ready = sem("cqn_ready")
        cq_turn_ps = sem("cq_turn_ps")
        cq_hi = sem("cq_hi")
        cq_lo = sem("cq_lo")
        q_sq = sem("q_sq")
        q_sum = sem("q_sum")
        q_std = sem("q_std")
        gq_ready = sem("gq_ready")
        qb_evac = sem("qb_evac")
        q_rows_ready = sem("q_rows_ready")
        q_turn_ps = sem("q_turn_ps")
        q_kept = sem("q_kept")
        w_ld = sem("w_ld")
        ex_ps = sem("ex_ps")
        key_sq = sem("key_sq")
        key_sum = sem("key_sum")
        key_std = sem("key_std")
        key_rows_ready = sem("key_rows_ready")
        key_turn_ps = sem("key_turn_ps")
        key_kept = sem("key_kept")
        vp_ps = sem("vp_ps")
        vp_ev = sem("vp_ev")
        qk_ps = sem("qk_ps")
        p_masked = sem("p_masked")
        p_max_ready = sem("p_max_ready")
        p_exp_ready = sem("p_exp_ready")
        p_ready = sem("p_ready")
        pt_ps = sem("pt_ps")
        pt_ev = sem("pt_ev")
        po_ps = sem("po_ps")
        oh_ready = sem("oh_ready")
        ol_ready = sem("ol_ready")
        c_ld = [sem(f"c_ld{i}") for i in range(2)]
        kr_ld = sem("kr_ld")
        cn_ld = [sem(f"cn_ld{i}") for i in range(2)]
        sc_ps = sem("sc_ps")
        s_max_ready = sem("s_max_ready")
        s_exp_ready = sem("s_exp_ready")
        s_out_ready = sem("s_out_ready")
        s_turn_ps = sem("s_turn_ps")
        s_out_kept = sem("s_out_kept")
        s_head_ps = sem("s_head_ps")
        out_st = sem("out_st")
        mask_ld = sem("mask_ld")

        block = ctx.enter_context(nc.Block())
        MIX, PI, PG, KV, DQ, QB, WO = (BASE[x] for x in ("mix", "pi0", "pg0", "kv", "dq", "qb", "wo"))
        PIN_BANK, PG_BANK = (4, 5, 6, 0, 1, 2, 3, 4), (5, 6, 0, 1)
        KV_BANK = (2, 3, 5)
        ITEMS = 6
        EX_BANK = (0, 1, 4, 5)
        UNITS = 2 * STREAMS
        CRED = SLOTS

        LEAD = 2

        def in_block(g, b):
            return MIX + 1 + 14 * g + b - (4 if g and b < LEAD else 0)

        def out_block(g, b):
            return MIX + 11 + 14 * g + b + (LEAD if g < GROUPS - 1 else 0)

        POOL_TILE = 2

        def convs_of_dve(g, b):
            return 5 * g + b + (1 if b < POOL_TILE else 0)

        def channels(g, b):
            return 4 * g + b if b < 4 else 16 + 4 * (b - 4) + g

        def tiles(t, w=P):
            return slice(t * w, (t + 1) * w)

        def bc(ap, shape, axis):
            return ap.unsqueeze(axis).broadcast_to(shape)

        def samp(t):
            return t[:, SAMP0:XPW].rearrange("p (s t) -> p s t", s=STREAMS)

        @block.sync
        def _(sp):
            sp.dma_start(gains[:, :, :], T["gains"]).then_inc(x_ld[0], 16)
            sp.dma_start(raw[:, 0, :], T["stream"][0]).then_inc(raw_loaded[0], 16)
            for x in range(2):
                sp.dma_start(h[:, 4 * x:4 * x + 4, :], T["x"][:, 4 * x:4 * x + 4, :]).then_inc(x_ld[x], 16)
            for r in range(1, SLOTS):
                sp.dma_start(raw[:, r, :], T["stream"][r]).then_inc(raw_loaded[r], 16)
            with sp.Fori(1, NBLK // SLOTS) as i:
                for r in range(SLOTS):
                    sp.wait_ge(lo_ready, i * SLOTS + (r - SLOTS + 1))
                    sp.dma_start(raw[:, r, :], T["stream"][i * SLOTS + r]).then_inc(raw_loaded[r], 16)

        @block.gpsimd
        def _(pool):
            c = [0]

            def step(ins):
                c[0] += 1
                ins.then_inc(sq_step, 1)
                pool.wait_ge(sq_step, c[0])

            def squares(m):
                acc = sqacc[:, m % 2, :]
                for k in range(KD):
                    pool.wait_ge(h_new, 8 * m + k + 1)
                    if k == 0:
                        step(pool.tensor_tensor(acc, h[:, k, :], h[:, k, :], ALU.mult))
                    else:
                        step(pool.tensor_tensor(sqt[:, :], h[:, k, :], h[:, k, :], ALU.mult))
                        step(pool.tensor_tensor(acc, acc, sqt[:, :], ALU.add))
                if m == 2:
                    pool.wait_ge(s_store, 16 * GROUPS)
                    pool.wait_ge(s1_store, 16 * GROUPS)
                    pool.wait_ge(out_st, 16)
                pool.sem_inc(sq_done, 1)

            pool.memset(ones[:, :], 1.0).then_inc(filled, 1)
            pool.memset(xp[:, :, :], 0.0).then_inc(filled, 1)
            squares(0)
            pool.dma_start(ident[:, :], T["ident"]).then_inc(const_ld, 16)
            for t, name in ((cstate, "cstate"), (cw, "cw"), (dcol, "dcol"), (ang, "ang"), (mask, "mask"),
                            (same, "same"), (ind, "ind"), (dts, "dts")):
                pool.dma_start(t[:], T[name]).then_inc(const_ld, 16)
            squares(1)
            pool.wait_ge(blk, CRED + MIX)
            pool.dma_start(S[:, :, :], T["ssm"][0]).then_inc(s_ld, 16)
            pool.memset(Cm[:, :, :], 0.0).then_inc(filled, 1)
            for g in range(GROUPS):
                pool.wait_ge(c0_ready, 6 * g + POOL_TILE + 1)
                for k in range(1, CONV_W):
                    step(pool.tensor_scalar(yoff[:, 0, 0:CW], xp[:, 0, k:k + CW], cw[:, channels(g, POOL_TILE), k:k + 1], None,
                                            ALU.mult))
                    ins = pool.tensor_tensor(cy[:, 0, 0:CW], cy[:, 0, 0:CW], yoff[:, 0, 0:CW], ALU.add)
                    if k < CONV_W - 1:
                        step(ins)
                    else:
                        ins.then_inc(conv_pool, 1)
                pool.wait_ge(s1_ready, 2 * g + 2)
                pool.dma_start(T["ssm_p"][g], S1[:, :]).then_inc(s1_store, 16)
                for b in range(STREAMS):
                    sv = S[:, b, :].rearrange("p (h d) -> p h d", h=HPG)
                    pool.wait_ge(s_read, 8 * g + b + 1)
                    pool.tensor_tensor(sv, sv, bc(dec[:, b, HPG * g:HPG * g + HPG], (P, HPG, HD), 2),
                                       ALU.mult).then_inc(s_dec, 1)
                pool.wait_ge(state_ready, 8 * g + 8)
                pool.dma_start(T["ssm_s"][g], S[:, :, :]).then_inc(s_store, 16)
                for i in range(4):
                    pool.wait_ge(y_ready, 4 * g + i + 1)
                    if g == 0 and i == 0:
                        step(pool.tensor_tensor(sqacc[:, 0, :], zs[:, i, :], zs[:, i, :], ALU.mult))
                    else:
                        step(pool.tensor_tensor(sqt[:, :], zs[:, i, :], zs[:, i, :], ALU.mult))
                        step(pool.tensor_tensor(sqacc[:, 0, :], sqacc[:, 0, :], sqt[:, :], ALU.add))
                    pool.sem_inc(y_sq, 1)
                if g < GROUPS - 1:
                    pool.wait_ge(s_store, 16 * (g + 1))
                    pool.dma_start(S[:, :, :], T["ssm"][g + 1]).then_inc(s_ld, 16)
            pool.wait_ge(cout_ready, KC)
            pool.dma_start(T["conv"], cout[:, :, :]).then_inc(out_st, 16)
            squares(2)
            pool.dma_start(praw, T["p"][0]).then_inc(p_ld, 16)
            pool.dma_start(kvg, T["kvg"]).then_inc(p_ld, 16)
            pool.dma_start(cosr[:], T["cos"]).then_inc(p_ld, 16)
            pool.dma_start(sinr[:], T["sin"]).then_inc(p_ld, 16)
            pool.memset(krow[:, :, :], 0.0).then_inc(filled, 1)
            squares(3)
            squares(4)
            pool.wait_ge(kv_done, TT)
            pool.dma_start(T["kvl"], ckv[:, :, :]).then_inc(out_st, 16)
            pool.dma_start(T["kr"], krow[:, :, NOPE:QD]).then_inc(out_st, 16)
            squares(5)
            pool.wait_ge(blk, CRED + DQ)
            pool.dma_start(qgr, T["qgr"]).then_inc(w_ld, 16)
            pool.dma_start(gr[:], T["gr"]).then_inc(w_ld, 16)
            pool.dma_start(gq[:, 0:2], T["gq"]).then_inc(w_ld, 16)
            pool.dma_start(wk[:], T["wk"]).then_inc(w_ld, 16)
            pool.dma_start(wv[:], T["wv"]).then_inc(w_ld, 16)
            pool.wait_ge(gq_ready, 2)
            for e in range(4 * TT):
                t, H2, x, qr = e % TT, ROPE // 2, q_rope(e), q_rows(e)[:, :, NOPE:QD]
                xs_ = q_sin
                pool.wait_ge(qb_evac, e + 1)
                if e:
                    pool.wait_ge(q_rows_ready, e)
                pool.tensor_tensor(xs_, x, bc(sinr[:, t, :], (P, 4, ROPE), 1), ALU.mult)
                step(pool.tensor_tensor(qr, x, bc(cosr[:, t, :], (P, 4, ROPE), 1), ALU.mult))
                pool.tensor_tensor(qr[:, :, 0:H2], qr[:, :, 0:H2], xs_[:, :, H2:ROPE], ALU.subtract)
                pool.tensor_tensor(qr[:, :, H2:ROPE], qr[:, :, H2:ROPE], xs_[:, :, 0:H2], ALU.add).then_inc(q_rows_ready, 1)
            pool.wait_ge(out_st, 16 * 3)
            pool.wait_ge(cT_ready, 1)
            pool.dma_start(mk, T["mk"]).then_inc(mask_ld, 16)
            for b in range(STREAMS):
                if b >= 2:
                    pool.wait_ge(past_ps, 8 * (b - 1))
                pool.dma_start(cTb[:, b % 2, :, :], T["cacheT"][b]).then_inc(c_ld[b % 2], 16)
            for x in range(0, MH, MH // 4):
                pool.wait_ge(qk_ps, x + MH // 4)
                pool.dma_start(wkT[0:QD, x:x + MH // 4], T["wkT"][:, x:x + MH // 4]).then_inc(wkT_ld, 16)

            def past_latent(b):
                if b < 2:
                    pool.wait_ge(past_ps, 8 * (STREAMS - 1 + b))
                else:
                    pool.wait_ge(sc_ps, 2 * (b - 1))
                pool.dma_start(cTb[:, b % 2, :, :], T["cacheT"][b]).then_inc(c_ld[b % 2], 16)
                if b < 2:
                    pool.wait_ge(po_ps, MH)
                else:
                    pool.wait_ge(po_ps, MH + 2 * (b - 1))
                pool.dma_start(cnat[:, b % 2], T["cache"][b]).then_inc(cn_ld[b % 2], 16)

            def past_rope(b):
                if b == 0:
                    pool.wait_ge(p_masked, MH)
                    pool.memset(krTb[:, :], 0.0).then_inc(filled, 1)
                    pool.wait_ge(filled, 5)
                else:
                    pool.wait_ge(sc_ps, 2 * b)
                pool.dma_start(krTb[NOPE:QD], T["krcT"][b]).then_inc(kr_ld, 16)

            past_latent(0)
            past_rope(0)
            pool.wait_ge(key_rows_ready, ITEMS)
            for g in range(2):
                pool.tensor_copy(rq[:, 0, tiles(g)].rearrange("p (h q) -> p h q", h=8),
                                 bc(rsn[:, 8 * g:8 * g + 8], (P, 8, STEPS), 2)).then_inc(new_rq, 1)
            pool.wait_ge(past_rstd, 1)
            for u in range(UNITS):
                b, g = divmod(u, 2)
                if u == 0:
                    pool.wait_ge(new_rt, 1)
                if u >= 2:
                    pool.wait_ge(rt_done, u - 1)
                for st in range(4):
                    ins = pool.tensor_copy(rq[:, u % 2, tiles(st)].rearrange("p (h q) -> p h q", h=8),
                                           bc(ksq[:, b, st, 8 * g:8 * g + 8], (P, 8, STEPS), 2))
                ins.then_inc(rq_ready, 1)
                if b + 1 < STREAMS:
                    if g == 0:
                        past_latent(b + 1)
                    else:
                        past_rope(b + 1)
            pool.wait_ge(cn_ld[1], 16 * 4)
            squares(6)
            pool.dma_start(praw, T["p"][1]).then_inc(p_ld, 16)
            squares(7)
            for k in range(KD):
                pool.wait_ge(h_new, 8 * NORMS + k + 1)
                pool.dma_start(T["y"][:, k, :], h[:, k, :]).then_inc(out_st, 16)
            pool.wait_ge(out_st, 16 * (3 + KD))

        @block.scalar
        def _(act):
            A = nc.scalar.activation
            c = [0]

            def step(ins):
                c[0] += 1
                ins.then_inc(act_chain, 1)
                act.wait_ge(act_chain, c[0])

            def hi_split(n, i=0):
                if n >= NBLK:
                    return
                r = n % SLOTS
                act.wait_ge(raw_loaded[r], i * 16 + 16 * (n // SLOTS + 1))
                act.wait_ge(blk, i * SLOTS + (n + 1))
                w = WIDTH[n]
                A(whi[:, r, 0:w], raw[:, r, 0:w], ACT.Copy).then_inc(hi_ready, 1)

            def norm_std(m):
                act.wait_ge(ms_ready, m + (m < 5))
                A(std[:, :], bank[7][:, 0:TOK], ACT.Sqrt, bias=EPS, scale=1.0 / D_MODEL).then_inc(std_ready, 1)

            def x_hi(m, k):
                act.wait_ge(h_new, 8 * m + k + 1)
                A(xh[:, k, :], h[:, k, :], ACT.Copy, scale=gains[:, m, k:k + 1]).then_inc(xh_ready, 1)

            def gate_up(u, m=None):
                base = BASE[f"gu{u}"]

                def pair(i, n0, last=False):
                    for j in range(2):
                        n, fs = base + n0 + 2 * j, KF * u + n0 // 2 + j
                        hi_split(n + 4, i)
                        act.wait_ge(gu_evac, i * 2 + (2 + fs + 1))
                        A(tg[:, j, :], tg[:, j, :], ACT.Silu).then_inc(sg_ready, 1)
                        if j == 0 or not last:
                            hi_split(n + 5, i)
                        act.wait_ge(a_ready, i * 2 + (fs + 1))
                        A(ah[:, i * 2 + (n0 // 2 + j), :], tu[:, j, :], ACT.Copy).then_inc(ah_ready, 1)
                hi_split(base + 3)
                if m is not None:
                    norm_std(m)
                act.preload_act_table(ACT.Silu)
                with act.Fori(0, KF // 2 - 1) as i:
                    pair(i, 0)
                pair(0, 2 * KF - 4, True)

            def down(u, m):
                for j in range(KD):
                    if u % 2 and j == KD - 2:
                        act.wait_ge(p_ld, 16 * (4 + u // 2))
                        A(phi[:, :, :], praw, ACT.Copy).then_inc(ph_ready, 1)
                    for b in range(3):
                        hi_split(BASE[f"dn{u}"] + 3 * j + b + 3)
                    x_hi(m, j)

            def kx_hi(k):
                act.wait_ge(h_new, 32 + k + 1)
                A(kxh[:, k, :], h[:, k, :], ACT.Copy, scale=gains[:, NORMS, k:k + 1]).then_inc(kxh_ready, 1)

            def ple_act(l, m):
                for i in range(2):
                    n = BASE[f"pi{l}"] + i
                    hi_split(n + 3)
                    act.wait_ge(blk, CRED + n + 1)
                    if i:
                        norm_std(m)
                    for jj in range(4):
                        A(pin[:, 4 * i + jj, :], bank[PIN_BANK[4 * i + jj]][:, 0:TOK], ACT.Copy).then_inc(pin_ready, 1)
                for j in range(KD):
                    n = BASE[f"pg{l}"] + j
                    hi_split(n + 3)
                    act.wait_ge(pg_evac, 8 * l + j + 1)
                    A(tp[:, j % 2, :], tp[:, j % 2, :], ACT.Sigmoid).then_inc(sgm_ready, 1)
                    if l == 0 and j:
                        kx_hi(j - 1)

            for r in range(AHEAD):
                act.wait_ge(raw_loaded[r], 16)
                A(whi[:, r, 0:WIDTH[r]], raw[:, r, 0:WIDTH[r]], ACT.Copy).then_inc(hi_ready, 1)
                if r == 0:
                    act.wait_ge(x_ld[0], 32)
                    for k in range(KD):
                        x_hi(0, k)
            gate_up(0, 0)
            down(0, 1)
            act.wait_ge(const_ld, 144)

            norm_std(1)
            hi_split(MIX + 3)

            def silu(g, b):
                s = b % 2
                if b == POOL_TILE:
                    act.wait_ge(conv_pool, g + 1)
                else:
                    act.wait_ge(conv_ready, convs_of_dve(g, b))
                dst = xsT[:, b, :] if b < 4 else BC[:, b - 4, :]
                A(dst[:, 0:SEQ], cy[:, s, 0:SEQ], ACT.Silu)
                A(dst[:, SEQ:TOK].rearrange("p (s t) -> p s t", t=STEPS), samp(cy[:, s, :])[:, :, 0:STEPS],
                  ACT.Silu).then_inc(conv_done, 1)

            def in_proj(g, b):
                s = b % 2
                hi_split(in_block(g, b) + 3)
                if b < 6:
                    ch = channels(g, b)
                    step(A(samp(xp[:, s, :])[:, :, 0:3], cstate[:, ch, :].rearrange("p (s t) -> p s t", t=3), ACT.Copy))
                    act.wait_ge(in_evac, 10 * g + b + 1)
                    A(cy[:, s, 0:CW], xp[:, s, 0:CW], ACT.Identity, bias=cw[:, ch, CONV_W:CONV_W + 1],
                      scale=cw[:, ch, 0:1]).then_inc(c0_ready, 1)
                    A(cout[:, ch, 0:3], xp[:, s, SEQ:SEQ + 3], ACT.Copy)
                    A(cout[:, ch, 3:27].rearrange("p (s t) -> p s t", t=3), samp(xp[:, s, :])[:, :, STEPS:STEPS + 3],
                      ACT.Copy).then_inc(cout_ready, 1)
                if 1 <= b <= 6:
                    silu(g, b - 1)
                if b >= 6:
                    act.wait_ge(in_evac, 10 * g + b + 1)
                    A(zs[:, b - 6, :], zs[:, b - 6, :], ACT.Silu).then_inc(z_done, 1)

            for g in range(GROUPS):
                for b in range(LEAD if g else 0, 10):
                    if g == 0 and b == 0:
                        act.wait_ge(dt_dve, 1)
                        step(A(dv[2], dv[1], ACT.Abs))
                        A(dts[:, 1:2], dts[:, 1:2], ACT.Exp)
                        A(dv[3], dv[2], ACT.Exp, scale=-1.0).then_inc(dt_act, 1)
                    in_proj(g, b)
                    if g == 0 and b == 1:
                        act.wait_ge(dt_dve, 2)
                        A(dv[5], dv[4], ACT.Ln).then_inc(dt_act, 1)
                    if g == 0 and b == 6:
                        act.wait_ge(acs_ready, 1)
                        A(toend[:], toend[:], ACT.Exp)
                        A(eacs[:], acs[:], ACT.Exp)
                        A(dec[:, 0:STREAMS, :], bank[5][:, 0:STREAMS * HEADS].rearrange("p (s h) -> p s h", h=HEADS), ACT.Exp)
                        A(dec[:, STREAMS, :], bank[6][:, 128:160], ACT.Exp).then_inc(da_ready, 1)
                for t in range(TT):
                    q = 3 * g + t
                    act.wait_ge(decay_arg, q + 1)
                    A(seg[:, q % 2, :], seg[:, q % 2, :], ACT.Exp).then_inc(decay_ready, 1)
                for i in range(4):
                    act.wait_ge(y_ready, 4 * g + i + 1)
                    A(yh[:, i, :], zs[:, i, :], ACT.Copy, scale=ang[:, 4 * g + i:4 * g + i + 1]).then_inc(yh_ready, 1)
                if g + 1 < GROUPS:
                    for b in range(LEAD):
                        in_proj(g + 1, b)
                for b in range(4):
                    if g == GROUPS - 1 and b == 2:
                        act.wait_ge(y_sum_ps, 1)
                        A(std[:, :], bank[0][:, 0:TOK], ACT.Sqrt, bias=EPS, scale=1.0 / D_INNER).then_inc(y_std, 1)
                    hi_split(out_block(g, b) + 3)
            for k in range(KD):
                x_hi(2, k)
            gate_up(1, 2)
            down(1, 3)
            ple_act(0, 3)

            kx_hi(KD - 1)
            for b in range(3):
                hi_split(KV + b + 3)

            def token_std(m, x):
                act.wait_ge(rt_ps, x + 1)
                A(rows[:, x, :], bank[4][:, 0:TT], ACT.Sqrt, bias=EPS, scale=1.0 / D_MODEL).then_inc(row_std, 1)

            token_std(4, 0)
            norm_std(4)
            act.wait_ge(blk, CRED + PG + KD)
            for k in range(KD):
                x_hi(4, k)
            for t in range(TT):
                act.wait_ge(kvr_ready, t + 1)
                A(sq5[:, 0, 0:256], kvr[:, t, 0:256], ACT.Square, accum_out=rsc[:, t, 0:1])
                step(A(sq5[:, 0, 256:288], kvr[:, t, 256:288], ACT.Square, accum_out=rsc[:, t, 1:2]))
                A(rsc[:, t, 2:3], rsc[:, t, 0:1], ACT.Sqrt, bias=EPS, scale=1.0 / KV_LORA)
                A(rsc[:, t, 3:4], rsc[:, t, 1:2], ACT.Sqrt, bias=EPS, scale=1.0 / ROPE).then_inc(kv_std, 1)
            gate_up(2)
            act.wait_ge(cT_ps, 1)
            for k in range(2):
                A(cT[:, k, :], bank[5 + k][:, 0:TOK], ACT.Copy)
            A(krT[0:QD, :], bank[4][0:QD, 0:TOK], ACT.Copy).then_inc(cT_ready, 1)
            down(2, 5)

            for b in range(4):
                hi_split(DQ + b + 3)
            token_std(5, 1)
            for t in range(TT):
                act.wait_ge(cq_ready, t + 1)
                step(A(sq5[:, 0, :], cqr[:, t, :], ACT.Square, accum_out=rsc[:, t, 0:1]))
                A(rsc[:, t, 2:3], rsc[:, t, 0:1], ACT.Sqrt, bias=EPS, scale=1.0 / Q_LORA).then_inc(cq_std, 1)
            act.wait_ge(cq_turn_ps, 1)
            for k in range(4):
                A(xh[:, k, :], bank[4 + k][:, 0:TOK], ACT.Copy).then_inc(cq_hi, 1)

            def q_square(e):
                cg, t = divmod(e, TT)
                act.wait_ge(blk, CRED + QB + 2 * cg + 2)
                if e >= 2:
                    act.wait_ge(q_sum, e - 1)
                A(sq5[:, e % 2, 0:384], bank[3 * (cg % 2) + t][:, 0:384], ACT.Square).then_inc(q_sq, 1)

            def q_evac(e):
                cg, t = divmod(e, TT)
                act.wait_ge(q_turn_ps, e + 1)
                src = bank[6 + e % 2][0:QD, :].rearrange("p (h t) -> p h t", h=4)
                if t < 2:
                    A(Qp[0:QD, 4 * cg:4 * cg + 4, tiles(t)], src, ACT.Copy, scale=gq[0:QD, 2:3]).then_inc(q_kept, 1)
                else:
                    A(Qs[0:QD, :, 4 * cg:4 * cg + 4, :],
                      bank[6 + e % 2][0:QD, :].rearrange("p (h b q) -> p b h q", h=4, q=STEPS),
                      ACT.Copy, scale=gq[0:QD, 2:3]).then_inc(q_kept, 1)
            act.wait_ge(gq_ready, 1)
            for cg in range(4):
                for b in range(2):
                    hi_split(QB + 2 * cg + b + 3)
                for t in range(TT):
                    e = 3 * cg + t
                    if e == 0:
                        q_square(0)
                    if t < 2:
                        q_square(e + 1)
                    o = 24 * (e % 2)
                    act.wait_ge(q_sum, e + 1)
                    A(sm[:, o + 8:o + 12], sm[:, o:o + 4], ACT.Sqrt, bias=EPS, scale=1.0 / NOPE)
                    A(sm[:, o + 12:o + 16], sm[:, o + 4:o + 8], ACT.Sqrt, bias=EPS, scale=1.0 / ROPE).then_inc(q_std, 1)
                    if e >= 3:
                        q_evac(e - 3)
                    if t == 2 and e + 1 < 12:
                        q_square(e + 1)
            for e in range(9, 12):
                q_evac(e)

            def key_square(w):
                act.wait_ge(ex_ps, w + 1)
                act.wait_ge(q_sum, 12)
                if w >= 2:
                    act.wait_ge(key_sum, w - 1)
                A(sq5[:, w % 2, :], bank[EX_BANK[w % 4]][:, :], ACT.Square).then_inc(key_sq, 1)

            def key_evac(w):
                t, g = divmod(w, 2)
                act.wait_ge(key_turn_ps, w + 1)
                for x in range(2):
                    last = A(Kp[0:QD, 8 * g + 4 * x:8 * g + 4 * x + 4, tiles(t)],
                             bank[2 + x][0:QD, :].rearrange("p (h t) -> p h t", h=4), ACT.Copy)
                last.then_inc(key_kept, 1)

            key_square(0)
            for w in range(ITEMS):
                if w + 1 < ITEMS:
                    key_square(w + 1)
                o = 48 + 24 * (w % 2)
                act.wait_ge(key_sum, w + 1)
                A(sm[:, o + 8:o + 16], sm[:, o:o + 8], ACT.Sqrt, bias=EPS, scale=1.0 / NOPE).then_inc(key_std, 1)
                if 1 <= w <= 4:
                    key_evac(w - 1)
            act.wait_ge(w_ld, 16 * 5)
            for k in range(2):
                A(wkh[:, k, :], wk[:, k, :], ACT.Copy).then_inc(wk_hi, 1)
            for v in range(4):
                act.wait_ge(vp_ps, v + 1)
                A(Vp[:, v // 2, 512 * (v % 2):512 * (v % 2) + 512], bank[4 + v][:, :], ACT.Copy).then_inc(vp_ev, 1)

            def past_split(b):
                act.wait_ge(c_ld[b % 2], 16 * (b // 2 + 1))
                A(cTh[:, b % 2], cTb[:, b % 2], ACT.Copy).then_inc(past_hi, 1)

            def past_square(w):
                act.wait_ge(past_ps, w + 1)
                if w < 2:
                    act.wait_ge(key_turn_ps, 4)
                else:
                    act.wait_ge(past_sum, w - 1)
                A(kn[:, w % 2, 0:512], bank[w % 2][:, :], ACT.Square).then_inc(past_sq, 1)

            def p_exp(x):
                s, o = x % 2, 48 + 8 * (x % 2)
                act.wait_ge(p_max_ready, x + 1)
                A(Pb[:, s, 0:128], Pb[:, s, 0:128], ACT.Exp, bias=sm[:, o + 2:o + 3], scale=SCALE, accum_out=sm[:, o + 4:o + 5])
                A(Pb[:, s, 128:384], Pb[:, s, 128:384], ACT.Exp, bias=sm[:, o + 3:o + 4], scale=SCALE,
                  accum_out=sm[:, o + 5:o + 6]).then_inc(p_exp_ready, 1)

            past_split(0)
            past_split(1)
            p_exp(0)
            for x in range(MH):
                if x + 1 < MH:
                    p_exp(x + 1)
                past_square(4 * x)
                past_square(4 * x + 1)
                act.wait_ge(pt_ps, x + 1)
                A(PT[:, 0:384], bank[6][:, 0:384], ACT.Copy).then_inc(pt_ev, 1)
                if x % 2 and 2 <= x // 2 + 1 < STREAMS:
                    past_split(x // 2 + 1)
                past_square(4 * x + 2)
                past_square(4 * x + 3)
                if x % 2:
                    act.wait_ge(po_ps, x + 1)
                    A(xh[:, x // 2, 0:SEQ], bank[7 if x // 2 % 2 else 3][:, 0:SEQ], ACT.Copy).then_inc(oh_ready, 1)

            act.wait_ge(past_sum, 8 * STREAMS)
            A(ksq[:], ksq[:], ACT.Sqrt, bias=EPS, scale=1.0 / NOPE).then_inc(past_std, 1)
            for j in range(8):
                act.wait_ge(qc_ps, j + 1)
                for k in range(2):
                    ins = A(QC[:, k, :, 2 * j:2 * j + 2, :],
                            bank[j % 4][:, tiles(k, 2 * P)].rearrange("p (h b q) -> p b h q", h=2, b=STREAMS), ACT.Copy)
                ins.then_inc(qc_ev, 1)
            act.wait_ge(new_rt, 1)
            A(rbn[:, :, :], bank[4][:, 0:2 * P].rearrange("p (g t) -> p g t", g=2), ACT.Copy).then_inc(new_rk, 1)

            def s_rstd(u):
                act.wait_ge(rt_done, u + 1)
                if u >= 2:
                    act.wait_ge(s_added, u - 1)
                A(rk[:, u % 2, 0:512], bank[3][:, :], ACT.Copy).then_inc(rk_ready, 1)

            def s_exp(u):
                b = u // 2
                act.wait_ge(s_max_ready, u + 1)
                s, o = u % 2, 64 + 8 * (u % 2)
                A(Pb[:, s, 0:PAST], Pb[:, s, 0:PAST], ACT.Exp, bias=sm[:, o + 2:o + 3], scale=SCALE, accum_out=sm[:, o + 4:o + 5])
                new = Pb[:, s, PAST + 16 * b:PAST + 16 * b + 16]
                A(new, new, ACT.Exp, bias=sm[:, o + 2:o + 3], scale=SCALE, accum_out=sm[:, o + 5:o + 6]).then_inc(s_exp_ready, 1)

            s_rstd(0)
            s_exp(0)
            for u in range(UNITS):
                act.wait_ge(pt_ps, MH + u + 1)
                A(PT[:, 0:512], bank[6][:, :], ACT.Copy)
                A(PT[:, 512:640], bank[0][:, 0:P], ACT.Copy).then_inc(pt_ev, 1)
                if u + 1 < UNITS:
                    s_rstd(u + 1)
                    s_exp(u + 1)
            for x in range(MH // 2):
                act.wait_ge(s_head_ps, x + 1)
                A(xh[:, x, SEQ:TOK], bank[x % 2][:, 0:P], ACT.Copy).then_inc(oh_ready, 1)
            for b in range(8):
                hi_split(WO + b + 3)
            act.wait_ge(blk, CRED + WO + 8)
            for k in range(KD):
                x_hi(6, k)
            gate_up(3, 6)
            down(3, 7)
            ple_act(1, 7)

        @block.vector
        def _(dve):
            V = nc.vector
            c = [0]

            def step(ins):
                c[0] += 1
                ins.then_inc(dve_chain, 1)
                dve.wait_ge(dve_chain, c[0])

            def lo_split(n, i=0):
                if n >= NBLK:
                    return
                r, w = n % SLOTS, WIDTH[n]
                dve.wait_ge(hi_ready, i * SLOTS + (n + 1))
                V.tensor_tensor(wlo[:, r, 0:w], raw[:, r, 0:w], whi[:, r, 0:w].bitcast(F32),
                                ALU.subtract).then_inc(lo_ready, 1)

            def norm_rstd(m):
                dve.wait_ge(std_ready, m + (m < 5))
                V.reciprocal(rstd[:, m % 2, :], std[:, :]).then_inc(rstd_ready, 1)
                dve.wait_ge(rstd_ready, m + (m < 5))

            def x_lo(m, k):
                dve.wait_ge(xh_ready, 8 * m + k + 1)
                V.scalar_tensor_tensor(out=xl[:, k, :], in0=h[:, k, :], scalar=gains[:, m, k:k + 1],
                                       in1=xh[:, k, :].bitcast(F32), op0=ALU.mult, op1=ALU.subtract).then_inc(xl_ready, 1)

            def gate_up(u, m):
                base, r = BASE[f"gu{u}"], rstd[:, m % 2, :]

                def pair(i, n0, last=False):
                    for j in range(2):
                        n, fs = base + n0 + 2 * j, KF * u + n0 // 2 + j
                        dve.wait_ge(blk, i * SLOTS + (CRED + n + 2))
                        V.tensor_tensor(tg[:, j, :], bank[2 * j][:, 0:TOK], r, ALU.mult)
                        V.tensor_tensor(tu[:, j, :], bank[2 * j + 1][:, 0:TOK], r, ALU.mult).then_inc(gu_evac, 1)
                        lo_split(n + 4, i)
                        dve.wait_ge(sg_ready, i * 2 + (fs + 1))
                        V.tensor_tensor(tu[:, j, :], tg[:, j, :], tu[:, j, :], ALU.mult).then_inc(a_ready, 1)
                        if j == 0 or not last:
                            lo_split(n + 5, i)
                        dve.wait_ge(ah_ready, i * 2 + (fs + 1))
                        f = i * 2 + (n0 // 2 + j)
                        V.tensor_tensor(al[:, f, :], tu[:, j, :], ah[:, f, :].bitcast(F32), ALU.subtract).then_inc(al_ready, 1)
                lo_split(base + 3)
                if m != 4:
                    norm_rstd(m)
                with dve.Fori(0, KF // 2 - 1) as i:
                    pair(i, 0)
                pair(0, 2 * KF - 4, True)

            def down(u, m):
                for j in range(KD):
                    n = BASE[f"dn{u}"] + 3 * j
                    if u % 2 and j == KD - 2:
                        dve.wait_ge(ph_ready, u // 2 + 1)
                        V.tensor_tensor(plo[:, :, :], praw, phi[:, :, :].bitcast(F32), ALU.subtract).then_inc(pl_ready, 1)
                    for b in range(3):
                        lo_split(n + b + 3)
                    dve.wait_ge(blk, CRED + n + 3)
                    V.scalar_tensor_tensor(out=h[:, j, :], in0=bank[j % 4][:, 0:TOK], scalar=0.5, in1=h[:, j, :],
                                           op0=ALU.mult, op1=ALU.add).then_inc(h_new, 1)
                    x_lo(m, j)

            def kx_lo(k):
                dve.wait_ge(kxh_ready, k + 1)
                V.scalar_tensor_tensor(out=kxl[:, k, :], in0=h[:, k, :], scalar=gains[:, NORMS, k:k + 1],
                                       in1=kxh[:, k, :].bitcast(F32), op0=ALU.mult, op1=ALU.subtract).then_inc(kxl_ready, 1)

            def ple_dve(l, m):
                for i in range(2):
                    lo_split(BASE[f"pi{l}"] + i + 3)
                norm_rstd(m)
                for j in range(KD):
                    n = BASE[f"pg{l}"] + j
                    lo_split(n + 3)
                    dve.wait_ge(blk, CRED + n + 1)
                    V.tensor_tensor(tp[:, j % 2, :], bank[PG_BANK[j % 4]][:, 0:TOK], rstd[:, m % 2, :], ALU.mult).then_inc(pg_evac, 1)
                    dve.wait_ge(sgm_ready, 8 * l + j + 1)
                    dve.wait_ge(pin_ready, 8 * l + 8)
                    step(V.tensor_tensor(tp[:, j % 2, :], tp[:, j % 2, :], pin[:, j, :], ALU.mult))
                    V.tensor_tensor(h[:, j, :], h[:, j, :], tp[:, j % 2, :], ALU.add).then_inc(h_new, 1)
                    if l == 0 and j:
                        kx_lo(j - 1)

            dve.sem_inc(gu_evac, 2)
            dve.sem_inc(blk, CRED)
            dve.wait_ge(x_ld[0], 32)
            dve.sem_inc(h_new, KD // 2)
            lo_split(0)
            for k in range(KD // 2):
                x_lo(0, k)
            dve.wait_ge(x_ld[1], 16)
            dve.sem_inc(h_new, KD // 2)
            for k in range(KD // 2, KD):
                x_lo(0, k)
            for r in range(1, AHEAD):
                lo_split(r)
            gate_up(0, 0)
            down(0, 1)
            dve.wait_ge(const_ld, 144)

            norm_rstd(1)
            r = rstd[:, 1, :]
            lo_split(MIX + 3)
            dve.wait_ge(filled, 2)

            def in_proj(g, b):
                n, s = in_block(g, b), b % 2
                dve.wait_ge(blk, CRED + n + 1)
                src = bank[b % 4]
                if b < 6:
                    ch = channels(g, b)
                    if b == POOL_TILE + 2:
                        dve.wait_ge(conv_pool, g + 1)
                    elif b >= 2:
                        dve.wait_ge(conv_ready, convs_of_dve(g, b - 2))
                    elif g:
                        dve.wait_ge(conv_ready, convs_of_dve(g - 1, b + 4))
                    V.tensor_tensor(xp[:, s, 3:3 + SEQ], src[:, 0:SEQ], r[:, 0:SEQ], ALU.mult)
                    V.tensor_tensor(samp(xp[:, s, :])[:, :, 3:3 + STEPS],
                                    src[:, SEQ:TOK].rearrange("p (s t) -> p s t", t=STEPS),
                                    r[:, SEQ:TOK].rearrange("p (s t) -> p s t", t=STEPS), ALU.mult).then_inc(in_evac, 1)
                    lo_split(n + 3)
                    if b != POOL_TILE:
                        dve.wait_ge(c0_ready, 6 * g + b + 1)
                        for k in range(1, CONV_W):
                            ins = V.scalar_tensor_tensor(out=cy[:, s, 0:CW], in0=xp[:, s, k:k + CW], scalar=cw[:, ch, k:k + 1],
                                                         in1=cy[:, s, 0:CW], op0=ALU.mult, op1=ALU.add)
                            if k < CONV_W - 1:
                                step(ins)
                            else:
                                ins.then_inc(conv_ready, 1)
                else:
                    if g:
                        dve.wait_ge(y_sq, 4 * g)
                    V.tensor_tensor(zs[:, b - 6, :], src[:, 0:TOK], r, ALU.mult).then_inc(in_evac, 1)
                    lo_split(n + 3)

            def dt_step(i):
                if i < 0:
                    step(V.tensor_tensor(dv[0], bank[4][0:HEADS, 0:TOK], r[0:HEADS, :], ALU.mult))
                    V.tensor_scalar(dv[1], dv[0], dts[:, 0:1], None, ALU.add).then_inc(dt_dve, 1)
                if i == 0:
                    dve.wait_ge(dt_act, 1)
                    V.tensor_scalar(dv[4], dv[3], 1.0, None, ALU.add).then_inc(dt_dve, 1)
                    dve.wait_ge(dt_dve, 2)
                    step(V.reciprocal(dv[6], dv[4]))
                if i == 2:
                    step(V.tensor_scalar(dv[0], dv[4], -1.0, None, ALU.add))
                    step(V.tensor_tensor(dv[0], dv[3], dv[0], ALU.subtract))
                    step(V.tensor_tensor(dv[0], dv[0], dv[6], ALU.mult))
                    dve.wait_ge(dt_act, 2)
                    step(V.tensor_scalar(dv[2], dv[1], 0.0, None, ALU.max))
                    step(V.tensor_tensor(dv[2], dv[2], dv[5], ALU.add))
                    step(V.tensor_tensor(dv[2], dv[2], dv[0], ALU.add))
                    V.tensor_scalar(dv[1], dv[2], dts[:, 1:2], -1.0, ALU.mult, ALU.mult).then_inc(dt_ready, 1)
                if i == 4:
                    dve.wait_ge(dtT_ps, 1)
                    V.tensor_copy(dtR[:, :, :], bank[5][:, 0:96].rearrange("p (t h) -> p t h", t=TT))
                    step(V.tensor_copy(aR[:, :, :], bank[5][:, 96:192].rearrange("p (t h) -> p t h", t=TT)))
                    V.tensor_tensor(am, bc(aR[:, 2, :], (P, STREAMS, HEADS), 1), bc(ind[:, :], (P, STREAMS, HEADS), 2),
                                    ALU.mult).then_inc(dtR_ready, 1)
                if i == 6:
                    dve.wait_ge(ac_ps, 1)
                    step(V.tensor_copy(acs[:, :, :], bank[6][:, 0:96].rearrange("p (t h) -> p t h", t=TT)))
                    V.tensor_tensor(toend[:, :, :], bank[6][:, 96:192].rearrange("p (t h) -> p t h", t=TT), acs[:, :, :],
                                    ALU.subtract).then_inc(acs_ready, 1)

            def b_rows(g):
                dve.wait_ge(bt_ps, g + 1)
                V.tensor_copy(Brow[:, :, :], bank[7][:, 0:TOK].rearrange("p (t n) -> p t n", t=TT)).then_inc(brow_ready, 1)
                dve.wait_ge(brow_ready, g + 1)
                V.tensor_tensor(Bm[:, :, :], bc(Brow[:, 2, :], (P, STREAMS, P), 1), bc(ind[:, :], (P, STREAMS, P), 2), ALU.mult)
                dve.wait_ge(filled, 3)
                V.tensor_copy(bass.AP(Cm, 0, [[STREAMS * P, P], [P + STEPS, STREAMS], [1, STEPS]]),
                              BC[:, 1, SEQ:TOK].rearrange("p (s t) -> p s t", t=STEPS)).then_inc(bm_ready, 1)

            def x_rows(g, t):
                hd, hs = (P, HPG, HD), slice(HPG * g, HPG * g + HPG)
                dve.wait_ge(xt_ps, 3 * g + t + 1)
                v3 = xdt[:, t, :].rearrange("p (h d) -> p h d", h=HPG)
                V.tensor_tensor(v3, bank[4 + t][:, :].rearrange("p (h d) -> p h d", h=HPG), bc(dtR[:, t, hs], hd, 2),
                                ALU.mult).then_inc(xdt_ready, 1)
                dve.wait_ge(xdt_ready, 3 * g + t + 1)
                V.tensor_tensor(xw[:, t, :].rearrange("p (h d) -> p h d", h=HPG), v3, bc(toend[:, t, hs], hd, 2),
                                ALU.mult).then_inc(xw_ready, 1)

            dt_step(-1)
            for g in range(GROUPS):
                hs = slice(HPG * g, HPG * g + HPG)
                hd = (P, HPG, HD)
                for b in range(LEAD if g else 0, 10):
                    in_proj(g, b)
                    if g == 0:
                        dt_step(b)
                    if b == 7:
                        b_rows(g)
                        if g == 0:
                            dve.wait_ge(da_ready, 1)
                        x_rows(g, 0)
                    if b == 8:
                        x_rows(g, 1)
                        x_rows(g, 2)
                dve.wait_ge(g_ps, g + 1)
                V.tensor_tensor(Gm[:, :], bank[7][:, 0:TOK], mask[:, :, :].rearrange("p t l -> p (t l)"),
                                ALU.mult).then_inc(gm_ready, 1)

                def decay(t):
                    q, s = 3 * g + t, (3 * g + t) % 2
                    dve.wait_ge(running_ps, q + 1)
                    if q >= 2:
                        dve.wait_ge(y_tile_ps, q - 1)
                    for x in range(2):
                        ins = V.tensor_tensor(seg[:, s, 512 * x:512 * x + 512].rearrange("p (h l) -> p h l", h=4),
                                              bank[4 + x][:, :].rearrange("p (h l) -> p h l", h=4),
                                              bc(acs[:, t, HPG * g + 4 * x:HPG * g + 4 * x + 4], (P, 4, P), 2), ALU.subtract)
                    ins.then_inc(decay_diff, 1)
                    dve.wait_ge(decay_diff, q + 1)
                    V.tensor_scalar(seg[:, s, :], seg[:, s, :], 0.0, None, ALU.min).then_inc(decay_arg, 1)

                def decay_cb(t):
                    q, s = 3 * g + t, (3 * g + t) % 2
                    dve.wait_ge(decay_ready, q + 1)
                    dve.wait_ge(gm_ready, g + 1)
                    v = seg[:, s, :].rearrange("p (h l) -> p h l", h=HPG)
                    V.tensor_tensor(v, v, bc(Gm[:, tiles(t)], (P, HPG, P), 1), ALU.mult).then_inc(decay_cb_ready, 1)

                def y_old(k):
                    if k == 0:
                        dve.wait_ge(y_old_ps, g + 1)
                    else:
                        dve.wait_ge(s_read, 8 * g + STREAMS)
                    V.tensor_tensor(yoff[:, k, :].rearrange("p (h d) -> p h d", h=HPG),
                                    bank[7][:, :].rearrange("p (h d) -> p h d", h=HPG), bc(eacs[:, k + 1, hs], hd, 2),
                                    ALU.mult).then_inc(yo_ready, 1)

                dve.wait_ge(state_ps, 10 * g + 1)
                if g:
                    dve.wait_ge(s1_store, 16 * g)
                V.tensor_copy(S1[:, :], bank[6][:, :]).then_inc(s1_ready, 1)
                decay(0)
                decay_cb(0)
                y_old(0)
                s1v = S1[:, :].rearrange("p (h d) -> p h d", h=HPG)
                step(V.tensor_tensor(s1v, s1v, bc(dec[:, STREAMS, hs], hd, 2), ALU.mult))
                dve.wait_ge(state_ps, 10 * g + 2)
                V.tensor_tensor(S1[:, :], S1[:, :], bank[6][:, :], ALU.add).then_inc(s1_ready, 1)
                decay(1)
                decay_cb(1)
                y_old(1)
                decay(2)
                for b in range(STREAMS):
                    if b == 3:
                        decay_cb(2)
                    dve.wait_ge(s_dec, 8 * g + b + 1)
                    dve.wait_ge(state_ps, 10 * g + 3 + b)
                    V.tensor_tensor(S[:, b, :], S[:, b, :], bank[6 + b % 2][:, :], ALU.add).then_inc(state_ready, 1)
                dve.wait_ge(y_tile_ps, 3 * g + 3)
                for i in range(5):
                    if i < 4:
                        dve.wait_ge(z_done, 4 * g + i + 1)
                        V.scalar_tensor_tensor(out=xsT[:, i, :], in0=xsT[:, i, :], scalar=dcol[:, 4 * g + i:4 * g + i + 1],
                                               in1=bank[i][:, 0:TOK], op0=ALU.mult, op1=ALU.add).then_inc(y_evac, 1)
                        dve.wait_ge(y_evac, 4 * g + i + 1)
                        V.tensor_tensor(zs[:, i, :], zs[:, i, :], xsT[:, i, :], ALU.mult).then_inc(y_ready, 1)
                    if i:
                        dve.wait_ge(yh_ready, 4 * g + i)
                        V.scalar_tensor_tensor(out=yl[:, i - 1, :], in0=zs[:, i - 1, :],
                                               scalar=ang[:, 4 * g + i - 1:4 * g + i], in1=yh[:, i - 1, :].bitcast(F32),
                                               op0=ALU.mult, op1=ALU.subtract).then_inc(yl_ready, 1)
                if g + 1 < GROUPS:
                    for b in range(LEAD):
                        in_proj(g + 1, b)
                for b in range(4):
                    n = out_block(g, b)
                    lo_split(n + 3)
                    if g == GROUPS - 1 and b == 2:
                        dve.wait_ge(y_std, 1)
                        step(V.reciprocal(rstd[:, 0, :], std[:, :]))
                    dve.wait_ge(blk, CRED + n + 1)
                    for j in (2 * b, 2 * b + 1):
                        src = bank[4 + j % 4][:, 0:TOK]
                        if g == 0:
                            V.tensor_copy(facc[:, j, :], src).then_inc(f_evac, 1)
                        else:
                            V.tensor_tensor(facc[:, j, :], facc[:, j, :], src, ALU.add).then_inc(f_evac, 1)
                    if g == GROUPS - 1 and b >= 2:
                        dve.wait_ge(f_evac, 8 * g + 2 * b + 2)
                        for j in range(3) if b == 2 else range(3, KD):
                            step(V.tensor_tensor(facc[:, j, :], facc[:, j, :], rstd[:, 0, :], ALU.mult))
                            V.tensor_tensor(h[:, j, :], h[:, j, :], facc[:, j, :], ALU.add).then_inc(h_new, 1)
                            if j:
                                x_lo(2, j - 1)
            x_lo(2, KD - 1)
            gate_up(1, 2)
            down(1, 3)
            ple_dve(0, 3)

            kx_lo(KD - 1)
            for b in range(3):
                lo_split(KV + b + 3)

            def token_rows(x):
                dve.wait_ge(row_std, x + 1)
                V.reciprocal(rows[:, x, :], rows[:, x, :]).then_inc(rows_ready, 1)
                dve.wait_ge(rows_ready, x + 1)

            token_rows(0)
            dve.wait_ge(blk, CRED + KV + 3)
            for t in range(TT):
                V.tensor_scalar(kvr[:, t, :], bank[KV_BANK[t]][:, 0:KV_LORA + ROPE], rows[:, 0, t:t + 1], None,
                                ALU.mult).then_inc(kvr_ready, 1)
            for k in range(KD):
                x_lo(4, k)
            norm_rstd(4)
            H2 = ROPE // 2
            dve.wait_ge(filled, 4)
            for t in range(TT):
                dve.wait_ge(kv_std, t + 1)
                step(V.reciprocal(rsc[:, t, 4:6], rsc[:, t, 2:4]))
                V.scalar_tensor_tensor(out=ckv[:, t, :], in0=kvr[:, t, 0:256], scalar=rsc[:, t, 4:5], in1=kvg[:, 0:256],
                                       op0=ALU.mult, op1=ALU.mult)
                x = krot[:, t, 0, :]
                step(V.scalar_tensor_tensor(out=x, in0=kvr[:, t, 256:288], scalar=rsc[:, t, 5:6], in1=kvg[:, 256:288],
                                            op0=ALU.mult, op1=ALU.mult))
                kr = krow[:, t, NOPE:QD]
                V.tensor_tensor(krot[:, t, 1, :], x, sinr[:, t, :], ALU.mult)
                step(V.tensor_tensor(kr, x, cosr[:, t, :], ALU.mult))
                V.tensor_tensor(kr[:, 0:H2], kr[:, 0:H2], krot[:, t, 1, H2:ROPE], ALU.subtract)
                V.tensor_tensor(kr[:, H2:ROPE], kr[:, H2:ROPE], krot[:, t, 1, 0:H2], ALU.add).then_inc(kv_done, 1)
            gate_up(2, 4)
            down(2, 5)

            for b in range(4):
                lo_split(DQ + b + 3)
            token_rows(1)
            dve.wait_ge(blk, CRED + DQ + 4)
            for t in range(TT):
                V.tensor_scalar(cqr[:, t, :], bank[t][:, :], rows[:, 1, t:t + 1], None, ALU.mult).then_inc(cq_ready, 1)
            dve.wait_ge(w_ld, 16 * 5)
            for t in range(TT):
                dve.wait_ge(cq_std, t + 1)
                step(V.reciprocal(rsc[:, t, 4:5], rsc[:, t, 2:3]))
                V.scalar_tensor_tensor(out=cqr[:, t, :], in0=cqr[:, t, :], scalar=rsc[:, t, 4:5], in1=qgr,
                                       op0=ALU.mult, op1=ALU.mult).then_inc(cqn_ready, 1)
            V.tensor_tensor(gq[:, 2:3], gq[:, 0:1], gq[:, 1:2], ALU.mult).then_inc(gq_ready, 1)
            V.tensor_tensor(cosr[:], cosr[:], bc(gr[:], (P, TT, ROPE), 1), ALU.mult)
            V.tensor_tensor(sinr[:], sinr[:], bc(gr[:], (P, TT, ROPE), 1), ALU.mult).then_inc(gq_ready, 1)
            dve.wait_ge(gq_ready, 2)
            for k in range(4):
                dve.wait_ge(cq_hi, k + 1)
                V.tensor_tensor(xl[:, k, :], bank[4 + k][:, 0:TOK], xh[:, k, :].bitcast(F32), ALU.subtract).then_inc(cq_lo, 1)
            def q_sums(e):
                o = 24 * (e % 2)
                dve.wait_ge(q_sq, e + 1)
                v = sq5[:, e % 2, 0:384].rearrange("p (h d) -> p h d", h=4)
                V.reduce_sum(sm[:, o:o + 4], v[:, :, 0:NOPE], axis=AX.X)
                V.reduce_sum(sm[:, o + 4:o + 8], v[:, :, NOPE:QD], axis=AX.X).then_inc(q_sum, 1)

            for cg in range(4):
                for b in range(2):
                    lo_split(QB + 2 * cg + b + 3)
                for t in range(TT):
                    e, s = 3 * cg + t, (3 * cg + t) % 2
                    o = 24 * s
                    if e == 0:
                        q_sums(0)
                    if t < 2:
                        q_sums(e + 1)
                    dve.wait_ge(q_std, e + 1)
                    step(V.reciprocal(sm[:, o + 16:o + 24], sm[:, o + 8:o + 16]))
                    if e >= 3:
                        dve.wait_ge(q_turn_ps, e - 2)
                    if e >= 2:
                        dve.wait_ge(q_rows_ready, e - 1)
                    src = bank[3 * (cg % 2) + t][:, 0:384].rearrange("p (h d) -> p h d", h=4)
                    q, x = q_rows(e), q_rope(e)
                    V.tensor_tensor(x, src[:, :, NOPE:QD], bc(sm[:, o + 20:o + 24], (P, 4, ROPE), 2), ALU.mult)
                    V.tensor_tensor(q[:, :, 0:NOPE], src[:, :, 0:NOPE], bc(sm[:, o + 16:o + 20], (P, 4, NOPE), 2),
                                    ALU.mult).then_inc(qb_evac, 1)
                    if t == 2 and e + 1 < 12:
                        q_sums(e + 1)

            def key_sums(w):
                o = 48 + 24 * (w % 2)
                dve.wait_ge(key_sq, w + 1)
                V.reduce_sum(sm[:, o:o + 8], sq5[:, w % 2, :].rearrange("p (h d) -> p h d", h=8), axis=AX.X).then_inc(key_sum, 1)

            key_sums(0)
            for w in range(ITEMS):
                if w + 1 < ITEMS:
                    key_sums(w + 1)
                o = 48 + 24 * (w % 2)
                dve.wait_ge(key_std, w + 1)
                if w >= 4:
                    V.reciprocal(rsn[:, 8 * (w - 4):8 * (w - 4) + 8], sm[:, o + 8:o + 16]).then_inc(key_rows_ready, 1)
                    continue
                step(V.reciprocal(sm[:, o + 16:o + 24], sm[:, o + 8:o + 16]))
                if w >= 2:
                    dve.wait_ge(key_turn_ps, w - 1)
                else:
                    dve.wait_ge(q_turn_ps, 12)
                src = bank[EX_BANK[w % 4]][:, :].rearrange("p (h d) -> p h d", h=8)
                kv_ = kn[:, w % 2, :].rearrange("p (h d) -> p h d", h=8)
                V.tensor_copy(kv_[:, :, NOPE:QD], bc(krow[:, w // 2, NOPE:QD], (P, 8, ROPE), 1))
                V.tensor_tensor(kv_[:, :, 0:NOPE], src, bc(sm[:, o + 16:o + 24], (P, 8, NOPE), 2), ALU.mult).then_inc(key_rows_ready, 1)
            dve.wait_ge(ex_ps, ITEMS)
            for k in range(2):
                dve.wait_ge(wk_hi, k + 1)
                V.tensor_tensor(wkl[:, k, :], wk[:, k, :], wkh[:, k, :].bitcast(F32), ALU.subtract).then_inc(wk_lo, 1)

            def past_split(b):
                dve.wait_ge(past_hi, b + 1)
                V.tensor_tensor(cTl[:, b % 2], cTb[:, b % 2], cTh[:, b % 2].bitcast(F32), ALU.subtract).then_inc(past_lo, 1)

            def past_sums(w):
                b, st, g = w // 8, w // 2 % 4, w % 2
                dve.wait_ge(past_sq, w + 1)
                V.reduce_sum(ksq[:, b, st, 8 * g:8 * g + 8], kn[:, w % 2, 0:512].rearrange("p (h d) -> p h d", h=8),
                             axis=AX.X).then_inc(past_sum, 1)

            def p_max(x):
                s, o = x % 2, 48 + 8 * (x % 2)
                dve.wait_ge(qk_ps, x + 1)
                if x >= 2:
                    dve.wait_ge(pt_ps, x - 1)
                V.tensor_tensor(Pb[:, s, 0:384], bank[4 + s][:, 0:384], mk, ALU.add).then_inc(p_masked, 1)
                dve.wait_ge(p_masked, x + 1)
                V.reduce_max(sm[:, o:o + 1], Pb[:, s, 0:128], axis=AX.X)
                step(V.reduce_max(sm[:, o + 1:o + 2], Pb[:, s, 128:384], axis=AX.X))
                V.tensor_scalar(sm[:, o + 2:o + 4], sm[:, o:o + 2], -SCALE, None, ALU.mult).then_inc(p_max_ready, 1)

            past_split(0)
            past_split(1)
            dve.wait_ge(mask_ld, 16)
            p_max(0)
            for x in range(MH):
                s, o = x % 2, 48 + 8 * (x % 2)
                if x + 1 < MH:
                    p_max(x + 1)
                dve.wait_ge(p_exp_ready, x + 1)
                step(V.reciprocal(sm[:, o + 6:o + 8], sm[:, o + 4:o + 6]))
                V.tensor_scalar(Pb[:, s, 0:128], Pb[:, s, 0:128], sm[:, o + 6:o + 7], None, ALU.mult)
                V.tensor_scalar(Pb[:, s, 128:384], Pb[:, s, 128:384], sm[:, o + 7:o + 8], None, ALU.mult).then_inc(p_ready, 1)
                for i in range(4):
                    past_sums(4 * x + i)
                    if i == 1 and x % 2 and 2 <= x // 2 + 1 < STREAMS:
                        past_split(x // 2 + 1)
                if x % 2:
                    dve.wait_ge(oh_ready, x // 2 + 1)
                    V.tensor_tensor(xl[:, x // 2, 0:SEQ], bank[7 if x // 2 % 2 else 3][:, 0:SEQ],
                                    xh[:, x // 2, 0:SEQ].bitcast(F32), ALU.subtract).then_inc(ol_ready, 1)

            dve.wait_ge(past_std, 1)
            V.reciprocal(ksq[:], ksq[:]).then_inc(past_rstd, 1)

            def s_max(u):
                b, g = divmod(u, 2)
                s, o = u % 2, 64 + 8 * (u % 2)
                dve.wait_ge(pt_ps, MH + max(u - 1, 0))
                step(V.memset(Pb[:, s, PAST:640], 0.0))
                new = slice(PAST + 16 * b, PAST + 16 * b + 16)
                nk = slice(16 * b, 16 * b + 16)
                if u == 0:
                    dve.wait_ge(new_rk, 1)
                dve.wait_ge(rk_ready, u + 1)
                dve.wait_ge(sc_ps, u + 1)
                V.tensor_tensor(Pb[:, s, 0:PAST], bank[2][:, :], rk[:, s, 0:512], ALU.mult)
                step(V.tensor_tensor(Pb[:, s, new], bank[5][:, nk], rbn[:, g, nk], ALU.mult))
                V.tensor_tensor(Pb[:, s, 0:PAST], Pb[:, s, 0:PAST], bank[4][:, :], ALU.add)
                V.tensor_tensor(Pb[:, s, new], Pb[:, s, new], bank[5][:, P + 16 * b:P + 16 * b + 16], ALU.add).then_inc(s_added, 1)
                dve.wait_ge(s_added, u + 1)
                V.reduce_max(sm[:, o:o + 1], Pb[:, s, 0:PAST], axis=AX.X)
                step(V.reduce_max(sm[:, o + 1:o + 2], Pb[:, s, new], axis=AX.X))
                step(V.tensor_tensor(sm[:, o + 3:o + 4], sm[:, o:o + 1], sm[:, o + 1:o + 2], ALU.max))
                V.tensor_scalar(sm[:, o + 2:o + 3], sm[:, o + 3:o + 4], -SCALE, None, ALU.mult).then_inc(s_max_ready, 1)

            def s_latent(u):
                b, g = divmod(u, 2)
                dve.wait_ge(s_turn_ps, u + 1)
                V.tensor_copy(QC[:, :, b, 8 * g:8 * g + 8, :],
                              bank[1][:, 0:256].rearrange("p (k h q) -> p k h q", k=2, h=8)).then_inc(s_out_kept, 1)

            s_max(0)
            for u in range(UNITS):
                o = 64 + 8 * (u % 2)
                dve.wait_ge(s_exp_ready, u + 1)
                step(V.tensor_tensor(sm[:, o + 6:o + 7], sm[:, o + 4:o + 5], sm[:, o + 5:o + 6], ALU.add))
                step(V.reciprocal(sm[:, o + 7:o + 8], sm[:, o + 6:o + 7]))
                if u:
                    s_latent(u - 1)
                if u + 1 < UNITS:
                    s_max(u + 1)
                dve.wait_ge(po_ps, MH + u + 1)
                V.tensor_scalar(ol[:, :], bank[7][:, 256:512], sm[:, o + 7:o + 8], None, ALU.mult).then_inc(s_out_ready, 1)
            s_latent(UNITS - 1)
            for x in range(MH // 2):
                dve.wait_ge(oh_ready, MH // 2 + x + 1)
                V.tensor_tensor(xl[:, x, SEQ:TOK], bank[x % 2][:, 0:P], xh[:, x, SEQ:TOK].bitcast(F32),
                                ALU.subtract).then_inc(ol_ready, 1)
            for b in range(8):
                lo_split(WO + b + 3)
                dve.wait_ge(blk, CRED + WO + b + 1)
                V.tensor_tensor(h[:, b, :], h[:, b, :], bank[2 + b % 4][:, 0:TOK], ALU.add).then_inc(h_new, 1)
            for k in range(KD):
                x_lo(6, k)
            gate_up(3, 6)
            down(3, 7)
            ple_dve(1, 7)

        @block.tensor
        def _(pe):
            M = nc.tensor.matmul

            def product(out, r, k0, k1, mh_, ml_, first, last):
                for k in range(k0, k1):
                    ws = slice(k * P, (k + 1) * P)
                    M(out, whi[:, r, ws], mh_(k), start=first and k == k0, stop=False)
                    M(out, whi[:, r, ws], ml_(k), start=False, stop=False)
                    ins = M(out, wlo[:, r, ws], mh_(k), start=False, stop=last and k == k1 - 1)
                return ins

            def row_product(out, r, w0, w, xh_, xl_, first, last):
                M(out, xh_, whi[:, r, w0:w0 + w], start=first, stop=False)
                M(out, xh_, wlo[:, r, w0:w0 + w], start=False, stop=False)
                return M(out, xl_, whi[:, r, w0:w0 + w], start=False, stop=last)

            def weights(n, i=0):
                pe.wait_ge(lo_ready, i * SLOTS + (n + 1))

            def norm_sum(m):
                pe.wait_ge(sq_done, m + 1)
                M(bank[7][:, 0:TOK], ones[:, :], sqacc[:, m % 2, :], start=True, stop=True).then_inc(ms_ready, 1)

            X = (lambda k: xh[:, k, :], lambda k: xl[:, k, :])

            def gate_up(u, m):
                base = BASE[f"gu{u}"]

                def pair(i, first):
                    for j in range(2):
                        pe.wait_ge(gu_evac, i * 2 + (KF * u + j + 1))
                        for half in range(2):
                            n = base + 2 * j + half
                            weights(n, i)
                            if first and j == 0 and half == 0:
                                for k in range(KD):
                                    pe.wait_ge(xl_ready, 8 * m + k + 1)
                                    ins = product(bank[0][:, 0:TOK], n % SLOTS, k, k + 1, *X, k == 0, k == KD - 1)
                            else:
                                ins = product(bank[2 * j + half][:, 0:TOK], n % SLOTS, 0, KD, *X, True, True)
                            ins.then_inc(blk, 1)
                            if first and (j, half) == ((1, 0) if m == 0 else (0, 1)) and m != 4:
                                norm_sum(m)
                pair(0, True)
                with pe.Fori(1, KF // 2) as i:
                    pair(i, False)

            def down(u, m):
                pe.wait_ge(gu_evac, 2 + KF * (u + 1))
                for j in range(KD):
                    k0 = 0
                    if j >= 4:
                        pe.wait_ge(h_new, 8 * m + j - 3)
                    for b, w in enumerate(DN_TILES):
                        n = BASE[f"dn{u}"] + 3 * j + b
                        if j == 0:
                            pe.wait_ge(al_ready, KF * u + k0 + w)
                        weights(n)
                        product(bank[j % 4][:, 0:TOK], n % SLOTS, 0, w, lambda k: ah[:, k0 + k, :],
                                lambda k: al[:, k0 + k, :], b == 0, b == 2).then_inc(blk, 1)
                        k0 += w

            def ple_pe(l, m):
                pe.wait_ge(pl_ready, l + 1)
                for i in range(2):
                    n = BASE[f"pi{l}"] + i
                    weights(n)
                    for jj in range(4):
                        if i and jj == 3:
                            pe.wait_ge(pin_ready, 8 * l + 1)
                        elif i or jj == 3:
                            pe.wait_ge(h_new, 8 * m + (jj + 6 if i else 5))
                        ins = product(bank[PIN_BANK[4 * i + jj]][:, 0:TOK], n % SLOTS, 2 * jj, 2 * jj + 2, lambda k: phi[:, k % 2, :],
                                      lambda k: plo[:, k % 2, :], True, True)
                    ins.then_inc(blk, 1)
                    if i == 0:
                        norm_sum(m)
                pe.wait_ge(pin_ready, 8 * l + 4)
                pe.wait_ge(xl_ready, 8 * (m + 1))
                for j in range(KD):
                    n = BASE[f"pg{l}"] + j
                    weights(n)
                    if j == 3:
                        pe.wait_ge(pin_ready, 8 * l + 5)
                    if j >= 4:
                        pe.wait_ge(pg_evac, 8 * l + j - 3)
                    product(bank[PG_BANK[j % 4]][:, 0:TOK], n % SLOTS, 0, KD, *X, True, True).then_inc(blk, 1)

            pe.wait_ge(filled, 1)
            gate_up(0, 0)
            down(0, 1)

            weights(MIX)
            for k in range(KD):
                pe.wait_ge(xl_ready, 8 + k + 1)
                ins = product(bank[4][:, 0:TOK], MIX % SLOTS, k, k + 1, *X, k == 0, k == KD - 1)
            ins.then_inc(blk, 1)
            norm_sum(1)

            def in_proj(g, b):
                n = in_block(g, b)
                weights(n)
                if b >= 4:
                    pe.wait_ge(in_evac, 10 * g + b - 3)
                elif g:
                    pe.wait_ge(y_evac, 4 * (g - 1) + b + 1)
                product(bank[b % 4][:, 0:TOK], n % SLOTS, 0, KD, *X, True, True).then_inc(blk, 1)

            for g in range(GROUPS):
                for b in range(LEAD if g else 0, 10):
                    in_proj(g, b)
                    if g == 0 and b == 4:
                        pe.wait_ge(dt_ready, 1)
                        pe.wait_ge(const_ld, 144)
                        for t in range(TT):
                            for x, v in ((0, dv[2]), (96, dv[1])):
                                ins = nc.tensor.transpose(bank[5][:, x + 32 * t:x + 32 * t + 32], v[:, tiles(t)],
                                                          ident[0:HEADS, 0:HEADS])
                        ins.then_inc(dtT_ps, 1)
                    if g == 0 and b == 6:
                        pe.wait_ge(dtR_ready, 1)
                        for t in range(TT):
                            M(bank[6][:, 32 * t:32 * t + 32], mask[:, t, :], aR[:, t, :], start=True, stop=True)
                            M(bank[6][:, 96 + 32 * t:128 + 32 * t], ones[:, :] if t < 2 else same[:, :], aR[:, t, :],
                              start=True, stop=True)
                        M(bank[5][:, 0:STREAMS * HEADS], ones[:, :], am.rearrange("p s h -> p (s h)"), start=True,
                          stop=True).then_inc(ac_ps, 1)
                    if b == 7:
                        if g:
                            pe.wait_ge(f_evac, 8 * g)
                        pe.wait_ge(conv_done, 6 * g + 6)
                        for t in range(TT):
                            ins = nc.tensor.transpose(bank[7][:, tiles(t)], BC[:, 0, tiles(t)], ident[:, :])
                        ins.then_inc(bt_ps, 1)
                        if g == 0:
                            pe.wait_ge(da_ready, 1)
                        for t in range(TT):
                            for i in range(4):
                                ins = nc.tensor.transpose(bank[4 + t][:, tiles(i)], xsT[:, i, tiles(t)], ident[:, :])
                            ins.then_inc(xt_ps, 1)
                    if b == 8:
                        pe.wait_ge(brow_ready, g + 1)
                        for t in range(TT):
                            ins = M(bank[7][:, tiles(t)], BC[:, 0, tiles(t)], BC[:, 1, tiles(t)], start=True, stop=True)
                        ins.then_inc(g_ps, 1)

                def running(t):
                    if t:
                        pe.wait_ge(decay_diff, 3 * g + t)
                    for hh in range(HPG):
                        a = aR[:, t, HPG * g + hh:HPG * g + hh + 1].broadcast_to((P, P))
                        ins = M(bank[4 + hh // 4][:, tiles(hh % 4)], a, mask[:, t, :], start=True, stop=True)
                    ins.then_inc(running_ps, 1)

                def y_tile(t):
                    s = (3 * g + t) % 2
                    pe.wait_ge(decay_cb_ready, 3 * g + t + 1)
                    if t:
                        pe.wait_ge(yo_ready, 2 * g + t)
                    for i in range(4):
                        if t:
                            M(bank[i][:, tiles(t)], yoff[:, t - 1, tiles(i)], ident[:, :], start=True, stop=False,
                              skip_group_check=True)
                        for e in range(2):
                            hh = 2 * i + e
                            ins = M(bank[i][HD * e:HD * e + HD, tiles(t)], xdt[:, t, hh * HD:hh * HD + HD],
                                    seg[:, s, tiles(hh)], start=t == 0, stop=True, skip_group_check=True)
                    ins.then_inc(y_tile_ps, 1)

                pe.wait_ge(xw_ready, 3 * g + 3)
                M(bank[6][:, :], Brow[:, 0, :], xw[:, 0, :], start=True, stop=True).then_inc(state_ps, 1)
                running(0)
                pe.wait_ge(s1_ready, 2 * g + 1)
                pe.wait_ge(gm_ready, g + 1)
                M(bank[7][:, :], BC[:, 1, tiles(1)], S1[:, :], start=True, stop=True).then_inc(y_old_ps, 1)
                M(bank[6][:, :], Brow[:, 1, :], xw[:, 1, :], start=True, stop=True).then_inc(state_ps, 1)
                running(1)
                pe.wait_ge(s_ld, 16 * (g + 1))
                pe.wait_ge(bm_ready, g + 1)
                pe.wait_ge(yo_ready, 2 * g + 1)
                for b in range(STREAMS):
                    M(bank[7][:, :], Cm[:, b, :], S[:, b, :], start=b == 0, stop=b == STREAMS - 1).then_inc(s_read, 1)
                pe.wait_ge(in_evac, 10 * g + 10)
                y_tile(0)
                running(2)
                y_tile(1)
                for b in range(STREAMS):
                    if b == 0:
                        pe.wait_ge(s1_ready, 2 * g + 2)
                    elif b == 1:
                        pe.wait_ge(yo_ready, 2 * g + 2)
                    else:
                        pe.wait_ge(state_ready, 8 * g + b - 1)
                    M(bank[6 + b % 2][:, :], Bm[:, b, :], xw[:, 2, :], start=True, stop=True).then_inc(state_ps, 1)
                y_tile(2)
                if g + 1 < GROUPS:
                    for b in range(LEAD):
                        in_proj(g + 1, b)
                for b in range(4):
                    n = out_block(g, b)
                    weights(n)
                    for x in range(2):
                        j = 2 * b + x
                        if j == 2:
                            pe.wait_ge(state_ready, 8 * g + 8)
                        if b >= 2:
                            pe.wait_ge(f_evac, 8 * g + j - 3)
                        for k in range(4):
                            if j == 0:
                                pe.wait_ge(yl_ready, 4 * g + k + 1)
                            ins = product(bank[4 + j % 4][:, 0:TOK], n % SLOTS, 4 * x + k, 4 * x + k + 1,
                                          lambda k: yh[:, k % 4, :], lambda k: yl[:, k % 4, :], k == 0, k == 3)
                    ins.then_inc(blk, 1)
                    if g == GROUPS - 1 and b == 1:
                        pe.wait_ge(y_sq, 4 * GROUPS)
                        pe.wait_ge(y_evac, 4 * GROUPS)
                        M(bank[0][:, 0:TOK], ones[:, :], sqacc[:, 0, :], start=True, stop=True).then_inc(y_sum_ps, 1)
            gate_up(1, 2)
            down(1, 3)
            ple_pe(0, 3)

            def token_rows(m):
                pe.wait_ge(sq_done, m + 1)
                for t in range(TT):
                    ins = M(bank[4][:, t:t + 1], sqacc[:, m % 2, tiles(t)], ones[:, 0:1], start=True, stop=True)
                ins.then_inc(rt_ps, 1)

            pe.wait_ge(pin_ready, 8)
            pe.wait_ge(pg_evac, 5)
            k = 0
            for b in range(3):
                weights(KV + b)
                for kk in range(WIDTH[KV + b] // 288):
                    pe.wait_ge(kxl_ready, k + 1)
                    for t in range(TT):
                        ins = row_product(bank[KV_BANK[t]][:, 0:288], (KV + b) % SLOTS, 288 * kk, 288, kxh[:, k, tiles(t)],
                                          kxl[:, k, tiles(t)], k == 0, k == KD - 1)
                    k += 1
                ins.then_inc(blk, 1)
            token_rows(4)
            norm_sum(4)
            gate_up(2, 4)
            pe.wait_ge(kv_done, TT)
            for t in range(TT):
                for k in range(2):
                    nc.tensor.transpose(bank[5 + k][:, tiles(t)], ckv[:, t, tiles(k)], ident[:, :])
                ins = nc.tensor.transpose(bank[4][0:QD, tiles(t)], krow[:, t, :], ident[:, :])
            ins.then_inc(cT_ps, 1)
            down(2, 5)

            for b in range(4):
                weights(DQ + b)
                for kk in range(2):
                    k = 2 * b + kk
                    pe.wait_ge(xl_ready, 40 + k + 1)
                    for t in range(TT):
                        ins = row_product(bank[t][:, :], (DQ + b) % SLOTS, 512 * kk, 512, xh[:, k, tiles(t)],
                                          xl[:, k, tiles(t)], k == 0, k == KD - 1)
                ins.then_inc(blk, 1)
                if b == 2:
                    pe.wait_ge(cT_ready, 1)
                    token_rows(5)
            for t in range(TT):
                pe.wait_ge(cqn_ready, t + 1)
                for k in range(4):
                    ins = nc.tensor.transpose(bank[4 + k][:, tiles(t)], cqr[:, t, tiles(k)], ident[:, :])
            ins.then_inc(cq_turn_ps, 1)
            def q_transpose(e):
                pe.wait_ge(q_rows_ready, e + 1)
                if e >= 2:
                    pe.wait_ge(q_kept, e - 1)
                for hh in range(4):
                    ins = nc.tensor.transpose(bank[6 + e % 2][0:QD, tiles(hh)], q_rows(e)[:, hh, :], ident[:, :])
                ins.then_inc(q_turn_ps, 1)

            for cg in range(4):
                if cg >= 2:
                    pe.wait_ge(qb_evac, 3 * (cg - 1))
                for b in range(2):
                    n = QB + 2 * cg + b
                    weights(n)
                    for kk in range(2):
                        k = 2 * b + kk
                        if cg == 0:
                            pe.wait_ge(cq_lo, k + 1)
                        for t in range(TT):
                            ins = row_product(bank[3 * (cg % 2) + t][:, 0:384], n % SLOTS, 384 * kk, 384, xh[:, k, tiles(t)],
                                              xl[:, k, tiles(t)], k == 0, k == 3)
                    ins.then_inc(blk, 1)
                    if b == 0 and cg >= 2:
                        q_transpose(3 * cg - 4)
                    elif b == 1 and cg:
                        q_transpose(3 * cg - 3)
                        q_transpose(3 * cg - 2)
            q_transpose(8)

            def expand(w):
                t, g = divmod(w, 2)
                if w >= 4:
                    pe.wait_ge(key_rows_ready, w - 3)
                for k in range(2):
                    ins = M(bank[EX_BANK[w % 4]][:, :], cT[:, k, tiles(t)], wk[:, k, 512 * g:512 * g + 512], start=k == 0, stop=k == 1)
                ins.then_inc(ex_ps, 1)

            pe.wait_ge(w_ld, 16 * 5)
            pe.wait_ge(qb_evac, 9)
            expand(0)
            expand(1)
            for e in range(9, 12):
                q_transpose(e)
            pe.wait_ge(qb_evac, 12)
            expand(2)
            for w in range(ITEMS):
                if w + 3 < ITEMS:
                    expand(w + 3)
                if w < 4:
                    pe.wait_ge(key_rows_ready, w + 1)
                    if w:
                        pe.wait_ge(key_kept, w)
                    for hh in range(8):
                        ins = nc.tensor.transpose(bank[2 + hh // 4][0:QD, tiles(hh % 4)], kn[:, w % 2, QD * hh:QD * hh + QD], ident[:, :])
                    ins.then_inc(key_turn_ps, 1)
            pe.wait_ge(q_kept, 12)
            for v in range(4):
                for k in range(2):
                    ins = M(bank[4 + v][:, :], cT[:, k, tiles(v // 2)], wv[:, k, 512 * (v % 2):512 * (v % 2) + 512],
                            start=k == 0, stop=k == 1)
                ins.then_inc(vp_ps, 1)
            pe.wait_ge(vp_ev, 4)
            pe.wait_ge(key_kept, 4)
            pe.wait_ge(key_rows_ready, ITEMS)

            def p_scores(x):
                if x >= 2:
                    pe.wait_ge(p_masked, x - 1)
                out = bank[4 + x % 2]
                M(out[:, 0:128], Qp[0:QD, x, 0:128], Kp[0:QD, x, 0:128], start=True, stop=True)
                M(out[:, 128:384], Qp[0:QD, x, 128:256], Kp[0:QD, x, 0:256], start=True, stop=True).then_inc(qk_ps, 1)

            def past_expand(w):
                b, st, g = w // 8, w // 2 % 4, w % 2
                if w % 8 == 0:
                    pe.wait_ge(past_lo, b + 1)
                if w >= 2:
                    pe.wait_ge(past_sq, w - 1)
                for k in range(2):
                    ch, cl = cTh[:, b % 2, k, tiles(st)], cTl[:, b % 2, k, tiles(st)]
                    half = slice(512 * g, 512 * g + 512)
                    M(bank[w % 2][:, :], ch, wkh[:, k, half], start=k == 0, stop=False)
                    M(bank[w % 2][:, :], ch, wkl[:, k, half], start=False, stop=False)
                    ins = M(bank[w % 2][:, :], cl, wkh[:, k, half], start=False, stop=k == 1)
                ins.then_inc(past_ps, 1)

            pe.wait_ge(wk_lo, 2)
            p_scores(0)
            for x in range(MH):
                if x + 1 < MH:
                    p_scores(x + 1)
                past_expand(4 * x)
                past_expand(4 * x + 1)
                pe.wait_ge(p_ready, x + 1)
                for j in range(3):
                    ins = nc.tensor.transpose(bank[6][:, tiles(j)], Pb[:, x % 2, tiles(j)], ident[:, :])
                ins.then_inc(pt_ps, 1)
                past_expand(4 * x + 2)
                pe.wait_ge(pt_ev, x + 1)
                if x % 2 == 0 and x >= 4:
                    pe.wait_ge(ol_ready, x // 2 - 1)
                o = bank[7 if x // 2 % 2 else 3][VH * (x % 2):VH * (x % 2) + VH, :]
                v0, v1 = (Vp[:, k, VH * x:VH * x + VH] for k in range(2))
                M(o[:, 0:128], v0, PT[:, 0:128], start=True, stop=True)
                M(o[:, 128:256], v0, PT[:, 128:256], start=True, stop=False)
                M(o[:, 128:256], v1, PT[:, 256:384], start=False, stop=True).then_inc(po_ps, 1)
                past_expand(4 * x + 3)

            pe.wait_ge(wkT_ld, 64)
            pe.wait_ge(ol_ready, MH // 2)
            pe.wait_ge(past_sq, 8 * STREAMS)
            for j in range(8):
                if j >= 4:
                    pe.wait_ge(qc_ev, j - 3)
                for k in range(2):
                    for hh in range(2):
                        x = 2 * j + hh
                        ins = M(bank[j % 4][:, tiles(2 * k + hh)], wkT[0:QD, x, tiles(k)], Qs[0:QD, :, x, :], start=True, stop=True)
                ins.then_inc(qc_ps, 1)
            pe.wait_ge(new_rq, 2)
            for g in range(2):
                ins = nc.tensor.transpose(bank[4][:, tiles(g)], rq[:, 0, tiles(g)], ident[:, :])
            ins.then_inc(new_rt, 1)
            pe.wait_ge(qc_ev, 8)
            pe.wait_ge(new_rk, 1)

            def s_nope(u):
                b, g = divmod(u, 2)
                if g == 0:
                    pe.wait_ge(c_ld[b % 2], 16 * (STREAMS // 2 + b // 2 + 1))
                if u:
                    pe.wait_ge(s_added, u)
                for k in range(2):
                    q = QC[:, k, b, 8 * g:8 * g + 8, :].rearrange("p h q -> p (h q)")
                    M(bank[2][:, :], q, cTb[:, b % 2, k, :], start=k == 0, stop=k == 1)
                    M(bank[5][:, 0:P], q, cT[:, k, SEQ:TOK], start=k == 0, stop=k == 1)

            def s_rope(u):
                b, g = divmod(u, 2)
                if u:
                    pe.wait_ge(rk_ready, u)
                pe.wait_ge(rq_ready, u + 1)
                for st in range(4):
                    ins = nc.tensor.transpose(bank[3][:, tiles(st)], rq[:, u % 2, tiles(st)], ident[:, :])
                ins.then_inc(rt_done, 1)
                if g == 0:
                    pe.wait_ge(kr_ld, 16 * (b + 1))
                q = Qs[0:QD, b, 8 * g:8 * g + 8, :].rearrange("p h q -> p (h q)")
                M(bank[4][:, :], q, krTb[0:QD, :], start=True, stop=True)
                M(bank[5][:, P:2 * P], q, krT[0:QD, SEQ:TOK], start=True, stop=True).then_inc(sc_ps, 1)

            def s_turn(u):
                pe.wait_ge(s_out_ready, u + 1)
                if u:
                    pe.wait_ge(s_out_kept, u)
                for k in range(2):
                    ins = nc.tensor.transpose(bank[1][:, tiles(k)], ol[:, tiles(k)], ident[:, :])
                ins.then_inc(s_turn_ps, 1)

            s_nope(0)
            s_rope(0)
            for u in range(UNITS):
                b = u // 2
                if u + 1 < UNITS:
                    s_nope(u + 1)
                if u:
                    s_turn(u - 1)
                pe.wait_ge(s_exp_ready, u + 1)
                for j in range(5):
                    ins = nc.tensor.transpose(bank[6][:, tiles(j)] if j < 4 else bank[0][:, 0:P], Pb[:, u % 2, tiles(j)], ident[:, :])
                ins.then_inc(pt_ps, 1)
                if u + 1 < UNITS:
                    s_rope(u + 1)
                pe.wait_ge(pt_ev, MH + u + 1)
                if u % 2 == 0:
                    pe.wait_ge(cn_ld[b % 2], 16 * (b // 2 + 1))
                for j in range(5):
                    ins = M(bank[7][:, 256:512], PT[:, tiles(j)], cnat[:, b % 2, j, :] if j < 4 else ckv[:, 2, :],
                            start=j == 0, stop=j == 4)
                ins.then_inc(po_ps, 1)
            s_turn(UNITS - 1)
            pe.wait_ge(s_out_kept, 2 * STREAMS)
            for x in range(MH):
                if x % 2 == 0 and x >= 4:
                    pe.wait_ge(ol_ready, MH // 2 + x // 2 - 1)
                o = bank[x // 2 % 2][VH * (x % 2):VH * (x % 2) + VH, 0:P]
                for k in range(2):
                    ins = M(o, wv[:, k, VH * x:VH * x + VH], QC[:, k, :, x, :], start=k == 0, stop=k == 1)
                if x % 2:
                    ins.then_inc(s_head_ps, 1)
            pe.wait_ge(ol_ready, MH)
            for b in range(8):
                weights(WO + b)
                if b >= 4:
                    pe.wait_ge(h_new, 48 + b - 3)
                product(bank[2 + b % 4][:, 0:TOK], (WO + b) % SLOTS, 0, KD, *X, True, True).then_inc(blk, 1)
            gate_up(3, 6)
            down(3, 7)
            ple_pe(1, 7)


def tile_blocks(w, cols=P):
    k, m = w.shape
    return w.reshape(k // P, P, m // cols, cols).transpose(2, 1, 0, 3).reshape(m // cols, P, -1)


def kernel(**inp):
    import concourse.bacc as bacc
    from concourse.bass_utils import run_bass_kernel_spmd
    A = {k: np.asarray(v) for k, v in inp.items()}
    f32 = np.float32

    stream = np.zeros((NBLK, P, 1024), f32)

    def put(stage, blocks, first=0):
        b0 = BASE[stage] + first
        for j, w in enumerate(blocks):
            stream[b0 + j, :, :w.shape[-1]] = w

    for u, (l, s) in enumerate(((0, 1), (0, 2), (1, 1), (1, 2))):
        gate, up = (tile_blocks(A[f"w{s}_{x}"][l]) for x in ("gate", "up"))
        put(f"gu{u}", np.stack([gate, up], 1).reshape(2 * KF, P, 1024))
        down, at = tile_blocks(A[f"w{s}_down"][l]), [0, 8, 15, 22]
        put(f"dn{u}", [down[j][:, at[b] * P:at[b + 1] * P] for j in range(KD) for b in range(3)])
    w_in = A["a_in_proj"][0]
    w_dt = np.zeros((D_MODEL, P), f32)
    w_dt[:, :HEADS] = w_in[:, D_INNER + CONV_DIM:]
    put("mix", tile_blocks(w_dt))
    zt, ct = tile_blocks(w_in[:, :D_INNER]), tile_blocks(w_in[:, D_INNER:D_INNER + CONV_DIM])
    w_out = A["a_out_proj"][0]
    lead = 2
    for g in range(GROUPS):
        blocks = [ct[4 * g + i] for i in range(4)] + [ct[16 + g], ct[20 + g]] + [zt[4 * g + i] for i in range(4)]
        put("mix", blocks[:lead], 1 + 14 * g - (4 if g else 0))
        put("mix", blocks[lead:], 1 + 14 * g + lead)
        o = tile_blocks(w_out[512 * g:512 * g + 512])
        put("mix", o.reshape(4, 2, P, 512).transpose(0, 2, 1, 3).reshape(4, P, 1024), 11 + 14 * g + (lead if g < GROUPS - 1 else 0))
    for l in range(2):
        o = tile_blocks(A["w_ple_in"][l])
        put(f"pi{l}", o.reshape(2, 4, P, 256).transpose(0, 2, 1, 3).reshape(2, P, 1024))
        put(f"pg{l}", tile_blocks(A["w_ple_gate"][l]))

    def row_blocks(w, per):
        k = w.reshape(KD if w.shape[0] == D_MODEL else w.shape[0] // P, P, -1)
        return [k[i:i + per].transpose(1, 0, 2).reshape(P, -1) for i in range(0, k.shape[0], per)]

    put("kv", row_blocks(A["w_kv_a"], 3))
    put("dq", row_blocks(A["b_w_dq"][0], 2))
    for cg in range(4):
        put("qb", row_blocks(np.ascontiguousarray(A["b_w_q_b"][0][:, 384 * cg:384 * cg + 384]), 2), 2 * cg)
    put("wo", tile_blocks(A["b_w_o"][0]))

    def feat(x):
        return np.ascontiguousarray(x.reshape(x.shape[0], -1, P).transpose(2, 1, 0))

    def both(a, b):
        return np.concatenate([a.reshape(SEQ, -1), b.reshape(TOK - SEQ, -1)])

    def col(v):
        return v.reshape(-1, P).T

    def every(v):
        return np.ascontiguousarray(np.broadcast_to(v, (P,) + v.shape))

    arr = {"stream": stream, "x": feat(both(A["x_prompt"], A["x_sample"]))}
    arr["p"] = np.stack([feat(both(A["p_prompt"][l], A["p_sample"][l])) for l in range(2)])
    norm_gains = [A["ln_ffn1"][0], A["ln_mix"][0], A["ln_ffn2"][0], A["ln_ple"][0], A["ln_ffn1"][1], A["ln_mix"][1],
                  A["ln_ffn2"][1], A["ln_ple"][1], A["ln_kv"]]
    arr["gains"] = np.stack([col(v) for v in norm_gains], 1)
    arr["ident"] = np.eye(P, dtype=f32)
    arr["cstate"] = A["state_conv"][0].reshape(STREAMS, 3, KC, P).transpose(3, 2, 0, 1).reshape(P, KC, STREAMS * 3)
    arr["cw"] = np.concatenate([A["a_conv_w"][0], A["a_conv_b"]], 0).reshape(CONV_W + 1, KC, P).transpose(2, 1, 0)
    arr["dcol"] = col(np.repeat(A["a_D"][0], HD))
    arr["ang"] = col(A["a_norm"][0])
    row, cl = np.arange(P)[:, None], np.arange(P)[None, :]
    tri, blk16 = (row <= cl), (row // STEPS == cl // STEPS)
    arr["mask"] = np.stack([tri, tri, tri & blk16], 1).astype(f32)
    arr["same"] = blk16.astype(f32)
    arr["ind"] = (row // STEPS == np.arange(STREAMS)[None, :]).astype(f32)
    arr["dts"] = np.stack([A["a_dt_bias"][0], A["a_A_log"][0]], 1)
    arr["ssm"] = A["state_ssm"][0].reshape(STREAMS, GROUPS, 512, N).transpose(1, 3, 0, 2)
    arr["kvg"] = every(np.concatenate([A["kv_norm"], A["kr_norm"]]))
    inv = f32(10000.0) ** (-np.arange(ROPE // 2, dtype=f32) / f32(ROPE // 2))
    pos = np.concatenate([np.arange(SEQ), np.tile(PAST + np.arange(STEPS), STREAMS)]).astype(f32)
    ang_ = pos[:, None] * inv[None, :]
    arr["cos"] = np.tile(np.cos(ang_).astype(f32), 2).reshape(TT, P, -1).transpose(1, 0, 2)
    arr["sin"] = np.tile(np.sin(ang_).astype(f32), 2).reshape(TT, P, -1).transpose(1, 0, 2)
    arr["qgr"] = every(A["b_q_norm"][0])
    arr["gr"] = every(A["b_qn_rope"][0])
    pad = np.ones(P - NOPE, f32)
    arr["gq"] = np.stack([np.concatenate([A["b_qn_nope"][0], pad]), np.concatenate([A["k_norm"], pad])], 1)
    wkv = A["w_kv_b"].reshape(2, P, MH, NOPE + VH)
    arr["wk"] = wkv[..., :NOPE].transpose(1, 0, 2, 3).reshape(P, 2, -1)
    arr["wv"] = wkv[..., NOPE:].transpose(1, 0, 2, 3).reshape(P, 2, -1)
    arr["wkT"] = np.zeros((QD, MH, KV_LORA), f32)
    arr["wkT"][:NOPE] = A["w_kv_b"].reshape(KV_LORA, MH, NOPE + VH)[..., :NOPE].transpose(2, 1, 0)
    diag = np.where((cl // 64) <= (row // 64), 0.0, -1e30).astype(f32)
    arr["mk"] = np.concatenate([diag, np.zeros((P, P), f32), diag], 1)
    cache = A["cache_kv_latent"]
    arr["cache"] = cache.reshape(STREAMS, 4, P, KV_LORA).transpose(0, 2, 1, 3)
    arr["cacheT"] = cache.reshape(STREAMS, PAST, 2, P).transpose(0, 3, 2, 1)
    arr["krcT"] = A["cache_k_rope"].transpose(0, 2, 1)
    outs = {"y": (P, KD, TOK), "ssm_p": (GROUPS, P, 512), "ssm_s": (GROUPS, P, STREAMS, 512),
            "conv": (P, KC, 27), "kvl": (P, TT, KV_LORA), "kr": (P, TT, ROPE)}

    nc = bacc.Bacc("TRN2", target_bir_lowering=False, num_devices=1)
    T = {}
    sent = {}
    for name, a in arr.items():
        sent[f"in_{name}"] = np.ascontiguousarray(a)
        T[name] = nc.dram_tensor(f"in_{name}", a.shape, F32, kind="ExternalInput").ap()
    for name, shape in outs.items():
        T[name] = nc.dram_tensor(f"out_{name}", shape, F32, kind="ExternalOutput").ap()
    build(nc, T)
    got = run_bass_kernel_spmd(nc, [sent], core_ids=[0]).results[0]
    got = {name: np.asarray(got[f"out_{name}"]) for name in outs}

    y = got["y"].transpose(2, 1, 0).reshape(TOK, D_MODEL)
    kvl = got["kvl"].transpose(1, 0, 2).reshape(TOK, KV_LORA)
    kr = got["kr"].transpose(1, 0, 2).reshape(TOK, ROPE)
    conv = got["conv"].transpose(2, 1, 0).reshape(27, CONV_DIM)
    ssm_p = got["ssm_p"].reshape(GROUPS, N, HPG, HD).transpose(0, 2, 3, 1).reshape(1, 1, HEADS, HD, N)
    ssm_s = got["ssm_s"].reshape(GROUPS, N, STREAMS, HPG, HD).transpose(2, 0, 3, 4, 1).reshape(1, STREAMS, HEADS, HD, N)
    outs_ = (y[:SEQ].reshape(1, SEQ, D_MODEL), y[SEQ:].reshape(STREAMS, STEPS, D_MODEL),
             conv[:3].reshape(1, 1, 3, CONV_DIM), ssm_p,
             kvl[:SEQ].reshape(1, SEQ, KV_LORA), kr[:SEQ].reshape(1, SEQ, ROPE),
             conv[3:].reshape(1, STREAMS, 3, CONV_DIM), ssm_s,
             kvl[SEQ:].reshape(STREAMS, STEPS, KV_LORA), kr[SEQ:].reshape(STREAMS, STEPS, ROPE))
    return tuple(np.ascontiguousarray(o) for o in outs_)
```
